# Optimizing a Trainium2 kernel written in Bass

```python
import jax, jax.numpy as jnp
from jax import lax
import numpy as np

D_MODEL = 1024
BATCH = 1
SEQ = 512
DEPTH = 2
DEC_BATCH = 1
DEC_SEQ = 32
PAST_LEN = 128

CHUNK = 64
D_POOL = D_MODEL // 4
POOL_WINDOWS = (2, 4, 8, 16)
N_POOL_GROUPS = len(POOL_WINDOWS)
POOL_GROUP = D_POOL // N_POOL_GROUPS
POOL_MAX = max(POOL_WINDOWS)
POOL_HIST = POOL_MAX - 1
D_RWKV = D_MODEL - D_POOL
HEAD_DIM = 64
N_HEADS = D_RWKV // HEAD_DIM
LORA_W = 64
LORA_A = 64
LORA_G = 128
D_SHIFT = 3 * D_RWKV + LORA_W + LORA_A + LORA_G
N_IN = D_POOL + D_SHIFT
RWKV_SPLITS = (D_RWKV, 2 * D_RWKV, 3 * D_RWKV, 3 * D_RWKV + LORA_W, 3 * D_RWKV + LORA_W + LORA_A)
D_FF = 2816
D_PLE = 256
ALPHA = (2.0 * DEPTH) ** 0.25
BETA = (8.0 * DEPTH) ** -0.25
LN_EPS = 1e-5
LNX_EPS = 64e-5

kernel_name = "pool_rwkv7_macaron_deepnorm_stream"

def layer_norm(x, g, b, eps=LN_EPS):
    xf = x.astype(jnp.float32)
    mu = jnp.mean(xf, axis=-1, keepdims=True)
    var = jnp.mean(jnp.square(xf - mu), axis=-1, keepdims=True)
    return ((xf - mu) * lax.rsqrt(var + eps) * g.astype(jnp.float32) + b.astype(jnp.float32)).astype(x.dtype)

def swiglu(x, w_in, w_out):
    gate, up = jnp.split(x @ w_in, 2, axis=-1)
    return (jax.nn.silu(gate) * up) @ w_out

def pool_mixer(u, u_hist, pos0, pool_w, pool_scale):
    B, T, _ = u.shape
    H = u_hist.shape[1]
    u_ext = jnp.concatenate([u_hist, u], axis=1)
    padded = jnp.pad(u_ext.astype(jnp.float32), ((0, 0), (POOL_MAX, 0), (0, 0)))
    cs = jnp.cumsum(padded, axis=1)
    end = cs[:, H + POOL_MAX:H + POOL_MAX + T]
    pos = pos0 + jnp.arange(T)
    means = []
    for gi, w in enumerate(POOL_WINDOWS):
        sl = slice(gi * POOL_GROUP, (gi + 1) * POOL_GROUP)
        s = end[..., sl] - cs[:, H + POOL_MAX - w:H + POOL_MAX - w + T, sl]
        cnt = jnp.minimum(pos + 1, w).astype(jnp.float32)[None, :, None]
        means.append(s / cnt)
    pooled = jnp.concatenate(means, axis=-1).astype(u.dtype) - u
    mixed = jnp.einsum('btgc,gcd->btgd', pooled.reshape(B, T, N_POOL_GROUPS, POOL_GROUP), pool_w)
    out = mixed.reshape(B, T, D_POOL) * pool_scale
    return out, u_ext[:, -POOL_HIST:]

def wkv_step(S, inp):
    r_t, w_t, k_t, v_t, a_t, b_t = inp
    sa = jnp.einsum('bhvk,bhk->bhv', S, a_t)
    S = S * w_t[:, :, None, :] + sa[..., None] * b_t[:, :, None, :] + v_t[..., None] * k_t[:, :, None, :]
    y = jnp.einsum('bhvk,bhk->bhv', S, r_t)
    return S, y

def rwkv7_mixer(zr, shift_prev, wkv_prev, mu_shift, w0, w2, a0, a2, g2, k_k, k_a, r_k, lnx_g, lnx_b):
    B, T, _ = zr.shape
    z_prev = jnp.concatenate([shift_prev[:, None, :], zr[:, :-1]], axis=1)
    zs = zr + (z_prev - zr) * mu_shift
    r, k, v, lw, la, lg = jnp.split(zs, RWKV_SPLITS, axis=-1)
    w = -jax.nn.softplus(-(w0 + jnp.tanh(lw) @ w2)) - 0.5
    decay = jnp.exp(-jnp.exp(w.astype(jnp.float32)))
    a = jax.nn.sigmoid(a0 + la @ a2)
    g = jax.nn.sigmoid(lg) @ g2

    def heads(t):
        return t.reshape(B, T, N_HEADS, HEAD_DIM).astype(jnp.float32)

    kk = heads(k * k_k)
    kk = kk / jnp.maximum(jnp.sqrt(jnp.sum(kk * kk, axis=-1, keepdims=True)), 1e-12)
    k = k * (1 + (a - 1) * k_a)
    rh, kh, vh, ah, wh = heads(r), heads(k), heads(v), heads(a), heads(decay)
    bh = kk * ah

    def tm(t):
        return jnp.moveaxis(t, 1, 0)

    S_final, ys = lax.scan(wkv_step, wkv_prev.astype(jnp.float32),
                           (tm(rh), tm(wh), tm(kh), tm(vh), tm(-kk), tm(bh)))
    ys = jnp.moveaxis(ys, 0, 1)
    ys = layer_norm(ys, lnx_g.reshape(N_HEADS, HEAD_DIM), lnx_b.reshape(N_HEADS, HEAD_DIM), LNX_EPS)
    ys = ys + jnp.sum(rh * kh * r_k.astype(jnp.float32), axis=-1, keepdims=True) * vh
    out = ys.reshape(B, T, D_RWKV).astype(zr.dtype) * g
    return out, zr[:, -1], S_final.astype(wkv_prev.dtype)

def run_trunk(x, p, pos0, pool_hist, shift_prev, wkv_prev, W):
    pools, shifts, wkvs = [], [], []
    for i in range(DEPTH):
        x = layer_norm(ALPHA * x + 0.5 * swiglu(x, W['ffn1_w_in'][i], W['ffn1_w_out'][i]),
                       W['ln1_g'][i], W['ln1_b'][i])
        z = x @ W['w_in'][i]
        u, zr = z[..., :D_POOL], z[..., D_POOL:]
        pool_out, pool_new = pool_mixer(u, pool_hist[i], pos0, W['pool_w'][i], W['pool_scale'][i])
        rwkv_out, shift_new, wkv_new = rwkv7_mixer(
            zr, shift_prev[i], wkv_prev[i], W['mu_shift'][i], W['w0'][i], W['w2'][i], W['a0'][i],
            W['a2'][i], W['g2'][i], W['k_k'][i], W['k_a'][i], W['r_k'][i], W['lnx_g'][i], W['lnx_b'][i])
        mix = jnp.concatenate([pool_out, rwkv_out], axis=-1) @ W['w_out'][i]
        x = layer_norm(ALPHA * x + mix, W['ln2_g'][i], W['ln2_b'][i])
        h = ALPHA * x + 0.5 * swiglu(x, W['ffn2_w_in'][i], W['ffn2_w_out'][i])
        gate = jax.nn.sigmoid(h @ W['ple_gate_w'][i] + W['ple_gate_b'][i])
        h = h + gate * (p[i] @ W['ple_w'][i])
        x = layer_norm(h, W['ln3_g'][i], W['ln3_b'][i])
        pools.append(pool_new)
        shifts.append(shift_new)
        wkvs.append(wkv_new)
    return x, jnp.stack(pools), jnp.stack(shifts), jnp.stack(wkvs)

def setup_inputs(seed: int = 0) -> dict:
    key = jax.random.key(seed)
    ks = iter(jax.random.split(key, 48))
    f32 = jnp.float32

    def nrm(shape, scale):
        return jax.random.normal(next(ks), shape, f32) * scale

    def gain(shape):
        return 1.0 + nrm(shape, 0.05)

    L = DEPTH
    w0_base = jnp.tile(jnp.linspace(-6.0, 1.0, HEAD_DIM, dtype=f32), N_HEADS)
    return {
        "x_prompt": nrm((BATCH, SEQ, D_MODEL), 1.0),
        "x_sample": nrm((DEC_BATCH, DEC_SEQ, D_MODEL), 1.0),
        "p_prompt": nrm((DEPTH, BATCH, SEQ, D_PLE), 1.0),
        "p_sample": nrm((DEPTH, DEC_BATCH, DEC_SEQ, D_PLE), 1.0),
        "state_pool": nrm((DEPTH, DEC_BATCH, POOL_HIST, D_POOL), 1.0),
        "state_shift": nrm((DEPTH, DEC_BATCH, D_SHIFT), 1.0),
        "state_wkv": nrm((DEPTH, DEC_BATCH, N_HEADS, HEAD_DIM, HEAD_DIM), 0.3),
        "ln1_g": gain((L, D_MODEL)), "ln1_b": nrm((L, D_MODEL), 0.02),
        "ln2_g": gain((L, D_MODEL)), "ln2_b": nrm((L, D_MODEL), 0.02),
        "ln3_g": gain((L, D_MODEL)), "ln3_b": nrm((L, D_MODEL), 0.02),
        "ffn1_w_in": nrm((L, D_MODEL, 2 * D_FF), D_MODEL ** -0.5),
        "ffn1_w_out": nrm((L, D_FF, D_MODEL), BETA * D_FF ** -0.5),
        "ffn2_w_in": nrm((L, D_MODEL, 2 * D_FF), D_MODEL ** -0.5),
        "ffn2_w_out": nrm((L, D_FF, D_MODEL), BETA * D_FF ** -0.5),
        "w_in": nrm((L, D_MODEL, N_IN), D_MODEL ** -0.5),
        "mu_shift": jax.random.uniform(next(ks), (L, D_SHIFT), f32, 0.05, 0.95),
        "pool_w": nrm((L, N_POOL_GROUPS, POOL_GROUP, POOL_GROUP), POOL_GROUP ** -0.5),
        "pool_scale": gain((L, D_POOL)),
        "w0": w0_base[None, :] + nrm((L, D_RWKV), 0.1),
        "w2": nrm((L, LORA_W, D_RWKV), 0.1 * LORA_W ** -0.5),
        "a0": nrm((L, D_RWKV), 0.1),
        "a2": nrm((L, LORA_A, D_RWKV), 0.3 * LORA_A ** -0.5),
        "g2": nrm((L, LORA_G, D_RWKV), LORA_G ** -0.5),
        "k_k": 0.85 + nrm((L, D_RWKV), 0.05),
        "k_a": gain((L, D_RWKV)),
        "r_k": nrm((L, N_HEADS, HEAD_DIM), 0.1),
        "lnx_g": gain((L, D_RWKV)), "lnx_b": nrm((L, D_RWKV), 0.02),
        "w_out": nrm((L, D_MODEL, D_MODEL), BETA * D_MODEL ** -0.5),
        "ple_gate_w": nrm((L, D_MODEL, D_MODEL), D_MODEL ** -0.5),
        "ple_gate_b": nrm((L, D_MODEL), 0.02),
        "ple_w": nrm((L, D_PLE, D_MODEL), BETA * D_PLE ** -0.5),
    }

def reference(x_prompt, x_sample, p_prompt, p_sample, state_pool, state_shift, state_wkv,
              ln1_g, ln1_b, ln2_g, ln2_b, ln3_g, ln3_b,
              ffn1_w_in, ffn1_w_out, ffn2_w_in, ffn2_w_out,
              w_in, mu_shift, pool_w, pool_scale, w0, w2, a0, a2, g2, k_k, k_a, r_k,
              lnx_g, lnx_b, w_out, ple_gate_w, ple_gate_b, ple_w):
    W = dict(ln1_g=ln1_g, ln1_b=ln1_b, ln2_g=ln2_g, ln2_b=ln2_b, ln3_g=ln3_g, ln3_b=ln3_b,
             ffn1_w_in=ffn1_w_in, ffn1_w_out=ffn1_w_out, ffn2_w_in=ffn2_w_in, ffn2_w_out=ffn2_w_out,
             w_in=w_in, mu_shift=mu_shift, pool_w=pool_w, pool_scale=pool_scale, w0=w0, w2=w2,
             a0=a0, a2=a2, g2=g2, k_k=k_k, k_a=k_a, r_k=r_k, lnx_g=lnx_g, lnx_b=lnx_b,
             w_out=w_out, ple_gate_w=ple_gate_w, ple_gate_b=ple_gate_b, ple_w=ple_w)
    B = x_prompt.shape[0]
    dt = x_prompt.dtype
    y_prompt, pool_prompt, shift_prompt, wkv_prompt = run_trunk(
        x_prompt, p_prompt, 0,
        jnp.zeros((DEPTH, B, 0, D_POOL), dt),
        jnp.zeros((DEPTH, B, D_SHIFT), dt),
        jnp.zeros((DEPTH, B, N_HEADS, HEAD_DIM, HEAD_DIM), dt), W)
    y_sample, pool_sample, shift_sample, wkv_sample = run_trunk(
        x_sample, p_sample, PAST_LEN, state_pool, state_shift, state_wkv, W)
    return (y_prompt, y_sample, pool_prompt, shift_prompt, wkv_prompt, pool_sample, shift_sample, wkv_sample)


_drawn_inputs = setup_inputs


def setup_inputs(seed=0):
    import zlib

    import numpy as np

    out = dict(_drawn_inputs(seed))
    spreads = {}
    factors = {'pool_scale': 5.553, 'w2': 8.0, 'lnx_g': 4.895, 'lnx_b': 8.0, 'ple_gate_b': 26.431}
    for name, (base, spread) in spreads.items():
        noise = np.random.default_rng([zlib.crc32(name.encode()), seed]).standard_normal(out[name].shape)
        drawn = base * np.exp(spread * noise) if base else spread * noise
        out[name] = __import__('jax').numpy.asarray(drawn.astype(out[name].dtype))
    for name, factor in factors.items():
        out[name] = (out[name] * factor).astype(out[name].dtype)
    return out
```

```python
from contextlib import ExitStack

import numpy as np

import concourse.bass as bass
from concourse import mybir

F32 = mybir.dt.float32
F32R = mybir.dt.float32r
ACT = mybir.ActivationFunctionType
ALU = mybir.AluOpType

P = 128
DEPTH = 2
D = 1024
KT = D // P
TP, TS = 512, 32
T = TP + TS
HT = T // 2
FF = 2816
FT = FF // P
DR = 768
NPAIR = DR // P
NSH = 20
NZ = 22
HIST = 15
CH = 64
NCH = TP // CH
ALPHA = (2.0 * DEPTH) ** 0.25
LN_EPS, LNX_EPS = 1e-5, 64e-5
DECAY = float(np.exp(-0.5))

COLS = [("ln1_g", 8), ("ln1_b", 8), ("ln2_g", 8), ("ln2_b", 8), ("ln3_g", 8), ("ln3_b", 8), ("gate_b", 8),
        ("mu", NSH), ("w0", 6), ("a0", 6), ("k_k", 6), ("k_a", 6), ("r_k", 6), ("lnx_g", 6), ("lnx_b", 6),
        ("pool_scale", 2), ("one_ka", 6)]
COL = {}
NPAR = 0
for _n, _w in COLS:
    COL[_n] = NPAR
    NPAR += _w

PHASES = [("f1i", FT, [8, 8]), ("f1o", 4, [8, 7, 7, 8, 7, 7]), ("z", NZ // 2, [8, 8]), ("wo", 4, [8, 8]),
          ("f2i", FT, [8, 8]), ("f2o", 4, [8, 7, 7, 8, 7, 7]), ("gp", 8, [8, 2])]
SLOT0, SLOTS = {}, 0
for _n, _b, _k in PHASES:
    SLOT0[_n] = SLOTS
    SLOTS += _b * len(_k)
TILE0, TILES = {}, 0
for _n, _c in [("f1i", 2 * FT), ("f1o", 8), ("z", NZ), ("wo", 8), ("f2i", 2 * FT), ("f2o", 8), ("gp", 16)]:
    TILE0[_n] = TILES
    TILES += _c

CONSTS = [("ident", P), ("mean_d", P), ("head_sum", P), ("head_mean", P), ("m4", P), ("m16", P), ("m64", P),
          ("m4t", P), ("am", 3 * P), ("reset", T), ("winv", 2), ("rcnt", 2 * HIST)]
CCOL, NCONST = {}, 0
for _n, _w in CONSTS:
    CCOL[_n] = (NCONST, _w)
    NCONST += _w

STEPS = ["A", "H1", "H2", "T4T", "E16", "X1", "X2", "X3", "T16T", "G", "Y0", "E64", "Y1", "Y2", "Y3", "WT"]
NSTEP = len(STEPS)
GROUPS = [(0, 1), (2, 3), (4,)]


def build(nc, xT, pT, w1i, w1o, wz, wo, w2i, w2o, wg, wp, params, consts, poolw, lora_w, g2_w,
          pool_hist, shift_hist, wkv_hist, y_out, pool_out, shift_out, wkv_out):
    ctx = ExitStack()
    with ctx:
        base = (nc.sbuf_base + 31) // 32 * 32
        top = [base]

        def at(name, shape, dt, addr):
            size = int(np.prod(shape[1:])) * 4
            return nc.alloc_sbuf_tensor_at(name, shape, dt, offset=addr), (addr + size + 31) // 32 * 32

        def sb(name, shape, dt=F32):
            t, top[0] = at(name, shape, dt, top[0])
            return t

        y = sb("y", [P, KT, T])
        xh_addr = top[0]
        xh = sb("xh", [P, KT, T], F32R)
        xl_addr = top[0]
        xl = sb("xl", [P, KT, T], F32R)
        w_raw = [sb(f"w_raw{i}", [P, 8, P]) for i in range(2)]
        w_hi = [sb(f"w_hi{i}", [P, 8, P], F32R) for i in range(2)]
        w_lo = [sb(f"w_lo{i}", [P, 8, P], F32R) for i in range(2)]
        cst = sb("cst", [P, NCONST])
        par = sb("par", [P, DEPTH * NPAR])
        shift_in = sb("shift_in", [P, DEPTH, NSH])
        wkv_in = sb("wkv_in", [P, DEPTH, NPAIR, 64])
        pool_w = sb("pool_w", [P, DEPTH, 2, 64])
        pool_hs = sb("pool_hs", [P, DEPTH, 2, HIST])
        pool_bd = sb("pool_bd", [P, 2, P])
        last_z = sb("last_z", [P, NSH, 2])
        eps = sb("eps", [P, 2])
        lora_all = sb("lora_all", [P, DR])
        g2_all = sb("g2_all", [P, DR])
        lora_st = sb("lora_st", [P, P])
        g2_st = sb("g2_st", [P, P])
        h_addr = top[0]
        hh = sb("hh", [P, FT, T], F32R)
        hl = sb("hl", [P, FT, T], F32R)
        sg = sb("sg", [P, T])
        hf = sb("hf", [P, T])
        sq = [sb(f"sq{i}", [P, T]) for i in range(2)]
        rs = sb("rs", [P, T])
        ysum = sb("ysum", [P, T])
        assert top[0] <= nc.sbuf_usable_end
        top[0] = h_addr
        zs = sb("zs", [P, 18, T])
        lora = sb("lora", [P, T])
        lgate = sb("lgate", [P, T])
        mix_addr = top[0]
        ar = sb("ar", [P, 2, T])
        bt = sb("bt", [P, T])
        kt = sb("kt", [P, T])
        vc = sb("vc", [P, T])
        Lb = sb("Lb", [P, T])
        Pb = sb("Pb", [P, T + 8])
        Pi = sb("Pi", [P, T])
        aa = sb("aa", [P, T])
        kkb = sb("kkb", [P, T])
        tA = sb("tA", [P, T])
        tB = sb("tB", [P, T])
        tm = sb("tm", [P, 5, 3, P])
        rhs = sb("rhs", [P, 5, 2, 2, 64])
        um = sb("um", [P, 5, P])
        wt = sb("wt", [P, T])
        S = [sb(f"S{i}", [P, P]) for i in range(2)]
        Ss = [sb(f"Ss{i}", [P, P]) for i in range(2)]
        dS = sb("dS", [P, P])
        nv, rn = Lb, tA

        def mats(name):
            return sb(name, [P, 8, P]), sb(name + "s", [TS, 2, TS])

        n16, n64, a4t, xm = mats("n16"), mats("n64"), mats("a4t"), mats("xm")
        em = a4t
        dec = sb("dec", [P, NPAIR * (NCH + 1)])
        nt = sb("nt", [P, T])
        pd = sb("pd", [P, T])
        psq = sb("psq", [P, T])
        assert top[0] <= nc.sbuf_usable_end
        a = xl_addr + 2 * T * 4
        am, a = at("am", [P, 8, 3, P], F32, a)
        ams, a = at("ams", [TS, 2, 3, TS], F32, a)
        assert a <= xl_addr + KT * T * 4
        a = xh_addr + 2 * T * 4
        t4, a = at("t4", [P, 8, P], F32, a)
        t4s, a = at("t4s", [TS, 2, TS], F32, a)
        tt, a = at("tt", [P, 8, P], F32, a)
        tts, a = at("tts", [TS, 2, TS], F32, a)
        ys, a = at("ys", [TS, 2, P], F32, a)
        y0s, a = at("y0s", [TS, 2, P], F32, a)
        prs, a = at("prs", [P, T], F32, a)
        assert a <= xh_addr + KT * T * 4
        t4, tt = (t4, t4s), (tt, tts)
        top[0] = mix_addr
        zb = [sb(f"zb{i}", [P, T + 8]) for i in range(2)]
        zd = sb("zd", [P, T])
        UW = HIST + TP + HIST + TS
        ub = [sb(f"ub{i}", [P, UW + 2]) for i in range(2)]
        swA = sb("swA", [P, UW + 2])
        swB = sb("swB", [P, UW + 2])
        pooled = [sb(f"pooled{i}", [P, T]) for i in range(2)]
        mf = [sb(f"mf{i}", [P, T]) for i in range(2)]

        ps = ctx.enter_context(nc.psum_tensor("ps", [P, 8, 512], F32))

        def pair_bank(i):
            return ps[:, i:i + 2, 0:HT]

        def halves(ap):
            return ap.rearrange("p (a b) -> p a b", a=2)

        def const(name, rows=P, cols=None):
            o, w = CCOL[name]
            return cst[0:rows, o:o + (cols or w)]

        def sem(name):
            return ctx.enter_context(nc.semaphore(name))

        loaded, x_loaded, layer_loaded, p_loaded = (sem(n) for n in ("loaded", "x_loaded", "layer_loaded", "p_loaded"))
        pool_stored, shift_stored, wkv_stored, y_stored = (sem(n) for n in ("pool_stored", "shift_stored", "wkv_stored", "y_stored"))
        w_loaded = [sem(f"w_loaded{i}") for i in range(2)]
        w_hi_done, w_split, slot_used = sem("w_hi_done"), sem("w_split"), sem("slot_used")
        tile_out = [sem(f"tile_out{i}") for i in range(2)]
        xh_ready, xl_ready, hh_ready, hl_ready = sem("xh_ready"), sem("xl_ready"), sem("hh_ready"), sem("hl_ready")
        ph_ready, pl_ready = sem("ph_ready"), sem("pl_ready")
        set_done, y_ready, sum_ready, mean_mm, d_ready = (sem(n) for n in ("set_done", "y_ready", "sum_ready", "mean_mm", "d_ready"))
        sq_ready, var_mm, rs_ready, t_ready, xf_ready, ax_ready = (
            sem(n) for n in ("sq_ready", "var_mm", "rs_ready", "t_ready", "xf_ready", "ax_ready"))
        z_set, zd_ready, last_ready, zs_ready, lora_act, u_part = (
            sem(n) for n in ("z_set", "zd_ready", "last_ready", "zs_ready", "lora_act", "u_part"))
        pool_step, pool_mm, mf_ready = sem("pool_step"), sem("pool_mm"), sem("mf_ready")
        staged, wa_mm, sig_ready, scan_ready, decay_ready, kf_ready = (
            sem(n) for n in ("staged", "wa_mm", "sig_ready", "scan_ready", "decay_ready", "kf_ready"))
        kk_ready, kksq_ready, kkn_mm, kkn_max, rn_ready, kkb_ready = (
            sem(n) for n in ("kk_ready", "kksq_ready", "kkn_mm", "kkn_max", "rn_ready", "kkb_ready"))
        ar_ready, bk_ready, vc_ready, rp_ready, rkk_ready, rk_mm, bonus_ready = (
            sem(n) for n in ("ar_ready", "bk_ready", "vc_ready", "rp_ready", "rkk_ready", "rk_mm", "bonus_ready"))
        tm_mm, tm_part, tm_ready, am_mm, am_part, am_ready = (
            sem(n) for n in ("tm_mm", "tm_part", "tm_ready", "am_mm", "am_part", "am_ready"))
        t_mm = [sem(f"t_mm{g}") for g in range(3)]
        t_part = [sem(f"t_part{g}") for g in range(3)]
        t_out = [sem(f"t_out{g}") for g in range(3)]
        n_ready = [sem(f"n_ready{g}") for g in range(3)]
        u_mm, um_ready, s_mm, ds_ready, s_ready, y_mm, yw_ready = (
            sem(n) for n in ("u_mm", "um_ready", "s_mm", "ds_ready", "s_ready", "y_mm", "yw_ready"))
        ss_part, ss_init, ss_done = sem("ss_part"), sem("ss_init"), sem("ss_done")
        g_staged, pm_mm, pg_mm, pd_ready, psq_ready, pv_mm, prs_ready = (
            sem(n) for n in ("g_staged", "pm_mm", "pg_mm", "pd_ready", "psq_ready", "pv_mm", "prs_ready"))
        pt_ready, pi_ready, pb_ready, po_ready, fin_ready = (
            sem(n) for n in ("pt_ready", "pi_ready", "pb_ready", "po_ready", "fin_ready"))
        ln_newton, kk_newton, hn_newton = sem("ln_newton"), sem("kk_newton"), sem("hn_newton")
        NLOAD = 6

        def flat(ap):
            return ap.rearrange("p a t -> p (a t)")

        def row(t, i):
            return flat(t[:, bass.ds(i, 1), :])

        def col(l, c):
            return par[:, bass.ds(l * NPAR + c, 1)]

        def out_count(l, name, m):
            return l * (TILES // 2) + TILE0[name] // 2 + m + 1

        def used_count(l, name, i):
            return l * SLOTS + SLOT0[name] + i + 3

        def group_view(g, wide):
            n, U = (P, 4) if g < 2 else (TS, 2)
            return ps[0:n, g, 0:U * P].rearrange("p (u c) -> p u c", u=U)[:, :, 0:wide]

        def a_view(g):
            n, tiles = (P, 2) if g < 2 else (TS, 1)
            return ps[0:n, 3:5, 0:tiles * P].rearrange("p h (j c) -> p h j c", j=tiles)[:, :, :, 0:n]

        def a_units(m, g):
            return units(m, g).rearrange("p (j h) c -> p h j c", h=2)

        def a_spread(name, g):
            n, tiles = (P, 2) if g < 2 else (TS, 1)
            return const(name, n, n).unsqueeze(1).unsqueeze(1).to_broadcast([n, 2, tiles, n])

        def units(m, g):
            return m[0][:, 4 * g:4 * g + 4, :] if g < 2 else m[1][:, :, :]

        def spread(name, g):
            n, U = (P, 4) if g < 2 else (TS, 2)
            return const(name, n, n).unsqueeze(1).to_broadcast([n, U, n])

        block = ctx.enter_context(nc.Block())

        SLOTS_A, SLOTS_B = 13, 14

        def heads(eng, l, half_a, half_b, prepare_1, prepare_2, normalise):
            for k in range(SLOTS_A):
                prepare_1(l, 0, k, True)
            for k in range(SLOTS_B):
                prepare_2(l, 0, k, True)
            half_a(l, 0, True, False, True)
            half_b(l, 0, True, False)
            with eng.Fori(0, NPAIR - 2) as q:
                half_a(l, q + 1, True, True, True)
                half_b(l, q + 1, True, True)
            half_a(l, NPAIR - 1, True, True, False)
            half_b(l, NPAIR - 1, False, True)
            half_a(l, NPAIR, False, True, False)
            for k in range(SLOTS_B):
                normalise(l, NPAIR - 1, k, True)

        @block.sync
        def _(sp):
            sp.dma_start(y[:, :, :], xT).then_inc(x_loaded, 16)
            for dst, src in ((cst[:, :], consts), (par[:, :], params), (shift_in[:, :, :], shift_hist),
                             (wkv_in[:, :, :, :], wkv_hist), (pool_w[:, :, :, :], poolw), (pool_hs[:, :, :, :], pool_hist)):
                sp.dma_start(dst, src).then_inc(loaded, 16)
            arrays = {"f1i": w1i, "f1o": w1o, "z": wz, "wo": wo, "f2i": w2i, "f2o": w2o}
            with sp.Fori(0, DEPTH) as l:
                sp.wait_ge(xl_ready, l * 40)
                sp.dma_start(lora_all[:, :], flat(lora_w[bass.ds(l, 1)].rearrange("a p n -> p a n"))).then_inc(layer_loaded, 16)
                sp.dma_start(g2_all[:, :], flat(g2_w[bass.ds(l, 1)].rearrange("a p n -> p a n"))).then_inc(layer_loaded, 16)
                for name, bodies, ks in PHASES:
                    B = len(ks)
                    if name == "f2o":
                        sp.wait_ge(var_mm, l * 24 + 16)
                        for k in range(2):
                            sp.dma_start(sq[k][:, :], flat(pT[bass.ds(l, 1), :, k, :].rearrange("a p t -> p a t"))).then_inc(p_loaded, 16)
                    with sp.Fori(0, bodies) as m:
                        for i, nk in enumerate(ks):
                            if name == "gp":
                                src = (wg, wp)[i][bass.ds(l * 8 + m, 1)]
                            elif name in ("f1o", "f2o"):
                                k0 = (0, 8, 15)[i % 3]
                                src = arrays[name][bass.ds(l * 8 + m * 2 + i // 3, 1), :, k0:k0 + nk, :]
                            else:
                                src = arrays[name][bass.ds(l * (bodies * B) + m * B + i, 1)]
                            sp.wait_ge(w_split, l * SLOTS + SLOT0[name] + m * B + i + 1)
                            sp.dma_start(w_raw[i % 2][:, 0:nk, :], src.rearrange("a p k n -> p (a k) n")).then_inc(w_loaded[i % 2], 16)
            for m in range(KT):
                sp.wait_ge(fin_ready, m + 1)
                sp.dma_start(y_out[:, m, :], y[:, m, :]).then_inc(y_stored, 16)
            sp.wait_ge(y_stored, 16 * KT)
            sp.wait_ge(pool_stored, DEPTH * 64)
            sp.wait_ge(shift_stored, DEPTH * 16)
            sp.wait_ge(wkv_stored, DEPTH * NPAIR * 64)

        @block.gpsimd
        def _(pool):
            pool.sem_inc(w_split, 2)

            def prepare_1(l, p, k, first):
                pass

            def prepare_2(l, p, k, first):
                n = l * NPAIR + p
                if k == 8:
                    pool.wait_ge(kf_ready, n * 2 + 2)
                    pool.wait_ge(ar_ready, n * 3 + 1)
                    pool.tensor_tensor(kt[:, :], tB[:, :], Pi[:, :], ALU.mult).then_inc(bk_ready, 1)
                    pool.wait_ge(kkb_ready, n + 1)
                    pool.tensor_tensor(bt[:, :], kkb[:, :], aa[:, :], ALU.mult).then_inc(bk_ready, 1)
                    pool.wait_ge(bk_ready, n * 3 + 2)
                    pool.tensor_tensor(bt[:, :], bt[:, :], Pi[:, :], ALU.mult).then_inc(bk_ready, 1)

            def normalise(l, p, k, last):
                if k == 11:
                    pool.wait_ge(hn_newton, (l * NPAIR + p) * 3 + 3)
                    pool.tensor_tensor(pd[:, :], pd[:, :], prs[:, :], ALU.mult).then_inc(pt_ready, 1)

            def half_a(l, p, left, right, nxt):
                pass

            def half_b(l, p, nxt, norm_before):
                for k in range(SLOTS_B):
                    if nxt:
                        prepare_2(l, p + 1, k, False)
                    if norm_before:
                        normalise(l, p - 1, k, False)

            with pool.Fori(0, DEPTH) as l:
                for name, bodies, ks in PHASES:
                    B = len(ks)
                    if name == "wo":
                        heads(pool, l, half_a, half_b, prepare_1, prepare_2, normalise)
                    with pool.Fori(0, bodies) as m:
                        for i, nk in enumerate(ks):
                            n, k = l * SLOTS + SLOT0[name] + m * B + i, i % 2
                            pool.wait_ge(w_loaded[k], (l * (SLOTS // 2) + m * (B // 2) + (SLOT0[name] // 2 + i // 2 + 1)) * 16)
                            due = pool.to_reg(n + 1)
                            pool.wait_ge(w_split, 2)
                            pool.wait_ge(slot_used, due)
                            pool.tensor_scalar(w_hi[k][:, 0:nk, :], w_raw[k][:, 0:nk, :], 1.0, 0.0, ALU.mult, ALU.add).then_inc(w_hi_done, 1)
                            pool.wait_ge(w_hi_done, n + 1)
                            pool.tensor_tensor(w_lo[k][:, 0:nk, :], w_raw[k][:, 0:nk, :], w_hi[k][:, 0:nk, :].bitcast(F32),
                                               ALU.subtract).then_inc(w_split, 1)

        @block.tensor
        def _(pe):
            pe.sem_inc(slot_used, 2)
            pe.sem_inc(y_mm, 5)

            def constants_there():
                pe.wait_ge(loaded, 16 * NLOAD)

            constants_there()

            def dense(l, name, hi, lo):
                _, bodies, ks = next(p for p in PHASES if p[0] == name)
                B = len(ks)
                per = B // 2
                with pe.Fori(0, bodies) as m:
                    for i, nk in enumerate(ks):
                        k, pair, part = i % 2, i // per, i % per
                        n = l * SLOTS + SLOT0[name] + m * B + i
                        if part == 0:
                            pe.wait_ge(tile_out[pair], out_count(l, name, m) - 1)
                        pe.wait_ge(w_split, n + 3)
                        x_hi, x_lo = (hh, hl) if name == "gp" and i == 1 else (hi, lo)
                        k0 = (0, 8, 15)[part]
                        for j in range(nk):
                            for q, (w, x) in enumerate(((w_hi[k], x_hi), (w_hi[k], x_lo), (w_lo[k], x_hi))):
                                for h in range(2):
                                    mm = pe.matmul(ps[:, 2 * pair + h, 0:HT], w[:, j, :], x[:, k0 + j, h * HT:(h + 1) * HT],
                                                   start=(part == 0 and j == 0 and q == 0),
                                                   stop=(part == per - 1 and j == nk - 1 and q == 2))
                        mm.then_inc(slot_used, 1)

            def two(bank, lhsT, r, start=True, stop=True):
                for h in range(2):
                    mm = pe.matmul(ps[:, bank + h, 0:HT], lhsT, r[:, h * HT:(h + 1) * HT], start=start, stop=stop)
                return mm

            def norm(inst):
                pe.wait_ge(sum_ready, inst * 9 + 9)
                two(4, const("mean_d"), ysum).then_inc(mean_mm, 1)
                for m in range(KT):
                    pe.wait_ge(sq_ready, inst * 8 + m + 1)
                    two(6, const("mean_d"), sq[m % 2], m == 0, m == KT - 1).then_inc(var_mm, 1)

            def step(s, g, n):
                name, tiles, rows = STEPS[s], GROUPS[g], (P if g < 2 else TS)
                due, blocks = pe.to_reg(n * NSTEP + s), pe.to_reg(n * 2 + 2)
                if g == 2:
                    constants_there()
                if name == "A":
                    if g == 2:
                        pe.wait_ge(n_ready[1], blocks)
                    else:
                        pe.wait_ge(am_ready, n * 10 + (4, 10)[g])
                if name == "E16":
                    pe.wait_ge(n_ready[g], blocks)
                pe.wait_ge(t_out[g], due)
                if name == "WT":
                    for q, j in enumerate(tiles):
                        src = xm[0][:, 2 * j, :] if g < 2 else ys[:, 0, :]
                        mm = pe.transpose(ps[:, g, q * P:q * P + rows], src, const("ident", rows, rows))
                    mm.then_inc(t_mm[g], 1)
                    return
                for q, (j, h) in enumerate((j, h) for j in tiles for h in range(2)):
                    u, hs, ts = 2 * j + h, slice(64 * h, 64 * h + 64), slice(j * P, j * P + rows)

                    def mat(m):
                        return m[0][:, u, :] if g < 2 else m[1][:, h, :]

                    b, o = (3 + h, q // 2 * P) if name == "A" else (g, q * P)
                    out = ps[0:rows, b, o:o + (P if name[0] == "Y" else 64 if name == "G" else rows)]
                    if name in ("T4T", "T16T"):
                        mm = pe.transpose(out, mat(t4 if name == "T4T" else xm), const("ident", rows, rows))
                        continue
                    y0v = t4[0][:, u, :] if g < 2 else y0s[:, h, :]
                    yv = xm[0][:, u, :] if g < 2 else ys[:, h, :]
                    lhsT, r = {
                        "A": (ar[hs, 0, ts], bt[hs, ts]), "H1": (mat(a4t), mat(xm)), "H2": (mat(a4t), mat(xm)),
                        "E16": (mat(n16), mat(tt)), "X1": (mat(em), mat(t4)), "X2": (mat(em), mat(xm)),
                        "X3": (mat(em), mat(xm)), "E64": (mat(n64), mat(tt)),
                        "G": (am[:, u, 1, :] if g < 2 else ams[:, h, 1, :], tm[0:rows, j, 2, hs]),
                        "Y0": (mat(tt), rhs[0:rows, j, h, :, :].rearrange("p a b -> p (a b)")),
                        "Y1": (mat(em), y0v), "Y2": (mat(em), yv), "Y3": (mat(em), yv),
                    }[name]
                    mm = pe.matmul(out, lhsT, r, start=True, stop=True)
                mm.then_inc(t_mm[g], 1)

            def chunk_in(c, l, p):
                n = l * NPAIR + p
                j, ro, rows = (c // 2, 64 * (c % 2), CH) if c < NCH else (4, 0, TS)
                st = S[c % 2] if c < NCH else Ss[0]
                ts = slice(c * CH, c * CH + rows)
                if c == 0:
                    return
                if c in (1, 4, 8):
                    pe.wait_ge(t_out[(1, 4, 8).index(c)], n * NSTEP + NSTEP)
                if c < NCH:
                    pe.wait_ge(s_ready, n * 8 + c)
                else:
                    pe.wait_ge(ss_init, n + 1)
                pe.matmul(ps[ro:ro + rows, 5, 0:P], wt[:, ts], st[:, :], start=True, stop=True).then_inc(u_mm, 1)
                first = c in (1, 2, 4, 6, 8)
                if first:
                    pe.wait_ge(yw_ready, n * 5 + j)
                    pe.wait_ge(rp_ready, n + 1)
                pe.matmul(ps[:, 7, ro:ro + rows], st[:, :], flat(zs[:, bass.ds(p, 1), ts]), start=first, stop=True, skip_group_check=True)

            def chunk_out(c, l, p):
                n = l * NPAIR + p
                j, ro, rows = (c // 2, 64 * (c % 2), CH) if c < NCH else (4, 0, TS)
                pe.wait_ge(um_ready, n * 9 + c + 1)
                pe.matmul(ps[:, 6, 0:P], tm[ro:ro + rows, j, 0, :], um[ro:ro + rows, j, :], start=True, stop=False)
                pe.matmul(ps[:, 6, 0:P], tm[ro:ro + rows, j, 1, :], tm[ro:ro + rows, j, 2, :], start=False, stop=True).then_inc(s_mm, 1)
                if c % 2 == 1 or c == NCH:
                    m = P if j < 4 else TS
                    for h in range(2):
                        hs = slice(64 * h, 64 * h + 64)
                        for src, q in ((um[0:m, j, hs], 0), (tm[0:m, j, 2, hs], 2)):
                            mm = pe.matmul(ps[hs, 7, 0:m], src, am[:, 2 * j + h, q, :] if j < 4 else ams[:, h, q, :],
                                           start=False, stop=True, skip_group_check=True)
                    mm.then_inc(y_mm, 1)

            def token_major(j, n, used):
                rows = P if j < 4 else TS
                for who, count in used:
                    pe.wait_ge(who, count)
                for q, src in enumerate((ar[:, 0, :], bt[:, :], kt[:, :], vc[:, :])):
                    mm = pe.transpose(ps[0:rows, 3 + j % 2, q * P:(q + 1) * P], src[:, j * P:j * P + rows], const("ident"))
                mm.then_inc(tm_mm, 1)

            def products(u, n):
                j, h = u // 2, u % 2
                rows, hs = (P if j < 4 else TS), slice(64 * h, 64 * h + 64)
                if u in (0, 4):
                    pe.wait_ge(tm_ready, n * 5 + (2 if u == 0 else 5))
                elif u not in (1, 5):
                    due = pe.to_reg(n * 10 + u - 1)
                    if j == 4:
                        constants_there()
                    pe.wait_ge(am_ready, due)
                for q, src in enumerate((bt, kt)):
                    mm = pe.matmul(ps[0:rows, 3 + u % 2, 2 * q * rows:2 * (q + 1) * rows].rearrange("p (a t) -> p a t", a=2),
                                   src[hs, j * P:j * P + rows], ar[hs, :, j * P:j * P + rows], start=(q == 0), stop=True,
                                   skip_group_check=True)
                mm.then_inc(am_mm, 1)

            def prepare_1(l, p, k, first):
                n = l * NPAIR + p
                if k == 5:
                    if not first:
                        pe.wait_ge(n_ready[0], n * 2)
                    pe.wait_ge(staged, n + 1)
                    two(3, lora_st[0:64, :], lora[0:64, :]).then_inc(wa_mm, 1)
                if k == 6:
                    pe.wait_ge(sig_ready, n * 2 + 1)
                    two(3, lora_st[64:128, :], lora[64:128, :]).then_inc(wa_mm, 1)
                if k == 8:
                    pe.wait_ge(sig_ready, n * 2 + 2)
                    pe.wait_ge(kksq_ready, n + 1)
                    two(3, const("head_sum"), tA).then_inc(kkn_mm, 1)

            def prepare_2(l, p, k, first):
                n = l * NPAIR + p
                if k == 7:
                    if first:
                        pe.wait_ge(kkn_max, n + 1)
                    else:
                        pe.wait_ge(n_ready[2], n * 2)
                    pe.wait_ge(rkk_ready, n + 1)
                    two(3, const("head_sum"), tA).then_inc(rk_mm, 1)

            def normalise(l, p, k, last):
                n = l * NPAIR + p
                if k == 8:
                    pe.wait_ge(po_ready, n)
                    if not last:
                        pe.wait_ge(n_ready[2], n * 2 + 4)
                        if not isinstance(p, int):
                            pe.wait_ge(bonus_ready, n + 3)
                    pe.wait_ge(yw_ready, n * 5 + 5)
                    for h in range(2):
                        mm = pe.matmul(ps[:, 3 + h, 0:HT], const("head_mean"), flat(zs[:, bass.ds(p, 1), h * HT:(h + 1) * HT]),
                                       start=True, stop=True)
                    mm.then_inc(pm_mm, 1)
                if k == 10:
                    pe.wait_ge(psq_ready, n + 1)
                    two(3, const("head_mean"), psq).then_inc(pv_mm, 1)
                if k == 12:
                    pe.wait_ge(hn_newton, n * 3 + 3)
                    pe.wait_ge(g_staged, n + 1)
                    two(3, g2_st[:, :], lgate).then_inc(pg_mm, 1)

            def half_a(l, p, left, right, nxt):
                n = l * NPAIR + p
                for k in range(SLOTS_A):
                    if right and k < 8:
                        step(8 + k, 1, n - 1)
                        step(8 + k, 2, n - 1)
                    if right and k >= 8:
                        chunk_in(k - 4, l, p - 1)
                    if left and k < 2:
                        used = []
                        if k == 0:
                            used = [(ar_ready, n * 3 + 3), (bk_ready, n * 3 + 3), (vc_ready, n + 1), (bonus_ready, n + 1)]
                            if right:
                                used.append((po_ready, n - 1))
                        token_major(k, n, used)
                    elif left and k < 4:
                        products(2 * k - 4, n)
                        products(2 * k - 3, n)
                    elif left and k < 12:
                        step(k - 4, 0, n)
                    if right and k >= 8:
                        chunk_out(k - 4, l, p - 1)
                    if nxt:
                        prepare_1(l, p + 1, k, False)

            def half_b(l, p, nxt, norm_before):
                n = l * NPAIR + p
                for k in range(SLOTS_B):
                    if k < 8:
                        step(8 + k, 0, n)
                    elif k < 12:
                        chunk_in(k - 8, l, p)
                    if k == 0:
                        token_major(2, n, [(n_ready[0], n * 2 + 2)] + ([(kkn_max, n + 2)] if nxt else []))
                    elif k == 1:
                        token_major(3, n, [])
                        token_major(4, n, [(tm_ready, n * 5 + 3)])
                    elif k < 5:
                        products(2 * k, n)
                        products(2 * k + 1, n)
                    if 5 <= k < 13:
                        step(k - 5, 1, n)
                    if 6 <= k:
                        step(k - 6, 2, n)
                    if 8 <= k < 12:
                        chunk_out(k - 8, l, p)
                    if nxt:
                        prepare_2(l, p + 1, k, False)
                    if norm_before:
                        normalise(l, p - 1, k, False)

            with pe.Fori(0, DEPTH) as l:
                due = pe.to_reg(l * 40 + 8)
                constants_there()
                pe.wait_ge(xl_ready, due)
                dense(l, "f1i", xh, xl)
                due = pe.to_reg(l * (2 * FT) + FT)
                constants_there()
                pe.wait_ge(hl_ready, due)
                dense(l, "f1o", hh, hl)
                norm(l * 3)
                due = pe.to_reg(l * 40 + 16)
                constants_there()
                pe.wait_ge(xl_ready, due)
                dense(l, "z", xh, xl)
                for q in range(2):
                    pe.wait_ge(pool_step, l * 16 + (7, 16)[q])
                    two(4 + 2 * q, pool_bd[:, q, :], pooled[q]).then_inc(pool_mm, 1)
                pe.wait_ge(xl_ready, l * 40 + 18)
                heads(pe, l, half_a, half_b, prepare_1, prepare_2, normalise)
                due = pe.to_reg(l * 40 + 24)
                constants_there()
                pe.wait_ge(xl_ready, due)
                dense(l, "wo", xh, xl)
                norm(l * 3 + 1)
                due = pe.to_reg(l * 40 + 32)
                constants_there()
                pe.wait_ge(xl_ready, due)
                dense(l, "f2i", xh, xl)
                due = pe.to_reg(l * (2 * FT) + 2 * FT)
                constants_there()
                pe.wait_ge(hl_ready, due)
                dense(l, "f2o", hh, hl)
                due = pe.to_reg(l * 40 + 40)
                constants_there()
                pe.wait_ge(xl_ready, due)
                due = pe.to_reg(l * 2 + 2)
                constants_there()
                pe.wait_ge(pl_ready, due)
                dense(l, "gp", xh, xl)
                norm(l * 3 + 2)

        @block.scalar
        def _(act):
            act.wait_ge(set_done, 3)
            act.wait_ge(loaded, 16 * NLOAD)
            act.wait_ge(x_loaded, 16)
            for m in range(KT):
                act.activation(xh[:, m, :], y[:, m, :], ACT.Copy).then_inc(xh_ready, 1)

            def ffn(l, which, name):
                with act.Fori(0, FT) as m:
                    act.wait_ge(slot_used, used_count(l, name, 2 * m))
                    act.wait_ge(tile_out[1], out_count(l, name, m) - 1)
                    act.activation(halves(sg[:, :]), pair_bank(0), ACT.Silu).then_inc(tile_out[0], 1)
                    act.wait_ge(tile_out[1], out_count(l, name, m))
                    act.activation(row(hh, m), hf[:, :], ACT.Copy).then_inc(hh_ready, 1)

            def norm(l, which, g, b):
                inst = l * 3 + which
                for m in range(KT):
                    act.wait_ge(d_ready, inst * 8 + m + 1)
                    if m >= 2:
                        act.wait_ge(var_mm, inst * 8 + m - 1)
                    act.activation(sq[m % 2][:, :], y[:, m, :], ACT.Square).then_inc(sq_ready, 1)
                act.wait_ge(var_mm, inst * 8 + 8)
                act.activation(halves(rs[:, :]), pair_bank(6), ACT.Abs_reciprocal_sqrt, bias=eps[:, 0:1]).then_inc(rs_ready, 1)
                for m in range(KT):
                    act.wait_ge(t_ready, inst * 8 + m + 1)
                    act.activation(y[:, m, :], y[:, m, :], ACT.Identity, scale=col(l, g + m), bias=col(l, b + m)).then_inc(xf_ready, 1)
                    act.wait_ge(xf_ready, inst * 8 + m + 1)
                    act.activation(xh[:, m, :], y[:, m, :], ACT.Copy).then_inc(xh_ready, 1)

            def z_copy(l, m, k):
                act.wait_ge(slot_used, used_count(l, "z", 2 * m + k))
                act.wait_ge(zs_ready, l * NSH + 2 * m + k + 1)
                act.activation(halves(zb[k][:, 1:T + 1]), pair_bank(2 * k), ACT.Copy).then_inc(tile_out[k], 1)

            def prepare_1(l, p, k, first):
                n = l * NPAIR + p
                if k == 3:
                    act.wait_ge(kk_ready, n + 1)
                    act.activation(tA[:, :], kkb[:, :], ACT.Square).then_inc(kksq_ready, 1)
                if k == 5:
                    act.wait_ge(bk_ready, n * 3)
                    act.wait_ge(wa_mm, n * 2 + 1)
                    act.activation(halves(tB[:, :]), pair_bank(3), ACT.Sigmoid, bias=col(l, p + COL["w0"])).then_inc(sig_ready, 1)
                if k == 6:
                    act.wait_ge(wa_mm, n * 2 + 2)
                    act.activation(halves(aa[:, :]), pair_bank(3), ACT.Sigmoid, bias=col(l, p + COL["a0"])).then_inc(sig_ready, 1)
                if k == 7:
                    act.wait_ge(scan_ready, n + 1)
                    act.activation(Pb[:, 1:T + 1], Lb[:, :], ACT.Exp, scale=-DECAY).then_inc(decay_ready, 1)
                    act.activation(Pi[:, :], Lb[:, :], ACT.Exp, scale=DECAY).then_inc(decay_ready, 1)
                    act.activation(dec[:, bass.ds(p * (NCH + 1), NCH)], Lb[:, CH - 1:TP:CH], ACT.Exp, scale=-DECAY).then_inc(decay_ready, 1)
                    act.activation(dec[:, bass.ds(p * (NCH + 1) + NCH, 1)], Lb[:, T - 1:T], ACT.Exp, scale=-DECAY).then_inc(decay_ready, 1)
                if k == 8:
                    act.wait_ge(kkn_max, n + 1)
                    act.activation(rn[:, :], nv[:, :], ACT.Abs_reciprocal_sqrt).then_inc(rn_ready, 1)

            def prepare_2(l, p, k, first):
                n = l * NPAIR + p
                if k == 6:
                    act.activation(vc[:, :], row(zs, p + 12), ACT.Copy).then_inc(vc_ready, 1)
                if k == 9:
                    act.wait_ge(rkk_ready, n + 1)
                    act.wait_ge(ar_ready, n * 3 + 1)
                    act.activation(row(zs, p), ar[:, 1, :], ACT.Copy).then_inc(rp_ready, 1)

            def normalise(l, p, k, last):
                n = l * NPAIR + p
                if k == 9:
                    act.wait_ge(pd_ready, n + 1)
                    act.activation(psq[:, :], pd[:, :], ACT.Square).then_inc(psq_ready, 1)
                if k == 10:
                    act.wait_ge(pv_mm, n + 1)
                    act.activation(halves(prs[:, :]), pair_bank(3), ACT.Abs_reciprocal_sqrt, bias=eps[:, 1:2]).then_inc(prs_ready, 1)
                if k == 12:
                    act.wait_ge(pt_ready, n + 1)
                    act.activation(psq[:, :], pd[:, :], ACT.Identity, scale=col(l, p + COL["lnx_g"]), bias=col(l, p + COL["lnx_b"])).then_inc(pi_ready, 1)

            def token_major(j, n):
                rows, b = (P if j < 4 else TS), 3 + j % 2
                act.wait_ge(tm_mm, n * 5 + j + 1)
                act.activation(rhs[0:rows, j, :, 0, :], ps[0:rows, b, 0:P].rearrange("p (h c) -> p h c", h=2), ACT.Copy).then_inc(tm_part, 1)
                act.activation(tm[0:rows, j, :, :].rearrange("p a b -> p (a b)"), ps[0:rows, b, P:4 * P], ACT.Copy).then_inc(tm_ready, 1)

            def step(s, g, n):
                name, tiles = STEPS[s], GROUPS[g]
                if name not in ("T4T", "T16T", "E16", "E64", "G", "Y0", "WT"):
                    return
                rows, nt_ = (P if g < 2 else TS), len(tiles)
                act.wait_ge(t_mm[g], n * NSTEP + s + 1)
                if name == "WT":
                    out, src = wt[:, tiles[0] * P:tiles[0] * P + rows * nt_], ps[:, g, 0:rows * nt_]
                elif name == "G":
                    out = rhs[0:rows, tiles[0]:tiles[0] + nt_, :, 1, :].rearrange("p j h c -> p (j h) c")
                    src = group_view(g, 64)
                elif name == "Y0":
                    out, src = (units(t4, g) if g < 2 else y0s[:, :, :]), group_view(g, P)
                else:
                    out, src = units(tt if name[0] == "T" else em, g), group_view(g, rows)
                act.activation(out, src, ACT.Copy).then_inc(t_out[g], 1)

            def y_tile(j, l, p):
                rows = P if j < 4 else TS
                act.wait_ge(y_mm, (l * NPAIR + p) * 5 + j + 6)
                act.activation(flat(zs[:, bass.ds(p, 1), j * P:j * P + rows]), ps[:, 7, 0:rows], ACT.Copy).then_inc(yw_ready, 1)

            def half_a(l, p, left, right, nxt):
                n = l * NPAIR + p
                for k in range(SLOTS_A):
                    if right and k < 8:
                        step(8 + k, 1, n - 1)
                        step(8 + k, 2, n - 1)
                    if left and k < 2:
                        token_major(k, n)
                    if left and 4 <= k < 12:
                        step(k - 4, 0, n)
                    if right and k in (9, 11, 12):
                        y_tile({9: 2, 11: 3, 12: 4}[k], l, p - 1)
                    if nxt:
                        prepare_1(l, p + 1, k, False)
                if right:
                    act.wait_ge(s_ready, n * 8)
                    act.wait_ge(ss_done, n)
                    for q, st in enumerate((S[0], Ss[1])):
                        for h in range(2):
                            hs = slice(64 * h, 64 * h + 64)
                            act.dma_start(wkv_out[bass.ds(n - 1, 1), q, hs, :].rearrange("a p v -> p (a v)"), st[hs, hs]).then_inc(wkv_stored, 16)

            def half_b(l, p, nxt, norm_before):
                n = l * NPAIR + p
                for k in range(SLOTS_B):
                    if k < 8:
                        step(8 + k, 0, n)
                    if k == 0:
                        token_major(2, n)
                    if k == 1:
                        token_major(3, n)
                        token_major(4, n)
                    if 5 <= k < 13:
                        step(k - 5, 1, n)
                    if 6 <= k:
                        step(k - 6, 2, n)
                    if k in (9, 11):
                        y_tile({9: 0, 11: 1}[k], l, p)
                    if nxt:
                        prepare_2(l, p + 1, k, False)
                    if norm_before:
                        normalise(l, p - 1, k, False)

            with act.Fori(0, DEPTH) as l:
                ffn(l, 0, "f1i")
                norm(l, 0, COL["ln1_g"], COL["ln1_b"])
                act.wait_ge(z_set, l + 1)
                with act.Fori(0, 9) as m:
                    for k in range(2):
                        z_copy(l, m, k)
                for k in range(2):
                    z_copy(l, 9, k)
                act.wait_ge(zs_ready, l * NSH + 19 + 2)
                act.activation(lora[0:64, :], lora[0:64, :], ACT.Tanh).then_inc(lora_act, 1)
                act.wait_ge(zs_ready, l * NSH + 20 + 2)
                act.activation(lgate[:, :], lgate[:, :], ACT.Sigmoid).then_inc(lora_act, 1)
                for q in range(2):
                    act.wait_ge(slot_used, used_count(l, "z", 20 + q))
                    act.activation(ub[q][:, HIST:HIST + HT], ps[:, 2 * q, 0:HT], ACT.Copy).then_inc(u_part, 1)
                    act.activation(ub[q][:, UW - TS:UW], ps[:, 2 * q + 1, TP - HT:HT], ACT.Copy).then_inc(u_part, 1)
                    act.activation(ub[q][:, HIST + HT:HIST + TP], ps[:, 2 * q + 1, 0:TP - HT], ACT.Copy).then_inc(tile_out[q], 1)
                    act.wait_ge(tile_out[q], out_count(l, "z", 10))
                    for s, a in enumerate((TP, UW - HIST)):
                        act.dma_start(pool_out[bass.ds(l, 1), s, :, q, :].rearrange("a p t -> p (a t)"),
                                      ub[q][:, a:a + HIST]).then_inc(pool_stored, 16)
                for q in range(2):
                    act.wait_ge(pool_mm, l * 2 + q + 1)
                    act.activation(halves(mf[q][:, :]), pair_bank(4 + 2 * q), ACT.Identity, scale=col(l, COL["pool_scale"] + q)).then_inc(mf_ready, 1)
                    act.wait_ge(mf_ready, l * 2 + q + 1)
                    act.activation(xh[:, q, :], mf[q][:, :], ACT.Copy).then_inc(xh_ready, 1)
                act.wait_ge(last_ready, l * NSH + NSH)
                act.dma_start(shift_out[bass.ds(l, 1)].rearrange("a p k s -> p (a k) s"), last_z[:, :, :]).then_inc(shift_stored, 16)
                heads(act, l, half_a, half_b, prepare_1, prepare_2, normalise)
                with act.Fori(0, NPAIR) as p:
                    act.wait_ge(po_ready, (l + 1) * NPAIR)
                    act.activation(row(xh, p + 2), row(zs, p), ACT.Copy).then_inc(xh_ready, 1)
                norm(l, 1, COL["ln2_g"], COL["ln2_b"])
                act.wait_ge(wkv_stored, (l + 1) * (NPAIR * 64))
                ffn(l, 1, "f2i")
                with act.Fori(0, 4) as m:
                    for k in range(2):
                        act.wait_ge(tile_out[k], out_count(l, "f2o", m))
                        act.activation(row(xh, 2 * m + k), row(y, 2 * m + k), ACT.Copy).then_inc(xh_ready, 1)
                act.wait_ge(p_loaded, l * 32 + 32)
                act.wait_ge(slot_used, used_count(l, "f2o", 23))
                for k in range(2):
                    act.activation(hh[:, k, :], sq[k][:, :], ACT.Copy).then_inc(ph_ready, 1)
                with act.Fori(0, 8) as m:
                    act.wait_ge(slot_used, used_count(l, "gp", 2 * m))
                    act.wait_ge(tile_out[1], out_count(l, "gp", m) - 1)
                    act.activation(halves(sg[:, :]), pair_bank(0), ACT.Sigmoid, bias=col(l, m + COL["gate_b"])).then_inc(tile_out[0], 1)
                norm(l, 2, COL["ln3_g"], COL["ln3_b"])

        @block.vector
        def _(dve):
            dve.memset(eps[:, 0:1], LN_EPS).then_inc(set_done, 1)
            dve.memset(eps[:, 1:2], LNX_EPS).then_inc(set_done, 1)
            dve.memset(pool_bd[:, :, :], 0.0).then_inc(set_done, 1)
            dve.sem_inc(zs_ready, 2)
            dve.wait_ge(loaded, 16 * NLOAD)

            def low_parts(m, count):
                dve.wait_ge(xh_ready, count)
                dve.tensor_tensor(xl[:, m, :], y[:, m, :], xh[:, m, :].bitcast(F32), ALU.subtract).then_inc(xl_ready, 1)
                dve.tensor_scalar(y[:, m, :], y[:, m, :], ALPHA, None, ALU.mult).then_inc(ax_ready, 1)

            pv = par[:, :].rearrange("p (l c) -> p l c", l=DEPTH)[:, :, COL["one_ka"]:COL["one_ka"] + NPAIR]
            dve.tensor_scalar(pv, pv, -1.0, 1.0, ALU.mult, ALU.add)
            for m in range(KT):
                low_parts(m, m + 1)

            def ffn(l, which, name):
                with dve.Fori(0, FT) as m:
                    f = l * (2 * FT) + which * FT + m
                    dve.wait_ge(slot_used, used_count(l, name, 2 * m + 1))
                    dve.wait_ge(tile_out[0], out_count(l, name, m))
                    dve.wait_ge(hl_ready, f)
                    dve.tensor_tensor(halves(hf[:, :]), halves(sg[:, :]), pair_bank(2), ALU.mult).then_inc(tile_out[1], 1)
                    dve.wait_ge(hh_ready, f + 1)
                    dve.tensor_tensor(row(hl, m), hf[:, :], row(hh, m).bitcast(F32), ALU.subtract).then_inc(hl_ready, 1)

            def residual(l, inst, name, scale, parts):
                if parts is None:
                    dve.memset(ysum[:, :], 0.0).then_inc(sum_ready, 1)
                due = dve.to_reg(inst * 8 + 8)
                dve.wait_ge(loaded, 16 * NLOAD)
                dve.wait_ge(ax_ready, due)
                per = 3 if name in ("f1o", "f2o") else 1
                with dve.Fori(0, 4) as m:
                    for k in range(2):
                        dve.wait_ge(slot_used, used_count(l, name, 2 * per * m + per * k + per - 1))
                        dve.scalar_tensor_tensor(halves(row(y, 2 * m + k)), pair_bank(2 * k), scale, halves(row(y, 2 * m + k)),
                                                 ALU.mult, ALU.add).then_inc(tile_out[k], 1)
                        if parts is None:
                            dve.wait_ge(tile_out[k], out_count(l, name, m))
                            dve.wait_ge(sum_ready, inst * 9 + 2 * m + k + 1)
                            dve.tensor_tensor(ysum[:, :], ysum[:, :], row(y, 2 * m + k), ALU.add).then_inc(sum_ready, 1)
                        else:
                            dve.wait_ge(xh_ready, parts + 2 * m + k + 1)
                            dve.tensor_tensor(row(xl, 2 * m + k), row(y, 2 * m + k), row(xh, 2 * m + k).bitcast(F32),
                                              ALU.subtract).then_inc(xl_ready, 1)

            def newton(r, tmp, v, bias, steps, count):
                dve.scalar_tensor_tensor(halves(tmp), v, bias, halves(r), ALU.add, ALU.mult).then_inc(steps, 1)
                dve.wait_ge(steps, count + 1)
                dve.scalar_tensor_tensor(tmp, tmp, -0.5, r, ALU.mult, ALU.mult).then_inc(steps, 1)
                dve.wait_ge(steps, count + 2)
                dve.scalar_tensor_tensor(r, tmp, 1.5, r, ALU.add, ALU.mult).then_inc(steps, 1)

            def norm(inst, count):
                dve.wait_ge(mean_mm, inst + 1)
                for m in range(KT):
                    dve.tensor_tensor(halves(y[:, m, :]), halves(y[:, m, :]), pair_bank(4), ALU.subtract).then_inc(d_ready, 1)
                dve.wait_ge(rs_ready, inst + 1)
                newton(rs[:, :], hf[:, :], pair_bank(6), LN_EPS, ln_newton, inst * 3)
                dve.wait_ge(ln_newton, inst * 3 + 3)
                for m in range(KT + 1):
                    if m < KT:
                        dve.tensor_tensor(y[:, m, :], y[:, m, :], rs[:, :], ALU.mult).then_inc(t_ready, 1)
                    if m >= 1:
                        low_parts(m - 1, count + m)

            def shifted(l, m, k, dst):
                i = l * NSH + 2 * m + k
                z = zb[k]
                dve.wait_ge(tile_out[k], out_count(l, "z", m))
                dve.wait_ge(zs_ready, i + 2)
                dve.tensor_tensor(zd[:, :], z[:, 0:T], z[:, 1:T + 1], ALU.subtract).then_inc(zd_ready, 1)
                dve.tensor_copy(last_z[:, bass.ds(2 * m + k, 1), :].rearrange("p a s -> p (a s)"), z[:, TP:T + 1:TS]).then_inc(last_ready, 1)
                dve.wait_ge(zd_ready, i * 2 + 1)
                dve.tensor_tensor(zd[:, TP:TP + 1], flat(shift_in[:, bass.ds(l, 1), bass.ds(2 * m + k, 1)]), z[:, TP + 1:TP + 2],
                                  ALU.subtract).then_inc(zd_ready, 1)
                dve.wait_ge(zd_ready, i * 2 + 2)
                dve.scalar_tensor_tensor(dst, zd[:, :], col(l, 2 * m + (k + COL["mu"])), z[:, 1:T + 1], ALU.mult, ALU.add).then_inc(zs_ready, 1)

            def pooling(l):
                step = [l * 16]

                def link(ins):
                    ins.then_inc(pool_step, 1)
                    step[0] = step[0] + 1
                    dve.wait_ge(pool_step, step[0])

                for q in range(2):
                    e = ub[q]
                    dve.wait_ge(tile_out[q], out_count(l, "z", 10))
                    link(dve.tensor_tensor(swA[:, 1:UW], e[:, 1:UW], e[:, 0:UW - 1], ALU.add))
                    link(dve.tensor_tensor(swB[:, 3:UW], swA[:, 3:UW], swA[:, 1:UW - 2], ALU.add))
                    if q == 1:
                        link(dve.tensor_tensor(swA[:, 7:UW], swB[:, 7:UW], swB[:, 3:UW - 4], ALU.add))
                        link(dve.tensor_tensor(swB[:, 15:UW], swA[:, 15:UW], swA[:, 7:UW - 8], ALU.add))
                    link(dve.tensor_copy(swB[0:64, 15:UW], swA[0:64, 15:UW]))
                    w = cst[:, CCOL["winv"][0] + q:CCOL["winv"][0] + q + 1]
                    link(dve.scalar_tensor_tensor(pooled[q][:, 0:TP], swB[:, HIST:HIST + TP], w, e[:, HIST:HIST + TP], ALU.mult, ALU.subtract))
                    link(dve.scalar_tensor_tensor(pooled[q][:, TP:T], swB[:, UW - TS:UW], w, e[:, UW - TS:UW], ALU.mult, ALU.subtract))
                    r = CCOL["rcnt"][0] + q * HIST
                    link(dve.tensor_tensor(swA[:, 0:HIST], swB[:, HIST:2 * HIST], cst[:, r:r + HIST], ALU.mult))
                    link(dve.tensor_tensor(pooled[q][:, 0:HIST], swA[:, 0:HIST], e[:, HIST:2 * HIST], ALU.subtract))

            def prepare_1(l, p, k, first):
                n = l * NPAIR + p
                r_, k_ = row(zs, p), row(zs, p + 6)
                if k == 2:
                    dve.wait_ge(wa_mm, n * 2)
                    dve.tensor_copy(lora_st[:, :], lora_all[:, bass.ds(p * P, P)]).then_inc(staged, 1)
                    dve.wait_ge(bk_ready, n * 3)
                    dve.tensor_scalar(kkb[:, :], k_, col(l, p + COL["k_k"]), None, ALU.mult).then_inc(kk_ready, 1)
                if k == 6:
                    dve.wait_ge(sig_ready, n * 2 + 1)
                    dve.tensor_tensor_scan(Lb[:, :], const("reset"), tB[:, :], 0.0, ALU.mult, ALU.add).then_inc(scan_ready, 1)
                if k == 7:
                    dve.wait_ge(sig_ready, n * 2 + 2)
                    dve.wait_ge(decay_ready, n * 4 + 4)
                    dve.tensor_scalar(tB[:, :], aa[:, :], col(l, p + COL["k_a"]), col(l, p + COL["one_ka"]), ALU.mult, ALU.add).then_inc(kf_ready, 1)
                    dve.wait_ge(kf_ready, n * 2 + 1)
                    dve.tensor_tensor(tB[:, :], k_, tB[:, :], ALU.mult).then_inc(kf_ready, 1)
                if k == 8:
                    dve.wait_ge(kkn_mm, n + 1)
                    dve.tensor_scalar(halves(nv[:, :]), pair_bank(3), 1e-24, None, ALU.max).then_inc(kkn_max, 1)
                if k == 9:
                    dve.wait_ge(rn_ready, n + 1)
                    newton(rn[:, :], nt[:, :], halves(nv[:, :]), 0.0, kk_newton, n * 3)
                if k == 10:
                    dve.wait_ge(kk_newton, n * 3 + 3)
                    dve.tensor_tensor(kkb[:, :], rn[:, :], kkb[:, :], ALU.mult).then_inc(kkb_ready, 1)
                if k == 11:
                    dve.wait_ge(kkb_ready, n + 1)
                    dve.wait_ge(kf_ready, n * 2 + 2)
                    dve.scalar_tensor_tensor(tA[:, :], r_, col(l, p + COL["r_k"]), tB[:, :], ALU.mult, ALU.mult).then_inc(rkk_ready, 1)

            def prepare_2(l, p, k, first):
                n = l * NPAIR + p
                r_, k_, v_ = row(zs, p), row(zs, p + 6), row(zs, p + 12)
                if k == 7:
                    dve.tensor_tensor(ar[:, 1, :], r_, Pb[:, 1:T + 1], ALU.mult).then_inc(ar_ready, 1)
                    dve.wait_ge(rk_mm, n + 1)
                    dve.tensor_tensor(halves(k_), pair_bank(3), halves(v_), ALU.mult).then_inc(bonus_ready, 1)
                if k == 9:
                    dve.scalar_tensor_tensor(ar[:, 0, :], kkb[:, :], -1.0, Pb[:, 0:T], ALU.mult, ALU.mult).then_inc(ar_ready, 1)
                    dve.wait_ge(ar_ready, n * 3 + 2)
                    dve.tensor_scalar(ar[:, 0, 0:T:CH], kkb[:, 0:T:CH], -1.0, None, ALU.mult).then_inc(ar_ready, 1)

            def normalise(l, p, k, last):
                n = l * NPAIR + p
                if k == 6:
                    dve.wait_ge(pg_mm, n)
                    dve.tensor_copy(g2_st[:, :], g2_all[:, bass.ds(p * P, P)]).then_inc(g_staged, 1)
                if k == 8:
                    dve.wait_ge(pm_mm, n + 1)
                    dve.tensor_tensor(halves(pd[:, :]), halves(row(zs, p)), pair_bank(3), ALU.subtract).then_inc(pd_ready, 1)
                if k == 11:
                    dve.wait_ge(prs_ready, n + 1)
                    newton(prs[:, :], psq[:, :], pair_bank(3), LNX_EPS, hn_newton, n * 3)
                if k == 13:
                    dve.wait_ge(pi_ready, n + 1)
                    dve.tensor_tensor(psq[:, :], psq[:, :], row(zs, p + 6), ALU.add).then_inc(pb_ready, 1)
                    dve.wait_ge(pb_ready, n + 1)
                    dve.wait_ge(pg_mm, n + 1)
                    dve.tensor_tensor(halves(row(zs, p)), halves(psq[:, :]), pair_bank(3), ALU.mult).then_inc(po_ready, 1)

            def products(u, n):
                j, h = u // 2, u % 2
                rows, b = (P if j < 4 else TS), 3 + u % 2
                dve.wait_ge(y_mm, n * 5 + j + 1)
                dve.wait_ge(am_mm, n * 10 + u + 1)
                dve.tensor_tensor(a4t[0][:, u, :] if j < 4 else a4t[1][:, h, :], ps[0:rows, b, 0:rows], const("m4t", rows, rows), ALU.mult).then_inc(am_part, 1)
                mask = const("am", rows).rearrange("p (a t) -> p a t", a=3)[:, :, 0:rows]
                dve.tensor_tensor(am[:, u, :, :] if j < 4 else ams[:, h, :, :], ps[0:rows, b, rows:4 * rows].rearrange("p (a t) -> p a t", a=3),
                                  mask, ALU.mult).then_inc(am_ready, 1)

            def step(s, g, n):
                name = STEPS[s]
                if name not in ("A", "H1", "H2", "X1", "X2", "X3", "Y1", "Y2", "Y3"):
                    return
                rows = P if g < 2 else TS
                dve.wait_ge(t_mm[g], n * NSTEP + s + 1)
                src = group_view(g, P if name[0] == "Y" else rows)
                if name == "A":
                    dve.tensor_tensor(a_units(xm, g), a_view(g), a_spread("m4", g), ALU.mult).then_inc(t_part[g], 1)
                    dve.wait_ge(t_part[g], n * (2, 2, 1)[g] + 1)
                    dve.tensor_tensor(units(xm, g), units(xm, g), spread("ident", g), ALU.add).then_inc(t_out[g], 1)
                    dve.tensor_tensor(a_units(n16, g), a_view(g), a_spread("m16", g), ALU.mult).then_inc(n_ready[g], 1)
                    dve.tensor_tensor(a_units(n64, g), a_view(g), a_spread("m64", g), ALU.mult).then_inc(n_ready[g], 1)
                elif name[0] == "H":
                    dve.tensor_tensor(units(xm if name == "H1" else t4, g), src, spread("ident", g), ALU.add).then_inc(t_out[g], 1)
                elif name == "Y3":
                    for q in range(2 if g < 2 else 1):
                        j = 2 * g + q
                        o = xm[0][:, 2 * j:2 * j + 2, :] if g < 2 else ys[:, :, :]
                        i1 = t4[0][:, 2 * j:2 * j + 2, :] if g < 2 else y0s[:, :, :]
                        dve.tensor_tensor(o.rearrange("p a (h c) -> p h a c", h=2), src[:, 2 * q:2 * q + 2, :].rearrange("p h (a c) -> p h a c", a=2),
                                          i1.rearrange("p h (a c) -> p h a c", a=2), ALU.add).then_inc((t_part if g < 2 and q == 0 else t_out)[g], 1)
                elif name[0] == "Y" and g == 2:
                    dve.tensor_tensor(ys[:, :, :], src, y0s[:, :, :], ALU.add).then_inc(t_out[g], 1)
                else:
                    dve.tensor_tensor(units(xm, g), src, units(t4, g), ALU.add).then_inc(t_out[g], 1)

            def chunk_in(c, n):
                j, ro, rows = (c // 2, 64 * (c % 2), CH) if c < NCH else (4, 0, TS)
                g_part = xm[0][ro:ro + rows, 2 * j + 1, :] if j < 4 else ys[:, 1, :]
                out = um[ro:ro + rows, j, :]
                if c == 0:
                    dve.wait_ge(t_out[0], n * NSTEP + NSTEP - 1)
                    dve.tensor_copy(out, g_part).then_inc(um_ready, 1)
                else:
                    dve.wait_ge(u_mm, n * 8 + c)
                    dve.tensor_tensor(out, ps[ro:ro + rows, 5, 0:P], g_part, ALU.add).then_inc(um_ready, 1)

            def chunk_out(c, l, p):
                n = l * NPAIR + p
                decay = dec[:, bass.ds(p * (NCH + 1) + c, 1)]
                dve.wait_ge(s_mm, n * 9 + c + 1)
                if c == 0:
                    dve.scalar_tensor_tensor(S[1][:, :], ps[:, 6, 0:P], decay, const("head_sum"), ALU.mult, ALU.mult).then_inc(s_ready, 1)
                    return
                dve.scalar_tensor_tensor(dS[:, :], ps[:, 6, 0:P], decay, const("head_sum"), ALU.mult, ALU.mult).then_inc(ds_ready, 1)
                dve.wait_ge(ds_ready, n * 8 + c)
                if c == NCH:
                    dve.scalar_tensor_tensor(Ss[1][:, :], Ss[0][:, :], decay, dS[:, :], ALU.mult, ALU.add).then_inc(ss_done, 1)
                    return
                if c == 1:
                    dve.wait_ge(wkv_stored, n * 64)
                dve.wait_ge(s_ready, n * 8 + c)
                dve.scalar_tensor_tensor(S[(c + 1) % 2][:, :], S[c % 2][:, :], decay, dS[:, :], ALU.mult, ALU.add).then_inc(s_ready, 1)

            def sample_state(l, p):
                n = l * NPAIR + p
                dve.wait_ge(y_mm, n * 5 + 5)
                dve.wait_ge(ss_done, n)
                for h in range(2):
                    hs = slice(64 * h, 64 * h + 64)
                    dve.tensor_copy(Ss[0][hs, hs], wkv_in[hs, bass.ds(l, 1), bass.ds(p, 1), :].rearrange("p a b v -> p (a b v)")).then_inc(
                        (ss_part, ss_init)[h], 1)

            def half_a(l, p, left, right, nxt):
                n = l * NPAIR + p
                for k in range(SLOTS_A):
                    if right and k < 8:
                        step(8 + k, 1, n - 1)
                        step(8 + k, 2, n - 1)
                    if right and k == 7:
                        sample_state(l, p - 1)
                    if right and k >= 8:
                        chunk_in(k - 4, n - 1)
                    if left and 2 <= k < 4:
                        products(2 * k - 4, n)
                        products(2 * k - 3, n)
                    if left and 4 <= k < 12:
                        step(k - 4, 0, n)
                    if right and k >= 8:
                        chunk_out(k - 4, l, p - 1)
                    if nxt:
                        prepare_1(l, p + 1, k, False)

            def half_b(l, p, nxt, norm_before):
                n = l * NPAIR + p
                for k in range(SLOTS_B):
                    if k < 8:
                        step(8 + k, 0, n)
                    elif k < 12:
                        chunk_in(k - 8, n)
                    if 2 <= k < 5:
                        products(2 * k, n)
                        products(2 * k + 1, n)
                    if 5 <= k < 13:
                        step(k - 5, 1, n)
                    if 6 <= k:
                        step(k - 6, 2, n)
                    if 8 <= k < 12:
                        chunk_out(k - 8, l, p)
                    if nxt:
                        prepare_2(l, p + 1, k, False)
                    if norm_before:
                        normalise(l, p - 1, k, False)

            with dve.Fori(0, DEPTH) as l:
                ffn(l, 0, "f1i")
                residual(l, l * 3, "f1o", 0.5, None)
                norm(l * 3, l * 40 + 8)
                dve.wait_ge(shift_stored, l * 16)
                for k in range(2):
                    dve.memset(zb[k][:, 0:1], 0.0)
                    dve.memset(ub[k][:, 0:HIST], 0.0)
                    dve.tensor_copy(ub[k][:, HIST + TP:HIST + TP + HIST], flat(pool_hs[:, bass.ds(l, 1), k, :]))
                    for h in range(2):
                        hs = slice(64 * h, 64 * h + 64)
                        ins = dve.tensor_copy(pool_bd[hs, k, hs], flat(pool_w[hs, bass.ds(l, 1), k, :]))
                ins.then_inc(z_set, 1)
                with dve.Fori(0, 9) as m:
                    for k in range(2):
                        shifted(l, m, k, row(zs, 2 * m + k))
                shifted(l, 9, 0, lora[:, :])
                shifted(l, 9, 1, lgate[:, :])
                pooling(l)
                for q in range(2):
                    dve.wait_ge(xh_ready, l * 40 + 17 + q)
                    dve.tensor_tensor(xl[:, q, :], mf[q][:, :], xh[:, q, :].bitcast(F32), ALU.subtract).then_inc(xl_ready, 1)
                dve.wait_ge(pool_stored, l * 64 + 64)
                dve.wait_ge(lora_act, l * 2 + 2)
                dve.wait_ge(layer_loaded, l * 32 + 32)
                dve.memset(Pb[:, 0:1], 1.0)
                dve.memset(Ss[0][:, :], 0.0).then_inc(set_done, 1)
                dve.wait_ge(set_done, l + 4)
                heads(dve, l, half_a, half_b, prepare_1, prepare_2, normalise)
                with dve.Fori(0, NPAIR) as p:
                    dve.wait_ge(xh_ready, l * 40 + p + 19)
                    dve.tensor_tensor(row(xl, p + 2), row(zs, p), row(xh, p + 2).bitcast(F32), ALU.subtract).then_inc(xl_ready, 1)
                residual(l, l * 3 + 1, "wo", 1.0, None)
                norm(l * 3 + 1, l * 40 + 24)
                due = dve.to_reg((l + 1) * (NPAIR * 64))
                dve.wait_ge(loaded, 16 * NLOAD)
                dve.wait_ge(wkv_stored, due)
                ffn(l, 1, "f2i")
                residual(l, l * 3 + 2, "f2o", 0.5, l * 40 + 32)
                for k in range(2):
                    dve.wait_ge(ph_ready, l * 2 + k + 1)
                    dve.tensor_tensor(hl[:, k, :], sq[k][:, :], hh[:, k, :].bitcast(F32), ALU.subtract).then_inc(pl_ready, 1)
                dve.memset(ysum[:, :], 0.0).then_inc(sum_ready, 1)
                with dve.Fori(0, KT) as m:
                    dve.wait_ge(slot_used, used_count(l, "gp", 2 * m + 1))
                    dve.wait_ge(tile_out[0], out_count(l, "gp", m))
                    dve.tensor_tensor(halves(hf[:, :]), halves(sg[:, :]), pair_bank(2), ALU.mult).then_inc(tile_out[1], 1)
                    dve.wait_ge(tile_out[1], out_count(l, "gp", m))
                    dve.tensor_tensor(row(y, m), row(y, m), hf[:, :], ALU.add).then_inc(y_ready, 1)
                    dve.wait_ge(y_ready, l * 8 + m + 1)
                    dve.wait_ge(sum_ready, l * 27 + 18 + m + 1)
                    dve.tensor_tensor(ysum[:, :], ysum[:, :], row(y, m), ALU.add).then_inc(sum_ready, 1)
                norm(l * 3 + 2, l * 40 + 40)
            dve.wait_ge(xl_ready, DEPTH * 40 + 8)
            dve.wait_ge(ax_ready, DEPTH * 24 + 8)
            for m in range(KT):
                dve.tensor_tensor(y[:, m, :], xh[:, m, :].bitcast(F32), xl[:, m, :].bitcast(F32), ALU.add).then_inc(fin_ready, 1)


def constants():
    i = np.arange(P)
    t, s = i[:, None], i[None, :]
    same = lambda n: (t // n) == (s // n)
    low = s < t
    c = {
        "ident": t == s, "mean_d": np.full((P, P), 1.0 / D), "head_sum": same(64), "head_mean": same(64) / 64.0,
        "m4": low & same(4), "m16": low & same(16) & ~same(4), "m64": low & same(64) & ~same(16), "m4t": (t < s) & same(4),
        "am": np.concatenate([(t <= s) & same(64), (t < s) & same(64), (t <= s) & same(64)], axis=1),
        "reset": np.tile((np.arange(T) % CH != 0), (P, 1)),
    }
    wins = np.array([[2, 8], [4, 16]])[i // 64]
    c["winv"] = 1.0 / wins
    c["rcnt"] = np.concatenate([1.0 / np.minimum(np.arange(HIST)[None, :] + 1, wins[:, q:q + 1]) for q in range(2)], axis=1)
    return np.ascontiguousarray(np.concatenate([np.asarray(c[n], np.float32) for n, _ in CONSTS], axis=1))


def kernel(**inputs):
    import concourse.bacc as bacc
    from concourse.bass_utils import run_bass_kernel_spmd

    a = {k: np.asarray(v) for k, v in inputs.items()}
    L = DEPTH

    def channels(x, n):
        x = x.reshape(x.shape[:-1] + (n, P))
        return np.moveaxis(x, -1, 0)

    def tokens(x):
        return x.T.reshape(-1, P, x.shape[0]).transpose(1, 0, 2)

    def slots(w):
        n, k, m = w.shape
        return w.reshape(n, k // P, P, m // P, P).transpose(0, 3, 2, 1, 4)

    def ffn_in(w):
        s = slots(w)
        return np.stack([s[:, :FT], s[:, FT:]], axis=2).reshape((L * 2 * FT,) + s.shape[2:])

    def flat_slots(s):
        return s.reshape((-1,) + s.shape[2:])

    z = slots(a["w_in"])
    cols = []
    for n, w in COLS:
        src = {"gate_b": "ple_gate_b", "mu": "mu_shift", "one_ka": "k_a"}.get(n, n)
        cols.append(channels(a[src].reshape(L, -1), w))
    lora = np.concatenate([a["w2"], a["a2"]], axis=1)
    pw = a["pool_w"].reshape(L, 2, 2, 64, 64)
    st = a["state_wkv"][:, 0].reshape(L, NPAIR, 2, 64, 64)
    arrays = {
        "xT": tokens(np.concatenate([a["x_prompt"][0], a["x_sample"][0]], axis=0)),
        "pT": np.stack([tokens(np.concatenate([a["p_prompt"][i, 0], a["p_sample"][i, 0]], axis=0)) for i in range(L)]),
        "w1i": ffn_in(a["ffn1_w_in"]), "w1o": flat_slots(slots(a["ffn1_w_out"])),
        "wz": flat_slots(np.concatenate([z[:, 2:], z[:, :2]], axis=1)), "wo": flat_slots(slots(a["w_out"])),
        "w2i": ffn_in(a["ffn2_w_in"]), "w2o": flat_slots(slots(a["ffn2_w_out"])),
        "wg": flat_slots(slots(a["ple_gate_w"])), "wp": flat_slots(slots(a["ple_w"])),
        "params": np.concatenate(cols, axis=2).reshape(P, L * NPAR),
        "consts": constants(),
        "poolw": pw.transpose(2, 3, 0, 1, 4).reshape(P, L, 2, 64),
        "lora_w": lora, "g2_w": a["g2"],
        "pool_hist": channels(a["state_pool"][:, 0].transpose(0, 1, 2), 2).transpose(0, 1, 3, 2),
        "shift_hist": channels(a["state_shift"][:, 0], NSH),
        "wkv_hist": st.transpose(2, 4, 0, 1, 3).reshape(P, L, NPAIR, 64),
    }
    arrays = {k: np.ascontiguousarray(v) for k, v in arrays.items()}
    outs = {"y_out": (P, KT, T), "pool_out": (L, 2, P, 2, HIST), "shift_out": (L, P, NSH, 2), "wkv_out": (L * NPAIR, 2, P, 64)}
    nc = bacc.Bacc("TRN2", target_bir_lowering=False, num_devices=1)
    args = [nc.dram_tensor("in_" + k, v.shape, F32, kind="ExternalInput").ap() for k, v in arrays.items()]
    args += [nc.dram_tensor(k, s, F32, kind="ExternalOutput").ap() for k, s in outs.items()]
    build(nc, *args)
    r = run_bass_kernel_spmd(nc, [{"in_" + k: v for k, v in arrays.items()}], core_ids=[0]).results[0]
    yo = np.asarray(r["y_out"]).transpose(2, 1, 0).reshape(T, D)
    po = np.asarray(r["pool_out"]).transpose(1, 0, 4, 3, 2).reshape(2, L, 1, HIST, 2 * P)
    so = np.asarray(r["shift_out"]).transpose(3, 0, 2, 1).reshape(2, L, 1, NSH * P)
    wo = np.asarray(r["wkv_out"]).reshape(L, NPAIR, 2, 2, 64, 64).transpose(2, 0, 1, 3, 5, 4).reshape(2, L, 1, 2 * NPAIR, 64, 64)
    c = np.ascontiguousarray
    return (c(yo[None, :TP]), c(yo[None, TP:]), c(po[0]), c(so[0]), c(wo[0]), c(po[1]), c(so[1]), c(wo[1]))
```

```python
from contextlib import ExitStack

import numpy as np

import concourse.bass as bass
from concourse import mybir

F32 = mybir.dt.float32
F32R = mybir.dt.float32r
ACT = mybir.ActivationFunctionType
ALU = mybir.AluOpType

P = 128
DEPTH = 2
D = 1024
KT = D // P
TP, TS = 512, 32
T = TP + TS
HT = T // 2
FF = 2816
FT = FF // P
DR = 768
NPAIR = DR // P
NSH = 20
NZ = 22
HIST = 15
CH = 64
NCH = TP // CH
ALPHA = (2.0 * DEPTH) ** 0.25
LN_EPS, LNX_EPS = 1e-5, 64e-5
DECAY = float(np.exp(-0.5))

COLS = [("ln1_g", 8), ("ln1_b", 8), ("ln2_g", 8), ("ln2_b", 8), ("ln3_g", 8), ("ln3_b", 8), ("gate_b", 8),
        ("mu", NSH), ("w0", 6), ("a0", 6), ("k_k", 6), ("k_a", 6), ("r_k", 6), ("lnx_g", 6), ("lnx_b", 6),
        ("pool_scale", 2), ("one_ka", 6), ("ab1", 8), ("ab2", 8), ("ab3", 8)]
COL = {}
NPAR = 0
for _n, _w in COLS:
    COL[_n] = NPAR
    NPAR += _w

PHASES = [("f1i", FT, [8, 8]), ("f1o", 4, [8, 7, 7, 8, 7, 7]), ("z", NZ // 2, [8, 8]), ("wo", 4, [8, 8]),
          ("f2i", FT, [8, 8]), ("f2o", 4, [8, 7, 7, 8, 7, 7]), ("gp", 8, [8, 2])]
SLOT0, SLOTS = {}, 0
for _n, _b, _k in PHASES:
    SLOT0[_n] = SLOTS
    SLOTS += _b * len(_k)
TILE0, TILES = {}, 0
for _n, _c in [("f1i", 2 * FT), ("f1o", 8), ("z", NZ), ("wo", 8), ("f2i", 2 * FT), ("f2o", 8), ("gp", 16)]:
    TILE0[_n] = TILES
    TILES += _c

CONSTS = [("ident", P), ("mean_d", P), ("head_sum", P), ("head_mean", P), ("m4", P), ("m16", P), ("m64", P),
          ("m4t", P), ("am", 3 * P), ("reset", T), ("winv", 2), ("rcnt", 2 * HIST)]
CCOL, NCONST = {}, 0
for _n, _w in CONSTS:
    CCOL[_n] = (NCONST, _w)
    NCONST += _w

STEPS = ["A", "H1", "H2", "T4T", "E16", "X1", "X2", "X3", "T16T", "G", "Y0", "E64", "Y1", "Y2", "Y3", "WT"]
NSTEP = len(STEPS)
GROUPS = [(0, 1), (2, 3), (4,)]


def build(nc, xT, pT, w1i, w1o, wz, wo, w2i, w2o, wg, wp, params, consts, poolw, lora_w, g2_w,
          pool_hist, shift_hist, wkv_hist, y_out, pool_out, shift_out, wkv_out):
    ctx = ExitStack()
    with ctx:
        base = (nc.sbuf_base + 31) // 32 * 32
        top = [base]

        def at(name, shape, dt, addr):
            size = int(np.prod(shape[1:])) * 4
            return nc.alloc_sbuf_tensor_at(name, shape, dt, offset=addr), (addr + size + 31) // 32 * 32

        def sb(name, shape, dt=F32):
            t, top[0] = at(name, shape, dt, top[0])
            return t

        y = sb("y", [P, KT, T])
        xh_addr = top[0]
        xh = sb("xh", [P, KT, T], F32R)
        xl_addr = top[0]
        xl = sb("xl", [P, KT, T], F32R)
        w_raw = [sb(f"w_raw{i}", [P, 8, P]) for i in range(2)]
        w_hi = [sb(f"w_hi{i}", [P, 8, P], F32R) for i in range(2)]
        w_lo = [sb(f"w_lo{i}", [P, 8, P], F32R) for i in range(2)]
        cst = sb("cst", [P, NCONST])
        par = sb("par", [P, DEPTH * NPAR])
        shift_in = sb("shift_in", [P, DEPTH, NSH])
        wkv_in = sb("wkv_in", [P, DEPTH, NPAIR, 64])
        pool_w = sb("pool_w", [P, DEPTH, 2, 64])
        pool_hs = sb("pool_hs", [P, DEPTH, 2, HIST])
        pool_bd = sb("pool_bd", [P, 2, P])
        last_z = sb("last_z", [P, NSH, 2])
        eps = sb("eps", [P, 2])
        lora_all = sb("lora_all", [P, DR])
        g2_all = sb("g2_all", [P, DR])
        lora_st = sb("lora_st", [P, P])
        g2_st = sb("g2_st", [P, P])
        h_addr = top[0]
        hh = sb("hh", [P, FT, T], F32R)
        hl = sb("hl", [P, FT, T], F32R)
        sg = sb("sg", [P, T])
        hf = sb("hf", [P, T])
        sq = [sb(f"sq{i}", [P, T]) for i in range(2)]
        rs = sb("rs", [P, T])
        ysum = sb("ysum", [P, T])
        assert top[0] <= nc.sbuf_usable_end
        top[0] = h_addr
        zs = sb("zs", [P, 18, T])
        lora = sb("lora", [P, T])
        lgate = sb("lgate", [P, T])
        mix_addr = top[0]
        ar = sb("ar", [P, 2, T])
        bt = sb("bt", [P, T])
        kt = sb("kt", [P, T])
        vc = sb("vc", [P, T])
        Lb = sb("Lb", [P, T])
        Pb = sb("Pb", [P, T + 8])
        Pi = sb("Pi", [P, T])
        aa = sb("aa", [P, T])
        kkb = sb("kkb", [P, T])
        tA = sb("tA", [P, T])
        tB = sb("tB", [P, T])
        tm = sb("tm", [P, 5, 3, P])
        rhs = sb("rhs", [P, 5, 2, 2, 64])
        um = sb("um", [P, 5, P])
        wt = sb("wt", [P, T])
        S = [sb(f"S{i}", [P, P]) for i in range(2)]
        Ss = [sb(f"Ss{i}", [P, P]) for i in range(2)]
        dS = sb("dS", [P, P])
        nv, rn = Lb, tA

        def mats(name):
            return sb(name, [P, 8, P]), sb(name + "s", [TS, 2, TS])

        n16, n64, a4t, xm = mats("n16"), mats("n64"), mats("a4t"), mats("xm")
        em = a4t
        dec = sb("dec", [P, NPAIR * (NCH + 1)])
        nt = sb("nt", [P, T])
        pd = sb("pd", [P, T])
        psq = sb("psq", [P, T])
        assert top[0] <= nc.sbuf_usable_end
        a = xl_addr + 2 * T * 4
        am, a = at("am", [P, 8, 3, P], F32, a)
        ams, a = at("ams", [TS, 2, 3, TS], F32, a)
        assert a <= xl_addr + KT * T * 4
        a = xh_addr + 2 * T * 4
        t4, a = at("t4", [P, 8, P], F32, a)
        t4s, a = at("t4s", [TS, 2, TS], F32, a)
        tt, a = at("tt", [P, 8, P], F32, a)
        tts, a = at("tts", [TS, 2, TS], F32, a)
        ys, a = at("ys", [TS, 2, P], F32, a)
        y0s, a = at("y0s", [TS, 2, P], F32, a)
        prs, a = at("prs", [P, T], F32, a)
        assert a <= xh_addr + KT * T * 4
        t4, tt = (t4, t4s), (tt, tts)
        top[0] = mix_addr
        zb = [sb(f"zb{i}", [P, T + 8]) for i in range(2)]
        zd = sb("zd", [P, T])
        UW = HIST + TP + HIST + TS
        ub = [sb(f"ub{i}", [P, UW + 2]) for i in range(2)]
        swA = sb("swA", [P, UW + 2])
        swB = sb("swB", [P, UW + 2])
        pooled = [sb(f"pooled{i}", [P, T]) for i in range(2)]
        mf = [sb(f"mf{i}", [P, T]) for i in range(2)]

        ps = ctx.enter_context(nc.psum_tensor("ps", [P, 8, 512], F32))

        def pair_bank(i):
            return ps[:, i:i + 2, 0:HT]

        def halves(ap):
            return ap.rearrange("p (a b) -> p a b", a=2)

        def const(name, rows=P, cols=None):
            o, w = CCOL[name]
            return cst[0:rows, o:o + (cols or w)]

        def sem(name):
            return ctx.enter_context(nc.semaphore(name))

        loaded, layer_loaded, p_loaded = (sem(n) for n in ("loaded", "layer_loaded", "p_loaded"))
        x_loaded = [sem(f"x_loaded{m}") for m in range(KT)]
        pool_stored, shift_stored, wkv_stored, y_stored = (sem(n) for n in ("pool_stored", "shift_stored", "wkv_stored", "y_stored"))
        w_loaded = [sem(f"w_loaded{i}") for i in range(2)]
        w_hi_done, w_split, slot_used = sem("w_hi_done"), sem("w_split"), sem("slot_used")
        tile_out = [sem(f"tile_out{i}") for i in range(2)]
        xh_ready, xl_ready, hh_ready, hl_ready = sem("xh_ready"), sem("xl_ready"), sem("hh_ready"), sem("hl_ready")
        ph_ready, pl_ready = sem("ph_ready"), sem("pl_ready")
        set_done, y_ready, sum_ready, mean_mm, d_ready = (sem(n) for n in ("set_done", "y_ready", "sum_ready", "mean_mm", "d_ready"))
        sq_ready, var_mm, rs_ready, t_ready, xf_ready, ax_ready = (
            sem(n) for n in ("sq_ready", "var_mm", "rs_ready", "t_ready", "xf_ready", "ax_ready"))
        z_set, zd_ready, last_ready, zs_ready, lora_act, u_part = (
            sem(n) for n in ("z_set", "zd_ready", "last_ready", "zs_ready", "lora_act", "u_part"))
        pool_step, pool_mm, mf_ready = sem("pool_step"), sem("pool_mm"), sem("mf_ready")
        staged, wa_mm, sig_ready, scan_ready, decay_ready, kf_ready = (
            sem(n) for n in ("staged", "wa_mm", "sig_ready", "scan_ready", "decay_ready", "kf_ready"))
        kk_ready, kksq_ready, kkn_mm, kkn_max, rn_ready, kkb_ready, kp_ready = (
            sem(n) for n in ("kk_ready", "kksq_ready", "kkn_mm", "kkn_max", "rn_ready", "kkb_ready", "kp_ready"))
        ar_ready, bk_ready, vc_ready, rp_ready, rkk_ready, rk_mm, bonus_ready = (
            sem(n) for n in ("ar_ready", "bk_ready", "vc_ready", "rp_ready", "rkk_ready", "rk_mm", "bonus_ready"))
        tm_mm, tm_part, tm_ready, am_mm, am_part, am_ready = (
            sem(n) for n in ("tm_mm", "tm_part", "tm_ready", "am_mm", "am_part", "am_ready"))
        t_mm = [sem(f"t_mm{g}") for g in range(3)]
        t_part = [sem(f"t_part{g}") for g in range(3)]
        t_out = [sem(f"t_out{g}") for g in range(3)]
        n_ready = [sem(f"n_ready{g}") for g in range(3)]
        u_mm, um_ready, s_mm, ds_ready, s_ready, y_mm, yw_ready = (
            sem(n) for n in ("u_mm", "um_ready", "s_mm", "ds_ready", "s_ready", "y_mm", "yw_ready"))
        ss_part, ss_init, ss_done = sem("ss_part"), sem("ss_init"), sem("ss_done")
        g_staged, pm_mm, pg_mm, pd_ready, psq_ready, pv_mm, prs_ready = (
            sem(n) for n in ("g_staged", "pm_mm", "pg_mm", "pd_ready", "psq_ready", "pv_mm", "prs_ready"))
        pt_ready, pi_ready, pb_ready, g_ready, po_ready, fin_ready = (
            sem(n) for n in ("pt_ready", "pi_ready", "pb_ready", "g_ready", "po_ready", "fin_ready"))
        ln_newton, kk_newton, hn_newton = sem("ln_newton"), sem("kk_newton"), sem("hn_newton")
        NLOAD = 6

        def flat(ap):
            return ap.rearrange("p a t -> p (a t)")

        def row(t, i):
            return flat(t[:, bass.ds(i, 1), :])

        def col(l, c):
            return par[:, bass.ds(l * NPAR + c, 1)]

        def out_count(l, name, m):
            return l * (TILES // 2) + TILE0[name] // 2 + m + 1

        def used_count(l, name, i):
            return l * SLOTS + SLOT0[name] + i + 3

        def group_view(g, wide):
            n, U = (P, 4) if g < 2 else (TS, 2)
            return ps[0:n, g, 0:U * P].rearrange("p (u c) -> p u c", u=U)[:, :, 0:wide]

        def a_view(g):
            n, tiles = (P, 2) if g < 2 else (TS, 1)
            return ps[0:n, 3:5, 0:tiles * P].rearrange("p h (j c) -> p h j c", j=tiles)[:, :, :, 0:n]

        def a_units(m, g):
            return units(m, g).rearrange("p (j h) c -> p h j c", h=2)

        def a_spread(name, g):
            n, tiles = (P, 2) if g < 2 else (TS, 1)
            return const(name, n, n).unsqueeze(1).unsqueeze(1).to_broadcast([n, 2, tiles, n])

        def units(m, g):
            return m[0][:, 4 * g:4 * g + 4, :] if g < 2 else m[1][:, :, :]

        def spread(name, g):
            n, U = (P, 4) if g < 2 else (TS, 2)
            return const(name, n, n).unsqueeze(1).to_broadcast([n, U, n])

        block = ctx.enter_context(nc.Block())

        SLOTS_A, SLOTS_B = 13, 14

        def heads(eng, l, half_a, half_b, prepare_1, prepare_2, normalise):
            for k in range(SLOTS_A):
                prepare_1(l, 0, k, True)
            for k in range(SLOTS_B):
                prepare_2(l, 0, k, True)
            half_a(l, 0, True, False, True)
            half_b(l, 0, True, False)
            with eng.Fori(0, NPAIR - 2) as q:
                half_a(l, q + 1, True, True, True)
                half_b(l, q + 1, True, True)
            half_a(l, NPAIR - 1, True, True, False)
            half_b(l, NPAIR - 1, False, True)
            half_a(l, NPAIR, False, True, False)
            for k in range(SLOTS_B):
                normalise(l, NPAIR - 1, k, False)

        @block.sync
        def _(sp):
            for m in range(KT):
                sp.dma_start(y[:, m, :], xT[:, m, :]).then_inc(x_loaded[m], 16)
            arrays = {"f1i": w1i, "f1o": w1o, "z": wz, "wo": wo, "f2i": w2i, "f2o": w2o}
            with sp.Fori(0, DEPTH) as l:
                sp.wait_ge(xl_ready, l * 40)
                sp.dma_start(lora_all[:, :], flat(lora_w[bass.ds(l, 1)].rearrange("a p n -> p a n"))).then_inc(layer_loaded, 16)
                sp.dma_start(g2_all[:, :], flat(g2_w[bass.ds(l, 1)].rearrange("a p n -> p a n"))).then_inc(layer_loaded, 16)
                for name, bodies, ks in PHASES:
                    B = len(ks)
                    if name == "wo":
                        with sp.Fori(0, NPAIR - 1) as p:
                            n = l * NPAIR + p
                            due, due_sample = sp.to_reg(n * 8 + 8), sp.to_reg(n + 1)
                            sp.wait_ge(s_ready, due)
                            sp.wait_ge(ss_done, due_sample)
                            for q, st in enumerate((S[0], Ss[1])):
                                for h in range(2):
                                    hs = slice(64 * h, 64 * h + 64)
                                    sp.dma_start(wkv_out[bass.ds(n, 1), q, hs, :].rearrange("a p v -> p (a v)"), st[hs, hs]).then_inc(wkv_stored, 16)
                    if name == "f2o":
                        sp.wait_ge(var_mm, l * 24 + 16)
                        for k in range(2):
                            sp.dma_start(sq[k][:, :], flat(pT[bass.ds(l, 1), :, k, :].rearrange("a p t -> p a t"))).then_inc(p_loaded, 16)
                    with sp.Fori(0, bodies) as m:
                        for i, nk in enumerate(ks):
                            if name == "gp":
                                src = (wg, wp)[i][bass.ds(l * 8 + m, 1)]
                            elif name in ("f1o", "f2o"):
                                k0 = (0, 8, 15)[i % 3]
                                src = arrays[name][bass.ds(l * 8 + m * 2 + i // 3, 1), :, k0:k0 + nk, :]
                            else:
                                src = arrays[name][bass.ds(l * (bodies * B) + m * B + i, 1)]
                            sp.wait_ge(w_split, l * SLOTS + SLOT0[name] + m * B + i + 1)
                            sp.dma_start(w_raw[i % 2][:, 0:nk, :], src.rearrange("a p k n -> p (a k) n")).then_inc(w_loaded[i % 2], 16)
            for m in range(KT):
                sp.wait_ge(fin_ready, m + 1)
                sp.dma_start(y_out[:, m, :], y[:, m, :]).then_inc(y_stored, 16)
            sp.wait_ge(y_stored, 16 * KT)
            sp.wait_ge(pool_stored, DEPTH * 64)
            sp.wait_ge(shift_stored, DEPTH * 16)
            sp.wait_ge(wkv_stored, DEPTH * NPAIR * 64)

        @block.gpsimd
        def _(pool):
            pool.sem_inc(w_split, 2)

            def prepare_1(l, p, k, first):
                n = l * NPAIR + p
                if k == 3:
                    pool.wait_ge(kf_ready, n + 1)
                    pool.tensor_tensor(tB[:, :], row(zs, p + 6), tB[:, :], ALU.mult).then_inc(kp_ready, 1)
                if k == 5:
                    pool.wait_ge(rn_ready, n + 1)
                    pool.tensor_tensor(nt[:, :], nv[:, :], rn[:, :], ALU.mult).then_inc(kk_newton, 1)
                    pool.wait_ge(kk_newton, n * 4 + 1)
                    pool.tensor_tensor(nt[:, :], nt[:, :], rn[:, :], ALU.mult).then_inc(kk_newton, 1)
                    due = pool.to_reg(n * 4 + 2)
                    pool.wait_ge(w_split, 2)
                    pool.wait_ge(kk_newton, due)
                    pool.tensor_scalar(nt[:, :], nt[:, :], -0.5, 1.5, ALU.mult, ALU.add).then_inc(kk_newton, 1)
                    pool.wait_ge(kk_newton, n * 4 + 3)
                    pool.tensor_tensor(rn[:, :], nt[:, :], rn[:, :], ALU.mult).then_inc(kk_newton, 1)
                    pool.wait_ge(kk_newton, n * 4 + 4)
                    pool.tensor_tensor(kkb[:, :], rn[:, :], kkb[:, :], ALU.mult).then_inc(kkb_ready, 1)

            def prepare_2(l, p, k, first):
                n = l * NPAIR + p
                if k == 8:
                    pool.wait_ge(kp_ready, n + 1)
                    pool.wait_ge(ar_ready, n * 3 + 1)
                    pool.tensor_tensor(kt[:, :], tB[:, :], Pi[:, :], ALU.mult).then_inc(bk_ready, 1)
                    pool.wait_ge(kkb_ready, n + 1)
                    pool.tensor_tensor(bt[:, :], kkb[:, :], aa[:, :], ALU.mult).then_inc(bk_ready, 1)
                    pool.wait_ge(bk_ready, n * 3 + 2)
                    pool.tensor_tensor(bt[:, :], bt[:, :], Pi[:, :], ALU.mult).then_inc(bk_ready, 1)

            def normalise(l, p, k, after_bonus):
                if k == 4:
                    pool.wait_ge(hn_newton, (l * NPAIR + p) * 3 + 3)
                    pool.tensor_tensor(pd[:, :], pd[:, :], prs[:, :], ALU.mult).then_inc(pt_ready, 1)
                if k == 6:
                    pool.wait_ge(pi_ready, l * NPAIR + p + 1)
                    pool.tensor_tensor(psq[:, :], psq[:, :], row(zs, p + 6), ALU.add).then_inc(pb_ready, 1)
                    pool.wait_ge(pb_ready, l * NPAIR + p + 1)
                    pool.wait_ge(g_ready, l * NPAIR + p + 1)
                    pool.tensor_tensor(row(zs, p), psq[:, :], nt[:, :], ALU.mult).then_inc(po_ready, 1)

            def half_a(l, p, left, right, nxt):
                for k in range(SLOTS_A):
                    if nxt:
                        prepare_1(l, p + 1, k, False)

            def half_b(l, p, nxt, norm_before):
                for k in range(SLOTS_B):
                    if norm_before:
                        normalise(l, p - 1, k, nxt)
                    if nxt:
                        prepare_2(l, p + 1, k, False)

            with pool.Fori(0, DEPTH) as l:
                for name, bodies, ks in PHASES:
                    B = len(ks)
                    if name == "wo":
                        heads(pool, l, half_a, half_b, prepare_1, prepare_2, normalise)
                    with pool.Fori(0, bodies) as m:
                        for i, nk in enumerate(ks):
                            n, k = l * SLOTS + SLOT0[name] + m * B + i, i % 2
                            pool.wait_ge(w_loaded[k], (l * (SLOTS // 2) + m * (B // 2) + (SLOT0[name] // 2 + i // 2 + 1)) * 16)
                            due = pool.to_reg(n + 1)
                            pool.wait_ge(w_split, 2)
                            pool.wait_ge(slot_used, due)
                            pool.tensor_scalar(w_hi[k][:, 0:nk, :], w_raw[k][:, 0:nk, :], 1.0, 0.0, ALU.mult, ALU.add).then_inc(w_hi_done, 1)
                            pool.wait_ge(w_hi_done, n + 1)
                            pool.tensor_tensor(w_lo[k][:, 0:nk, :], w_raw[k][:, 0:nk, :], w_hi[k][:, 0:nk, :].bitcast(F32),
                                               ALU.subtract).then_inc(w_split, 1)

        @block.tensor
        def _(pe):
            pe.sem_inc(slot_used, 2)
            pe.sem_inc(y_mm, 5)

            def constants_there():
                pe.wait_ge(loaded, 16 * NLOAD)

            def dense(l, name, hi, lo, ready, base):
                _, bodies, ks = next(p for p in PHASES if p[0] == name)
                B = len(ks)
                per = B // 2

                def body(m, first):
                    for i, nk in enumerate(ks):
                        k, pair, part = i % 2, i // per, i % per
                        n = l * SLOTS + SLOT0[name] + m * B + i
                        if part == 0:
                            pe.wait_ge(tile_out[pair], out_count(l, name, m) - 1)
                        if name == "gp" and i == 1 and first:
                            pe.wait_ge(pl_ready, l * 2 + 2)
                        pe.wait_ge(w_split, n + 3)
                        x_hi, x_lo = (hh, hl) if name == "gp" and i == 1 else (hi, lo)
                        k0 = (0, 8, 15)[part]
                        for j in range(nk):
                            if first and pair == 0:
                                pe.wait_ge(ready, base + k0 + j + 1)
                            for q, (w, x) in enumerate(((w_hi[k], x_hi), (w_hi[k], x_lo), (w_lo[k], x_hi))):
                                for h in range(2):
                                    mm = pe.matmul(ps[:, 2 * pair + h, 0:HT], w[:, j, :], x[:, k0 + j, h * HT:(h + 1) * HT],
                                                   start=(part == 0 and j == 0 and q == 0),
                                                   stop=(part == per - 1 and j == nk - 1 and q == 2))
                        mm.then_inc(slot_used, 1)

                body(0, True)
                with pe.Fori(1, bodies) as m:
                    body(m, False)

            def two(bank, lhsT, r, start=True, stop=True):
                for h in range(2):
                    mm = pe.matmul(ps[:, bank + h, 0:HT], lhsT, r[:, h * HT:(h + 1) * HT], start=start, stop=stop)
                return mm

            def norm(inst):
                constants_there()
                pe.wait_ge(sum_ready, inst * 9 + 9)
                two(4, const("mean_d"), ysum).then_inc(mean_mm, 1)
                for m in range(KT):
                    pe.wait_ge(sq_ready, inst * 8 + m + 1)
                    two(6, const("mean_d"), sq[m % 2], m == 0, m == KT - 1).then_inc(var_mm, 1)

            def step_waits(name, s, g, n):
                due, blocks = pe.to_reg(n * NSTEP + s), pe.to_reg(n * 2 + 2)
                if g == 2:
                    constants_there()
                if name == "A":
                    if g == 2:
                        pe.wait_ge(n_ready[1], blocks)
                    else:
                        pe.wait_ge(am_ready, n * 10 + (4, 10)[g])
                if name == "E16":
                    pe.wait_ge(n_ready[g], blocks)
                pe.wait_ge(t_out[g], due)

            def step(s, g, n, part=None):
                name, tiles, rows = STEPS[s], GROUPS[g], (P if g < 2 else TS)
                if part != 1:
                    step_waits(name, s, g, n)
                if name == "WT":
                    for q, j in enumerate(tiles):
                        src = xm[0][:, 2 * j, :] if g < 2 else ys[:, 0, :]
                        mm = pe.transpose(ps[:, g, q * P:q * P + rows], src, const("ident", rows, rows))
                    mm.then_inc(t_mm[g], 1)
                    return
                for q, (j, h) in enumerate((j, h) for j in tiles for h in range(2)):
                    if part is not None and q // 2 != part:
                        continue
                    u, hs, ts = 2 * j + h, slice(64 * h, 64 * h + 64), slice(j * P, j * P + rows)

                    def mat(m):
                        return m[0][:, u, :] if g < 2 else m[1][:, h, :]

                    b, o = (3 + h, q // 2 * P) if name == "A" else (g, q * P)
                    out = ps[0:rows, b, o:o + (P if name[0] == "Y" else 64 if name == "G" else rows)]
                    if name in ("T4T", "T16T"):
                        mm = pe.transpose(out, mat(t4 if name == "T4T" else xm), const("ident", rows, rows))
                        continue
                    y0v = t4[0][:, u, :] if g < 2 else y0s[:, h, :]
                    yv = xm[0][:, u, :] if g < 2 else ys[:, h, :]
                    lhsT, r = {
                        "A": (ar[hs, 0, ts], bt[hs, ts]), "H1": (mat(a4t), mat(xm)), "H2": (mat(a4t), mat(xm)),
                        "E16": (mat(n16), mat(tt)), "X1": (mat(em), mat(t4)), "X2": (mat(em), mat(xm)),
                        "X3": (mat(em), mat(xm)), "E64": (mat(n64), mat(tt)),
                        "G": (am[:, u, 1, :] if g < 2 else ams[:, h, 1, :], tm[0:rows, j, 2, hs]),
                        "Y0": (mat(tt), rhs[0:rows, j, h, :, :].rearrange("p a b -> p (a b)")),
                        "Y1": (mat(em), y0v), "Y2": (mat(em), yv), "Y3": (mat(em), yv),
                    }[name]
                    mm = pe.matmul(out, lhsT, r, start=True, stop=True)
                if part != 0:
                    mm.then_inc(t_mm[g], 1)

            def chunk_in(c, l, p):
                n = l * NPAIR + p
                j, ro, rows = (c // 2, 64 * (c % 2), CH) if c < NCH else (4, 0, TS)
                st = S[c % 2] if c < NCH else Ss[0]
                ts = slice(c * CH, c * CH + rows)
                if c == 0:
                    return
                if c in (1, 4, 8):
                    pe.wait_ge(t_out[(1, 4, 8).index(c)], n * NSTEP + NSTEP)
                if c < NCH:
                    pe.wait_ge(s_ready, n * 8 + c)
                else:
                    pe.wait_ge(ss_init, n + 1)
                pe.matmul(ps[ro:ro + rows, 5, 0:P], wt[:, ts], st[:, :], start=True, stop=True).then_inc(u_mm, 1)
                first = c in (1, 2, 4, 6, 8)
                if first:
                    pe.wait_ge(yw_ready, n * 5 + j)
                    pe.wait_ge(rp_ready, n + 1)
                pe.matmul(ps[:, 7, ro:ro + rows], st[:, :], flat(zs[:, bass.ds(p, 1), ts]), start=first, stop=True, skip_group_check=True)

            def chunk_out(c, l, p):
                n = l * NPAIR + p
                j, ro, rows = (c // 2, 64 * (c % 2), CH) if c < NCH else (4, 0, TS)
                pe.wait_ge(um_ready, n * 9 + c + 1)
                pe.matmul(ps[:, 6, 0:P], tm[ro:ro + rows, j, 0, :], um[ro:ro + rows, j, :], start=True, stop=False)
                pe.matmul(ps[:, 6, 0:P], tm[ro:ro + rows, j, 1, :], tm[ro:ro + rows, j, 2, :], start=False, stop=True).then_inc(s_mm, 1)

            def chunk_y(c, l, p):
                j = c // 2
                if c % 2 == 1 or c == NCH:
                    m = P if j < 4 else TS
                    for h in range(2):
                        hs = slice(64 * h, 64 * h + 64)
                        for src, q in ((um[0:m, j, hs], 0), (tm[0:m, j, 2, hs], 2)):
                            mm = pe.matmul(ps[hs, 7, 0:m], src, am[:, 2 * j + h, q, :] if j < 4 else ams[:, h, q, :],
                                           start=False, stop=True, skip_group_check=True)
                    mm.then_inc(y_mm, 1)

            def token_major(j, n, used):
                rows = P if j < 4 else TS
                for who, count in used:
                    pe.wait_ge(who, count)
                for q, src in enumerate((ar[:, 0, :], bt[:, :], kt[:, :], vc[:, :])):
                    mm = pe.transpose(ps[0:rows, 3 + j % 2, q * P:(q + 1) * P], src[:, j * P:j * P + rows], const("ident"))
                mm.then_inc(tm_mm, 1)

            def products(u, n):
                j, h = u // 2, u % 2
                rows, hs = (P if j < 4 else TS), slice(64 * h, 64 * h + 64)
                if u in (0, 4):
                    pe.wait_ge(tm_ready, n * 5 + (2 if u == 0 else 5))
                elif u not in (1, 5):
                    due = pe.to_reg(n * 10 + u - 1)
                    if j == 4:
                        constants_there()
                    pe.wait_ge(am_ready, due)
                for q, src in enumerate((bt, kt)):
                    mm = pe.matmul(ps[0:rows, 3 + u % 2, 2 * q * rows:2 * (q + 1) * rows].rearrange("p (a t) -> p a t", a=2),
                                   src[hs, j * P:j * P + rows], ar[hs, :, j * P:j * P + rows], start=(q == 0), stop=True,
                                   skip_group_check=True)
                mm.then_inc(am_mm, 1)

            def prepare_1(l, p, k, first):
                n = l * NPAIR + p
                if k == 1:
                    if first:
                        pe.wait_ge(bonus_ready, n)
                    else:
                        pe.wait_ge(s_ready, n * 8 - 12)
                    pe.wait_ge(staged, n + 1)
                    two(5, lora_st[0:64, :], lora[0:64, :]).then_inc(wa_mm, 1)
                if k == 2:
                    pe.wait_ge(sig_ready, n * 2 + 1)
                    two(5, lora_st[64:128, :], lora[64:128, :]).then_inc(wa_mm, 1)
                if k == 4:
                    pe.wait_ge(sig_ready, n * 2 + 2)
                    pe.wait_ge(kksq_ready, n + 1)
                    two(5, const("head_sum"), tA).then_inc(kkn_mm, 1)

            def prepare_2(l, p, k, first):
                n = l * NPAIR + p
                if k == 0:
                    if not first:
                        pe.wait_ge(ss_done, n - 1)
                    pe.wait_ge(rkk_ready, n + 1)
                    two(5, const("head_sum"), tA).then_inc(rk_mm, 1)

            def normalise(l, p, k, after_bonus):
                n = l * NPAIR + p
                if k == 1:
                    pe.wait_ge(ss_done, n + 1)
                    if after_bonus:
                        pe.wait_ge(bonus_ready, n + 3)
                    pe.wait_ge(yw_ready, n * 5 + 5)
                    for h in range(2):
                        mm = pe.matmul(ps[:, 5 + h, 0:HT], const("head_mean"), flat(zs[:, bass.ds(p, 1), h * HT:(h + 1) * HT]),
                                       start=True, stop=True)
                    mm.then_inc(pm_mm, 1)
                if k == 3:
                    pe.wait_ge(psq_ready, n + 1)
                    two(5, const("head_mean"), psq).then_inc(pv_mm, 1)
                if k == 5:
                    pe.wait_ge(hn_newton, n * 3 + 1)
                    pe.wait_ge(g_staged, n + 1)
                    two(5, g2_st[:, :], lgate).then_inc(pg_mm, 1)

            def half_a(l, p, left, right, nxt):
                n = l * NPAIR + p
                for k in range(SLOTS_A):
                    if right and k < 8:
                        step(8 + k, 1, n - 1)
                        step(8 + k, 2, n - 1)
                    if right and k == 8 and nxt:
                        pe.wait_ge(kkn_max, n + 2)
                    if right and k >= 8:
                        chunk_in(k - 4, l, p - 1)
                    if left and k < 2:
                        used = []
                        if k == 0:
                            used = [(ar_ready, n * 3 + 3), (bk_ready, n * 3 + 3), (vc_ready, n + 1), (n_ready[2], n * 2)]
                        token_major(k, n, used)
                    elif left and k < 4:
                        products(2 * k - 4, n)
                        products(2 * k - 3, n)
                    elif left and k < 8:
                        step(k - 4, 0, n)
                    elif left and k < 12:
                        step(k - 4, 0, n, 0)
                    if right and k >= 8:
                        chunk_out(k - 4, l, p - 1)
                    if left and 8 <= k < 12:
                        step(k - 4, 0, n, 1)
                    if right and k >= 8:
                        chunk_y(k - 4, l, p - 1)
                    if nxt:
                        prepare_1(l, p + 1, k, not right)

            def half_b(l, p, nxt, norm_before):
                n = l * NPAIR + p
                for k in range(SLOTS_B):
                    if k < 8:
                        step(8 + k, 0, n)
                    elif k < 12:
                        if k == 8:
                            pe.wait_ge(g_ready, n)
                            if nxt:
                                pe.wait_ge(bonus_ready, n + 2)
                        chunk_in(k - 8, l, p)
                    if k == 0:
                        token_major(2, n, [(n_ready[0], n * 2 + 2)])
                    elif k == 1:
                        token_major(3, n, [])
                        token_major(4, n, [(tm_ready, n * 5 + 3)])
                    elif k < 5:
                        products(2 * k, n)
                        products(2 * k + 1, n)
                    if 5 <= k < 8 or k == 12:
                        step(k - 5, 1, n)
                    if 8 <= k < 12:
                        step(k - 5, 1, n, 0)
                        chunk_out(k - 8, l, p)
                        step(k - 5, 1, n, 1)
                        chunk_y(k - 8, l, p)
                    if 6 <= k:
                        step(k - 6, 2, n)
                    if nxt:
                        prepare_2(l, p + 1, k, False)
                    if norm_before:
                        normalise(l, p - 1, k, nxt)

            with pe.Fori(0, DEPTH) as l:
                dense(l, "f1i", xh, xl, xl_ready, l * 40)
                dense(l, "f1o", hh, hl, hl_ready, l * (2 * FT))
                norm(l * 3)
                dense(l, "z", xh, xl, xl_ready, l * 40 + 8)
                for q in range(2):
                    pe.wait_ge(pool_step, l * 16 + (7, 16)[q])
                    two(4 + 2 * q, pool_bd[:, q, :], pooled[q]).then_inc(pool_mm, 1)
                pe.wait_ge(xl_ready, l * 40 + 18)
                heads(pe, l, half_a, half_b, prepare_1, prepare_2, normalise)
                dense(l, "wo", xh, xl, xl_ready, l * 40 + 16)
                norm(l * 3 + 1)
                dense(l, "f2i", xh, xl, xl_ready, l * 40 + 24)
                dense(l, "f2o", hh, hl, hl_ready, l * (2 * FT) + FT)
                dense(l, "gp", xh, xl, xl_ready, l * 40 + 32)
                norm(l * 3 + 2)

        @block.scalar
        def _(act):
            for m in range(KT):
                act.wait_ge(x_loaded[m], 16)
                act.activation(xh[:, m, :], y[:, m, :], ACT.Copy).then_inc(xh_ready, 1)
            for dst, src in ((cst[:, :], consts), (par[:, :], params), (shift_in[:, :, :], shift_hist),
                             (wkv_in[:, :, :, :], wkv_hist), (pool_w[:, :, :, :], poolw), (pool_hs[:, :, :, :], pool_hist)):
                act.dma_start(dst, src).then_inc(loaded, 16)
            for m in range(KT):
                act.wait_ge(xl_ready, m + 1)
                act.activation(y[:, m, :], y[:, m, :], ACT.Copy, scale=ALPHA).then_inc(ax_ready, 1)
            act.wait_ge(set_done, 3)
            act.wait_ge(loaded, 16 * NLOAD)

            def ffn(l, which, name):
                with act.Fori(0, FT) as m:
                    act.wait_ge(slot_used, used_count(l, name, 2 * m))
                    act.wait_ge(tile_out[1], out_count(l, name, m) - 1)
                    act.activation(halves(sg[:, :]), pair_bank(0), ACT.Silu).then_inc(tile_out[0], 1)
                    act.wait_ge(tile_out[1], out_count(l, name, m))
                    act.activation(row(hh, m), hf[:, :], ACT.Copy).then_inc(hh_ready, 1)

            def norm(l, which, b, ab, count):
                inst = l * 3 + which
                for m in range(KT):
                    act.wait_ge(d_ready, inst * 8 + m + 1)
                    if m >= 2:
                        act.wait_ge(var_mm, inst * 8 + m - 1)
                    act.activation(sq[m % 2][:, :], y[:, m, :], ACT.Square).then_inc(sq_ready, 1)
                act.wait_ge(var_mm, inst * 8 + 8)
                act.activation(halves(rs[:, :]), pair_bank(6), ACT.Abs_reciprocal_sqrt, bias=eps[:, 0:1]).then_inc(rs_ready, 1)
                for m in range(KT):
                    act.wait_ge(t_ready, inst * 8 + m + 1)
                    act.activation(xh[:, m, :], y[:, m, :], ACT.Identity, bias=col(l, b + m)).then_inc(xh_ready, 1)
                for m in range(KT):
                    act.wait_ge(xl_ready, count + m + 1)
                    act.activation(y[:, m, :], y[:, m, :], ACT.Identity, scale=ALPHA, bias=col(l, ab + m)).then_inc(ax_ready, 1)

            def z_copy(l, m, k):
                act.wait_ge(slot_used, used_count(l, "z", 2 * m + k))
                act.wait_ge(zs_ready, l * NSH + 2 * m + k + 1)
                act.activation(halves(zb[k][:, 1:T + 1]), pair_bank(2 * k), ACT.Copy).then_inc(tile_out[k], 1)

            def prepare_1(l, p, k, first):
                n = l * NPAIR + p
                if k == 1:
                    act.wait_ge(ar_ready, n * 3)
                    act.wait_ge(bk_ready, n * 3)
                    act.wait_ge(rk_mm, n)
                    act.activation(kkb[:, :], row(zs, p + 6), ACT.Identity, scale=col(l, p + COL["k_k"])).then_inc(kk_ready, 1)
                    act.wait_ge(kk_ready, n + 1)
                    act.activation(tA[:, :], kkb[:, :], ACT.Square).then_inc(kksq_ready, 1)
                if k == 1:
                    act.wait_ge(wa_mm, n * 2 + 1)
                    act.activation(halves(tB[:, :]), pair_bank(5), ACT.Sigmoid, bias=col(l, p + COL["w0"])).then_inc(sig_ready, 1)
                if k == 2:
                    act.wait_ge(wa_mm, n * 2 + 2)
                    act.activation(halves(aa[:, :]), pair_bank(5), ACT.Sigmoid, bias=col(l, p + COL["a0"])).then_inc(sig_ready, 1)
                if k == 3:
                    act.wait_ge(scan_ready, n + 1)
                    act.activation(Pb[:, 1:T + 1], Lb[:, :], ACT.Exp, scale=-DECAY).then_inc(decay_ready, 1)
                    act.activation(Pi[:, :], Lb[:, :], ACT.Exp, scale=DECAY).then_inc(decay_ready, 1)
                    act.activation(dec[:, bass.ds(p * (NCH + 1), NCH)], Lb[:, CH - 1:TP:CH], ACT.Exp, scale=-DECAY).then_inc(decay_ready, 1)
                    act.activation(dec[:, bass.ds(p * (NCH + 1) + NCH, 1)], Lb[:, T - 1:T], ACT.Exp, scale=-DECAY).then_inc(decay_ready, 1)
                    act.wait_ge(sig_ready, n * 2 + 2)
                    act.activation(tB[:, :], aa[:, :], ACT.Identity, scale=col(l, p + COL["k_a"]), bias=col(l, p + COL["one_ka"])).then_inc(kf_ready, 1)
                if k == 5:
                    act.wait_ge(kkn_max, n + 1)
                    act.activation(rn[:, :], nv[:, :], ACT.Abs_reciprocal_sqrt).then_inc(rn_ready, 1)

            def prepare_2(l, p, k, first):
                n = l * NPAIR + p
                if k == 6:
                    act.activation(vc[:, :], row(zs, p + 12), ACT.Copy).then_inc(vc_ready, 1)
                if k == 9:
                    act.wait_ge(rkk_ready, n + 1)
                    act.wait_ge(ar_ready, n * 3 + 1)
                    act.activation(row(zs, p), ar[:, 1, :], ACT.Copy).then_inc(rp_ready, 1)

            def normalise(l, p, k, after_bonus):
                n = l * NPAIR + p
                if k == 2:
                    act.wait_ge(po_ready, n)
                    act.wait_ge(pd_ready, n + 1)
                    act.activation(psq[:, :], pd[:, :], ACT.Square).then_inc(psq_ready, 1)
                if k == 3:
                    act.wait_ge(pv_mm, n + 1)
                    act.activation(halves(prs[:, :]), pair_bank(5), ACT.Abs_reciprocal_sqrt, bias=eps[:, 1:2]).then_inc(prs_ready, 1)
                if k == 5:
                    act.wait_ge(pt_ready, n + 1)
                    act.activation(psq[:, :], pd[:, :], ACT.Identity, scale=col(l, p + COL["lnx_g"]), bias=col(l, p + COL["lnx_b"])).then_inc(pi_ready, 1)
                if k == 6:
                    act.wait_ge(pg_mm, n + 1)
                    act.activation(halves(nt[:, :]), pair_bank(5), ACT.Copy).then_inc(g_ready, 1)

            def token_major(j, n):
                rows, b = (P if j < 4 else TS), 3 + j % 2
                act.wait_ge(tm_mm, n * 5 + j + 1)
                act.activation(rhs[0:rows, j, :, 0, :], ps[0:rows, b, 0:P].rearrange("p (h c) -> p h c", h=2), ACT.Copy).then_inc(tm_part, 1)
                act.activation(tm[0:rows, j, :, :].rearrange("p a b -> p (a b)"), ps[0:rows, b, P:4 * P], ACT.Copy).then_inc(tm_ready, 1)

            def step(s, g, n):
                name, tiles = STEPS[s], GROUPS[g]
                if name not in ("T4T", "T16T", "E16", "E64", "G", "Y0", "WT"):
                    return
                rows, nt_ = (P if g < 2 else TS), len(tiles)
                act.wait_ge(t_mm[g], n * NSTEP + s + 1)
                if name == "WT":
                    out, src = wt[:, tiles[0] * P:tiles[0] * P + rows * nt_], ps[:, g, 0:rows * nt_]
                elif name == "G":
                    out = rhs[0:rows, tiles[0]:tiles[0] + nt_, :, 1, :].rearrange("p j h c -> p (j h) c")
                    src = group_view(g, 64)
                elif name == "Y0":
                    out, src = (units(t4, g) if g < 2 else y0s[:, :, :]), group_view(g, P)
                else:
                    out, src = units(tt if name[0] == "T" else em, g), group_view(g, rows)
                act.activation(out, src, ACT.Copy).then_inc(t_out[g], 1)

            def y_tile(j, l, p):
                rows = P if j < 4 else TS
                act.wait_ge(y_mm, (l * NPAIR + p) * 5 + j + 6)
                act.activation(flat(zs[:, bass.ds(p, 1), j * P:j * P + rows]), ps[:, 7, 0:rows], ACT.Copy).then_inc(yw_ready, 1)

            def half_a(l, p, left, right, nxt):
                n = l * NPAIR + p
                for k in range(SLOTS_A):
                    if right and k < 8:
                        step(8 + k, 1, n - 1)
                        step(8 + k, 2, n - 1)
                    if left and k < 2:
                        token_major(k, n)
                    if left and 4 <= k < 12:
                        step(k - 4, 0, n)
                    if right and k in (9, 11, 12):
                        y_tile({9: 2, 11: 3, 12: 4}[k], l, p - 1)
                    if nxt:
                        prepare_1(l, p + 1, k, False)
                if not left:
                    act.wait_ge(s_ready, n * 8)
                    act.wait_ge(ss_done, n)
                    for q, st in enumerate((S[0], Ss[1])):
                        for h in range(2):
                            hs = slice(64 * h, 64 * h + 64)
                            act.dma_start(wkv_out[bass.ds(n - 1, 1), q, hs, :].rearrange("a p v -> p (a v)"), st[hs, hs]).then_inc(wkv_stored, 16)

            def half_b(l, p, nxt, norm_before):
                n = l * NPAIR + p
                for k in range(SLOTS_B):
                    if k < 8:
                        step(8 + k, 0, n)
                    if k == 0:
                        token_major(2, n)
                    if k == 1:
                        token_major(3, n)
                        token_major(4, n)
                    if 5 <= k < 13:
                        step(k - 5, 1, n)
                    if 6 <= k:
                        step(k - 6, 2, n)
                    if k in (9, 11):
                        y_tile({9: 0, 11: 1}[k], l, p)
                    if nxt:
                        prepare_2(l, p + 1, k, False)
                    if norm_before:
                        normalise(l, p - 1, k, nxt)

            with act.Fori(0, DEPTH) as l:
                ffn(l, 0, "f1i")
                norm(l, 0, COL["ln1_b"], COL["ab1"], l * 40 + 8)
                act.wait_ge(z_set, l + 1)
                with act.Fori(0, 9) as m:
                    for k in range(2):
                        z_copy(l, m, k)
                for k in range(2):
                    z_copy(l, 9, k)
                act.wait_ge(zs_ready, l * NSH + 19 + 2)
                act.activation(lora[0:64, :], lora[0:64, :], ACT.Tanh).then_inc(lora_act, 1)
                act.wait_ge(zs_ready, l * NSH + 20 + 2)
                act.activation(lgate[:, :], lgate[:, :], ACT.Sigmoid).then_inc(lora_act, 1)
                for q in range(2):
                    act.wait_ge(slot_used, used_count(l, "z", 20 + q))
                    act.activation(ub[q][:, HIST:HIST + HT], ps[:, 2 * q, 0:HT], ACT.Copy).then_inc(u_part, 1)
                    act.activation(ub[q][:, UW - TS:UW], ps[:, 2 * q + 1, TP - HT:HT], ACT.Copy).then_inc(u_part, 1)
                    act.activation(ub[q][:, HIST + HT:HIST + TP], ps[:, 2 * q + 1, 0:TP - HT], ACT.Copy).then_inc(tile_out[q], 1)
                    act.wait_ge(tile_out[q], out_count(l, "z", 10))
                    for s, a in enumerate((TP, UW - HIST)):
                        act.dma_start(pool_out[bass.ds(l, 1), s, :, q, :].rearrange("a p t -> p (a t)"),
                                      ub[q][:, a:a + HIST]).then_inc(pool_stored, 16)
                for q in range(2):
                    act.wait_ge(pool_mm, l * 2 + q + 1)
                    act.activation(halves(mf[q][:, :]), pair_bank(4 + 2 * q), ACT.Identity, scale=col(l, COL["pool_scale"] + q)).then_inc(mf_ready, 1)
                    act.wait_ge(mf_ready, l * 2 + q + 1)
                    act.activation(xh[:, q, :], mf[q][:, :], ACT.Copy).then_inc(xh_ready, 1)
                act.wait_ge(last_ready, l * NSH + NSH)
                act.dma_start(shift_out[bass.ds(l, 1)].rearrange("a p k s -> p (a k) s"), last_z[:, :, :]).then_inc(shift_stored, 16)
                act.wait_ge(xl_ready, l * 40 + 18)
                heads(act, l, half_a, half_b, prepare_1, prepare_2, normalise)
                with act.Fori(0, NPAIR) as p:
                    act.wait_ge(po_ready, (l + 1) * NPAIR)
                    act.activation(row(xh, p + 2), row(zs, p), ACT.Copy).then_inc(xh_ready, 1)
                norm(l, 1, COL["ln2_b"], COL["ab2"], l * 40 + 24)
                act.wait_ge(wkv_stored, (l + 1) * (NPAIR * 64))
                ffn(l, 1, "f2i")
                with act.Fori(0, 4) as m:
                    for k in range(2):
                        act.wait_ge(tile_out[k], out_count(l, "f2o", m))
                        act.activation(row(xh, 2 * m + k), row(y, 2 * m + k), ACT.Copy).then_inc(xh_ready, 1)
                act.wait_ge(p_loaded, l * 32 + 32)
                act.wait_ge(slot_used, used_count(l, "f2o", 23))
                for k in range(2):
                    act.activation(hh[:, k, :], sq[k][:, :], ACT.Copy).then_inc(ph_ready, 1)
                with act.Fori(0, 8) as m:
                    act.wait_ge(slot_used, used_count(l, "gp", 2 * m))
                    act.wait_ge(tile_out[1], out_count(l, "gp", m) - 1)
                    act.activation(halves(sg[:, :]), pair_bank(0), ACT.Sigmoid, bias=col(l, m + COL["gate_b"])).then_inc(tile_out[0], 1)
                norm(l, 2, COL["ln3_b"], COL["ab3"], l * 40 + 40)

        @block.vector
        def _(dve):
            dve.memset(eps[:, 0:1], LN_EPS).then_inc(set_done, 1)
            dve.memset(eps[:, 1:2], LNX_EPS).then_inc(set_done, 1)
            dve.memset(pool_bd[:, :, :], 0.0).then_inc(set_done, 1)
            dve.sem_inc(zs_ready, 2)

            for m in range(KT):
                dve.wait_ge(xh_ready, m + 1)
                dve.tensor_tensor(xl[:, m, :], y[:, m, :], xh[:, m, :].bitcast(F32), ALU.subtract).then_inc(xl_ready, 1)
            dve.wait_ge(loaded, 16 * NLOAD)
            pv = par[:, :].rearrange("p (l c) -> p l c", l=DEPTH)
            ka, ab = (pv[:, :, COL[c]:COL[c] + w] for c, w in (("one_ka", NPAIR), ("ab1", 3 * KT)))
            dve.tensor_scalar(ka, ka, -1.0, 1.0, ALU.mult, ALU.add)
            dve.tensor_scalar(ab, ab, ALPHA, None, ALU.mult)

            def ffn(l, which, name):
                with dve.Fori(0, FT) as m:
                    f = l * (2 * FT) + which * FT + m
                    dve.wait_ge(slot_used, used_count(l, name, 2 * m + 1))
                    dve.wait_ge(tile_out[0], out_count(l, name, m))
                    dve.wait_ge(hl_ready, f)
                    dve.tensor_tensor(halves(hf[:, :]), halves(sg[:, :]), pair_bank(2), ALU.mult).then_inc(tile_out[1], 1)
                    dve.wait_ge(hh_ready, f + 1)
                    dve.tensor_tensor(row(hl, m), hf[:, :], row(hh, m).bitcast(F32), ALU.subtract).then_inc(hl_ready, 1)

            def residual(l, inst, name, scale, parts):
                if parts is None:
                    dve.memset(ysum[:, :], 0.0).then_inc(sum_ready, 1)
                due = dve.to_reg(inst * 8 + 8)
                dve.wait_ge(loaded, 16 * NLOAD)
                dve.wait_ge(ax_ready, due)
                per = 3 if name in ("f1o", "f2o") else 1
                with dve.Fori(0, 4) as m:
                    for k in range(2):
                        dve.wait_ge(slot_used, used_count(l, name, 2 * per * m + per * k + per - 1))
                        dve.scalar_tensor_tensor(halves(row(y, 2 * m + k)), pair_bank(2 * k), scale, halves(row(y, 2 * m + k)),
                                                 ALU.mult, ALU.add).then_inc(tile_out[k], 1)
                        if parts is None:
                            dve.wait_ge(tile_out[k], out_count(l, name, m))
                            dve.wait_ge(sum_ready, inst * 9 + 2 * m + k + 1)
                            dve.tensor_tensor(ysum[:, :], ysum[:, :], row(y, 2 * m + k), ALU.add).then_inc(sum_ready, 1)
                        else:
                            dve.wait_ge(xh_ready, parts + 2 * m + k + 1)
                            dve.tensor_tensor(row(xl, 2 * m + k), row(y, 2 * m + k), row(xh, 2 * m + k).bitcast(F32),
                                              ALU.subtract).then_inc(xl_ready, 1)

            def newton(r, tmp, v, bias, steps, count):
                dve.scalar_tensor_tensor(halves(tmp), v, bias, halves(r), ALU.add, ALU.mult).then_inc(steps, 1)
                dve.wait_ge(steps, count + 1)
                dve.scalar_tensor_tensor(tmp, tmp, -0.5, r, ALU.mult, ALU.mult).then_inc(steps, 1)
                dve.wait_ge(steps, count + 2)
                dve.scalar_tensor_tensor(r, tmp, 1.5, r, ALU.add, ALU.mult).then_inc(steps, 1)

            def norm(l, inst, count, g, b):
                dve.wait_ge(mean_mm, inst + 1)
                for m in range(KT):
                    dve.tensor_tensor(halves(y[:, m, :]), halves(y[:, m, :]), pair_bank(4), ALU.subtract).then_inc(d_ready, 1)
                dve.wait_ge(rs_ready, inst + 1)
                newton(rs[:, :], hf[:, :], pair_bank(6), LN_EPS, ln_newton, inst * 3)
                dve.wait_ge(ln_newton, inst * 3 + 3)
                for m in range(KT + 1):
                    if m < KT:
                        dve.scalar_tensor_tensor(y[:, m, :], y[:, m, :], col(l, g + m), rs[:, :], ALU.mult, ALU.mult).then_inc(t_ready, 1)
                    if m >= 1:
                        dve.wait_ge(xh_ready, count + m)
                        dve.scalar_tensor_tensor(xl[:, m - 1, :], y[:, m - 1, :], col(l, b + m - 1), xh[:, m - 1, :].bitcast(F32),
                                                 ALU.add, ALU.subtract).then_inc(xl_ready, 1)

            def shifted(l, m, k, dst):
                i = l * NSH + 2 * m + k
                z = zb[k]
                dve.wait_ge(tile_out[k], out_count(l, "z", m))
                dve.wait_ge(zs_ready, i + 2)
                dve.tensor_tensor(zd[:, :], z[:, 0:T], z[:, 1:T + 1], ALU.subtract).then_inc(zd_ready, 1)
                dve.tensor_copy(last_z[:, bass.ds(2 * m + k, 1), :].rearrange("p a s -> p (a s)"), z[:, TP:T + 1:TS]).then_inc(last_ready, 1)
                dve.wait_ge(zd_ready, i * 2 + 1)
                dve.tensor_tensor(zd[:, TP:TP + 1], flat(shift_in[:, bass.ds(l, 1), bass.ds(2 * m + k, 1)]), z[:, TP + 1:TP + 2],
                                  ALU.subtract).then_inc(zd_ready, 1)
                dve.wait_ge(zd_ready, i * 2 + 2)
                dve.scalar_tensor_tensor(dst, zd[:, :], col(l, 2 * m + (k + COL["mu"])), z[:, 1:T + 1], ALU.mult, ALU.add).then_inc(zs_ready, 1)

            def pooling(l):
                step = [l * 16]

                def link(ins):
                    ins.then_inc(pool_step, 1)
                    step[0] = step[0] + 1
                    dve.wait_ge(pool_step, step[0])

                for q in range(2):
                    e = ub[q]
                    dve.wait_ge(tile_out[q], out_count(l, "z", 10))
                    link(dve.tensor_tensor(swA[:, 1:UW], e[:, 1:UW], e[:, 0:UW - 1], ALU.add))
                    link(dve.tensor_tensor(swB[:, 3:UW], swA[:, 3:UW], swA[:, 1:UW - 2], ALU.add))
                    if q == 1:
                        link(dve.tensor_tensor(swA[:, 7:UW], swB[:, 7:UW], swB[:, 3:UW - 4], ALU.add))
                        link(dve.tensor_tensor(swB[:, 15:UW], swA[:, 15:UW], swA[:, 7:UW - 8], ALU.add))
                    link(dve.tensor_copy(swB[0:64, 15:UW], swA[0:64, 15:UW]))
                    w = cst[:, CCOL["winv"][0] + q:CCOL["winv"][0] + q + 1]
                    link(dve.scalar_tensor_tensor(pooled[q][:, 0:TP], swB[:, HIST:HIST + TP], w, e[:, HIST:HIST + TP], ALU.mult, ALU.subtract))
                    link(dve.scalar_tensor_tensor(pooled[q][:, TP:T], swB[:, UW - TS:UW], w, e[:, UW - TS:UW], ALU.mult, ALU.subtract))
                    r = CCOL["rcnt"][0] + q * HIST
                    link(dve.tensor_tensor(swA[:, 0:HIST], swB[:, HIST:2 * HIST], cst[:, r:r + HIST], ALU.mult))
                    link(dve.tensor_tensor(pooled[q][:, 0:HIST], swA[:, 0:HIST], e[:, HIST:2 * HIST], ALU.subtract))

            def prepare_1(l, p, k, first):
                n = l * NPAIR + p
                r_ = row(zs, p)
                if k == 0:
                    dve.wait_ge(wa_mm, n * 2)
                    dve.tensor_copy(lora_st[:, :], lora_all[:, bass.ds(p * P, P)]).then_inc(staged, 1)
                if k == 2:
                    dve.wait_ge(sig_ready, n * 2 + 1)
                    dve.tensor_tensor_scan(Lb[:, :], const("reset"), tB[:, :], 0.0, ALU.mult, ALU.add).then_inc(scan_ready, 1)
                if k == 5:
                    dve.wait_ge(decay_ready, n * 4 + 4)
                    dve.wait_ge(kkn_mm, n + 1)
                    dve.tensor_scalar(halves(nv[:, :]), pair_bank(5), 1e-24, None, ALU.max).then_inc(kkn_max, 1)
                if k == 10:
                    dve.wait_ge(kkb_ready, n + 1)
                    dve.wait_ge(kp_ready, n + 1)
                    dve.scalar_tensor_tensor(tA[:, :], r_, col(l, p + COL["r_k"]), tB[:, :], ALU.mult, ALU.mult).then_inc(rkk_ready, 1)

            def prepare_2(l, p, k, first):
                n = l * NPAIR + p
                r_, k_, v_ = row(zs, p), row(zs, p + 6), row(zs, p + 12)
                if k == 8:
                    dve.tensor_tensor(ar[:, 1, :], r_, Pb[:, 1:T + 1], ALU.mult).then_inc(ar_ready, 1)
                if k == 1:
                    dve.wait_ge(rk_mm, n + 1)
                    dve.tensor_tensor(halves(k_), pair_bank(5), halves(v_), ALU.mult).then_inc(bonus_ready, 1)
                if k == 9:
                    dve.scalar_tensor_tensor(ar[:, 0, :], kkb[:, :], -1.0, Pb[:, 0:T], ALU.mult, ALU.mult).then_inc(ar_ready, 1)
                    dve.wait_ge(ar_ready, n * 3 + 2)
                    dve.tensor_scalar(ar[:, 0, 0:T:CH], kkb[:, 0:T:CH], -1.0, None, ALU.mult).then_inc(ar_ready, 1)

            def normalise(l, p, k, after_bonus):
                n = l * NPAIR + p
                if k == 0:
                    dve.wait_ge(pg_mm, n)
                    dve.tensor_copy(g2_st[:, :], g2_all[:, bass.ds(p * P, P)]).then_inc(g_staged, 1)
                if k == 2:
                    dve.wait_ge(pm_mm, n + 1)
                    dve.tensor_tensor(halves(pd[:, :]), halves(row(zs, p)), pair_bank(5), ALU.subtract).then_inc(pd_ready, 1)
                if k == 4:
                    dve.wait_ge(prs_ready, n + 1)
                    newton(prs[:, :], psq[:, :], pair_bank(5), LNX_EPS, hn_newton, n * 3)

            def products(u, n):
                j, h = u // 2, u % 2
                rows, b = (P if j < 4 else TS), 3 + u % 2
                dve.wait_ge(y_mm, n * 5 + j + 1)
                dve.wait_ge(am_mm, n * 10 + u + 1)
                dve.tensor_tensor(a4t[0][:, u, :] if j < 4 else a4t[1][:, h, :], ps[0:rows, b, 0:rows], const("m4t", rows, rows), ALU.mult).then_inc(am_part, 1)
                mask = const("am", rows).rearrange("p (a t) -> p a t", a=3)[:, :, 0:rows]
                dve.tensor_tensor(am[:, u, :, :] if j < 4 else ams[:, h, :, :], ps[0:rows, b, rows:4 * rows].rearrange("p (a t) -> p a t", a=3),
                                  mask, ALU.mult).then_inc(am_ready, 1)

            def step(s, g, n):
                name = STEPS[s]
                if name not in ("A", "H1", "H2", "X1", "X2", "X3", "Y1", "Y2", "Y3"):
                    return
                rows = P if g < 2 else TS
                dve.wait_ge(t_mm[g], n * NSTEP + s + 1)
                src = group_view(g, P if name[0] == "Y" else rows)
                if name == "A":
                    dve.tensor_tensor(a_units(xm, g), a_view(g), a_spread("m4", g), ALU.mult).then_inc(t_part[g], 1)
                    dve.wait_ge(t_part[g], n * (2, 2, 1)[g] + 1)
                    dve.tensor_tensor(units(xm, g), units(xm, g), spread("ident", g), ALU.add).then_inc(t_out[g], 1)
                    dve.tensor_tensor(a_units(n16, g), a_view(g), a_spread("m16", g), ALU.mult).then_inc(n_ready[g], 1)
                    dve.tensor_tensor(a_units(n64, g), a_view(g), a_spread("m64", g), ALU.mult).then_inc(n_ready[g], 1)
                elif name[0] == "H":
                    dve.tensor_tensor(units(xm if name == "H1" else t4, g), src, spread("ident", g), ALU.add).then_inc(t_out[g], 1)
                elif name == "Y3":
                    for q in range(2 if g < 2 else 1):
                        j = 2 * g + q
                        o = xm[0][:, 2 * j:2 * j + 2, :] if g < 2 else ys[:, :, :]
                        i1 = t4[0][:, 2 * j:2 * j + 2, :] if g < 2 else y0s[:, :, :]
                        dve.tensor_tensor(o.rearrange("p a (h c) -> p h a c", h=2), src[:, 2 * q:2 * q + 2, :].rearrange("p h (a c) -> p h a c", a=2),
                                          i1.rearrange("p h (a c) -> p h a c", a=2), ALU.add).then_inc((t_part if g < 2 and q == 0 else t_out)[g], 1)
                elif name[0] == "Y" and g == 2:
                    dve.tensor_tensor(ys[:, :, :], src, y0s[:, :, :], ALU.add).then_inc(t_out[g], 1)
                else:
                    dve.tensor_tensor(units(xm, g), src, units(t4, g), ALU.add).then_inc(t_out[g], 1)

            def chunk_in(c, n):
                j, ro, rows = (c // 2, 64 * (c % 2), CH) if c < NCH else (4, 0, TS)
                g_part = xm[0][ro:ro + rows, 2 * j + 1, :] if j < 4 else ys[:, 1, :]
                out = um[ro:ro + rows, j, :]
                if c == 0:
                    dve.wait_ge(t_out[0], n * NSTEP + NSTEP - 1)
                    dve.tensor_copy(out, g_part).then_inc(um_ready, 1)
                else:
                    dve.wait_ge(u_mm, n * 8 + c)
                    dve.tensor_tensor(out, ps[ro:ro + rows, 5, 0:P], g_part, ALU.add).then_inc(um_ready, 1)

            def chunk_out(c, l, p):
                n = l * NPAIR + p
                decay = dec[:, bass.ds(p * (NCH + 1) + c, 1)]
                dve.wait_ge(s_mm, n * 9 + c + 1)
                if c == 0:
                    dve.scalar_tensor_tensor(S[1][:, :], ps[:, 6, 0:P], decay, const("head_sum"), ALU.mult, ALU.mult).then_inc(s_ready, 1)
                    return
                dve.scalar_tensor_tensor(dS[:, :], ps[:, 6, 0:P], decay, const("head_sum"), ALU.mult, ALU.mult).then_inc(ds_ready, 1)
                dve.wait_ge(ds_ready, n * 8 + c)
                if c == NCH:
                    dve.scalar_tensor_tensor(Ss[1][:, :], Ss[0][:, :], decay, dS[:, :], ALU.mult, ALU.add).then_inc(ss_done, 1)
                    return
                if c == 1:
                    dve.wait_ge(wkv_stored, n * 64)
                dve.wait_ge(s_ready, n * 8 + c)
                dve.scalar_tensor_tensor(S[(c + 1) % 2][:, :], S[c % 2][:, :], decay, dS[:, :], ALU.mult, ALU.add).then_inc(s_ready, 1)

            def sample_state(l, p):
                n = l * NPAIR + p
                dve.wait_ge(y_mm, n * 5 + 5)
                dve.wait_ge(ss_done, n)
                for h in range(2):
                    hs = slice(64 * h, 64 * h + 64)
                    dve.tensor_copy(Ss[0][hs, hs], wkv_in[hs, bass.ds(l, 1), bass.ds(p, 1), :].rearrange("p a b v -> p (a b v)")).then_inc(
                        (ss_part, ss_init)[h], 1)

            def half_a(l, p, left, right, nxt):
                n = l * NPAIR + p
                for k in range(SLOTS_A):
                    if right and k < 8:
                        step(8 + k, 1, n - 1)
                        step(8 + k, 2, n - 1)
                    if right and k == 7:
                        sample_state(l, p - 1)
                    if right and k >= 8:
                        chunk_in(k - 4, n - 1)
                        chunk_out(k - 4, l, p - 1)
                    if left and 2 <= k < 4:
                        products(2 * k - 4, n)
                        products(2 * k - 3, n)
                    if left and 4 <= k < 12:
                        step(k - 4, 0, n)
                    if nxt:
                        prepare_1(l, p + 1, k, False)

            def half_b(l, p, nxt, norm_before):
                n = l * NPAIR + p
                for k in range(SLOTS_B):
                    if k < 8:
                        step(8 + k, 0, n)
                    elif k < 12:
                        chunk_in(k - 8, n)
                        chunk_out(k - 8, l, p)
                    if 2 <= k < 5:
                        products(2 * k, n)
                        products(2 * k + 1, n)
                    if 5 <= k < 13:
                        step(k - 5, 1, n)
                    if 6 <= k:
                        step(k - 6, 2, n)
                    if nxt:
                        prepare_2(l, p + 1, k, False)
                    if norm_before:
                        normalise(l, p - 1, k, nxt)

            with dve.Fori(0, DEPTH) as l:
                ffn(l, 0, "f1i")
                residual(l, l * 3, "f1o", 0.5, None)
                norm(l, l * 3, l * 40 + 8, COL["ln1_g"], COL["ln1_b"])
                dve.wait_ge(shift_stored, l * 16)
                for k in range(2):
                    dve.memset(zb[k][:, 0:1], 0.0)
                    dve.memset(ub[k][:, 0:HIST], 0.0)
                    dve.tensor_copy(ub[k][:, HIST + TP:HIST + TP + HIST], flat(pool_hs[:, bass.ds(l, 1), k, :]))
                    for h in range(2):
                        hs = slice(64 * h, 64 * h + 64)
                        ins = dve.tensor_copy(pool_bd[hs, k, hs], flat(pool_w[hs, bass.ds(l, 1), k, :]))
                ins.then_inc(z_set, 1)
                with dve.Fori(0, 9) as m:
                    for k in range(2):
                        shifted(l, m, k, row(zs, 2 * m + k))
                shifted(l, 9, 0, lora[:, :])
                shifted(l, 9, 1, lgate[:, :])
                pooling(l)
                for q in range(2):
                    dve.wait_ge(xh_ready, l * 40 + 17 + q)
                    dve.tensor_tensor(xl[:, q, :], mf[q][:, :], xh[:, q, :].bitcast(F32), ALU.subtract).then_inc(xl_ready, 1)
                dve.wait_ge(pool_stored, l * 64 + 64)
                dve.wait_ge(lora_act, l * 2 + 2)
                dve.wait_ge(layer_loaded, l * 32 + 32)
                dve.memset(Pb[:, 0:1], 1.0)
                dve.memset(Ss[0][:, :], 0.0).then_inc(set_done, 1)
                dve.wait_ge(set_done, l + 4)
                heads(dve, l, half_a, half_b, prepare_1, prepare_2, normalise)
                with dve.Fori(0, NPAIR) as p:
                    dve.wait_ge(xh_ready, l * 40 + p + 19)
                    dve.tensor_tensor(row(xl, p + 2), row(zs, p), row(xh, p + 2).bitcast(F32), ALU.subtract).then_inc(xl_ready, 1)
                residual(l, l * 3 + 1, "wo", 1.0, None)
                norm(l, l * 3 + 1, l * 40 + 24, COL["ln2_g"], COL["ln2_b"])
                due = dve.to_reg((l + 1) * (NPAIR * 64))
                dve.wait_ge(loaded, 16 * NLOAD)
                dve.wait_ge(wkv_stored, due)
                ffn(l, 1, "f2i")
                residual(l, l * 3 + 2, "f2o", 0.5, l * 40 + 32)
                for k in range(2):
                    dve.wait_ge(ph_ready, l * 2 + k + 1)
                    dve.tensor_tensor(hl[:, k, :], sq[k][:, :], hh[:, k, :].bitcast(F32), ALU.subtract).then_inc(pl_ready, 1)
                dve.memset(ysum[:, :], 0.0).then_inc(sum_ready, 1)
                with dve.Fori(0, KT) as m:
                    dve.wait_ge(slot_used, used_count(l, "gp", 2 * m + 1))
                    dve.wait_ge(tile_out[0], out_count(l, "gp", m))
                    dve.tensor_tensor(halves(hf[:, :]), halves(sg[:, :]), pair_bank(2), ALU.mult).then_inc(tile_out[1], 1)
                    dve.wait_ge(tile_out[1], out_count(l, "gp", m))
                    dve.tensor_tensor(row(y, m), row(y, m), hf[:, :], ALU.add).then_inc(y_ready, 1)
                    dve.wait_ge(y_ready, l * 8 + m + 1)
                    dve.wait_ge(sum_ready, l * 27 + 18 + m + 1)
                    dve.tensor_tensor(ysum[:, :], ysum[:, :], row(y, m), ALU.add).then_inc(sum_ready, 1)
                norm(l, l * 3 + 2, l * 40 + 40, COL["ln3_g"], COL["ln3_b"])
            dve.wait_ge(xl_ready, DEPTH * 40 + 8)
            dve.wait_ge(ax_ready, DEPTH * 24 + 8)
            for m in range(KT):
                dve.tensor_tensor(y[:, m, :], xh[:, m, :].bitcast(F32), xl[:, m, :].bitcast(F32), ALU.add).then_inc(fin_ready, 1)


def constants():
    i = np.arange(P)
    t, s = i[:, None], i[None, :]
    same = lambda n: (t // n) == (s // n)
    low = s < t
    c = {
        "ident": t == s, "mean_d": np.full((P, P), 1.0 / D), "head_sum": same(64), "head_mean": same(64) / 64.0,
        "m4": low & same(4), "m16": low & same(16) & ~same(4), "m64": low & same(64) & ~same(16), "m4t": (t < s) & same(4),
        "am": np.concatenate([(t <= s) & same(64), (t < s) & same(64), (t <= s) & same(64)], axis=1),
        "reset": np.tile((np.arange(T) % CH != 0), (P, 1)),
    }
    wins = np.array([[2, 8], [4, 16]])[i // 64]
    c["winv"] = 1.0 / wins
    c["rcnt"] = np.concatenate([1.0 / np.minimum(np.arange(HIST)[None, :] + 1, wins[:, q:q + 1]) for q in range(2)], axis=1)
    return np.ascontiguousarray(np.concatenate([np.asarray(c[n], np.float32) for n, _ in CONSTS], axis=1))


def kernel(**inputs):
    import concourse.bacc as bacc
    from concourse.bass_utils import run_bass_kernel_spmd

    a = {k: np.asarray(v) for k, v in inputs.items()}
    L = DEPTH

    def channels(x, n):
        x = x.reshape(x.shape[:-1] + (n, P))
        return np.moveaxis(x, -1, 0)

    def tokens(x):
        return x.T.reshape(-1, P, x.shape[0]).transpose(1, 0, 2)

    def slots(w):
        n, k, m = w.shape
        return w.reshape(n, k // P, P, m // P, P).transpose(0, 3, 2, 1, 4)

    def ffn_in(w):
        s = slots(w)
        return np.stack([s[:, :FT], s[:, FT:]], axis=2).reshape((L * 2 * FT,) + s.shape[2:])

    def flat_slots(s):
        return s.reshape((-1,) + s.shape[2:])

    z = slots(a["w_in"])
    cols = []
    for n, w in COLS:
        src = {"gate_b": "ple_gate_b", "mu": "mu_shift", "one_ka": "k_a", "ab1": "ln1_b", "ab2": "ln2_b", "ab3": "ln3_b"}.get(n, n)
        cols.append(channels(a[src].reshape(L, -1), w))
    lora = np.concatenate([a["w2"], a["a2"]], axis=1)
    pw = a["pool_w"].reshape(L, 2, 2, 64, 64)
    st = a["state_wkv"][:, 0].reshape(L, NPAIR, 2, 64, 64)
    arrays = {
        "xT": tokens(np.concatenate([a["x_prompt"][0], a["x_sample"][0]], axis=0)),
        "pT": np.stack([tokens(np.concatenate([a["p_prompt"][i, 0], a["p_sample"][i, 0]], axis=0)) for i in range(L)]),
        "w1i": ffn_in(a["ffn1_w_in"]), "w1o": flat_slots(slots(a["ffn1_w_out"])),
        "wz": flat_slots(np.concatenate([z[:, 2:], z[:, :2]], axis=1)), "wo": flat_slots(slots(a["w_out"])),
        "w2i": ffn_in(a["ffn2_w_in"]), "w2o": flat_slots(slots(a["ffn2_w_out"])),
        "wg": flat_slots(slots(a["ple_gate_w"])), "wp": flat_slots(slots(a["ple_w"])),
        "params": np.concatenate(cols, axis=2).reshape(P, L * NPAR),
        "consts": constants(),
        "poolw": pw.transpose(2, 3, 0, 1, 4).reshape(P, L, 2, 64),
        "lora_w": lora, "g2_w": a["g2"],
        "pool_hist": channels(a["state_pool"][:, 0].transpose(0, 1, 2), 2).transpose(0, 1, 3, 2),
        "shift_hist": channels(a["state_shift"][:, 0], NSH),
        "wkv_hist": st.transpose(2, 4, 0, 1, 3).reshape(P, L, NPAIR, 64),
    }
    arrays = {k: np.ascontiguousarray(v) for k, v in arrays.items()}
    outs = {"y_out": (P, KT, T), "pool_out": (L, 2, P, 2, HIST), "shift_out": (L, P, NSH, 2), "wkv_out": (L * NPAIR, 2, P, 64)}
    nc = bacc.Bacc("TRN2", target_bir_lowering=False, num_devices=1)
    args = [nc.dram_tensor("in_" + k, v.shape, F32, kind="ExternalInput").ap() for k, v in arrays.items()]
    args += [nc.dram_tensor(k, s, F32, kind="ExternalOutput").ap() for k, s in outs.items()]
    build(nc, *args)
    r = run_bass_kernel_spmd(nc, [{"in_" + k: v for k, v in arrays.items()}], core_ids=[0]).results[0]
    yo = np.asarray(r["y_out"]).transpose(2, 1, 0).reshape(T, D)
    po = np.asarray(r["pool_out"]).transpose(1, 0, 4, 3, 2).reshape(2, L, 1, HIST, 2 * P)
    so = np.asarray(r["shift_out"]).transpose(3, 0, 2, 1).reshape(2, L, 1, NSH * P)
    wo = np.asarray(r["wkv_out"]).reshape(L, NPAIR, 2, 2, 64, 64).transpose(2, 0, 1, 3, 5, 4).reshape(2, L, 1, 2 * NPAIR, 64, 64)
    c = np.ascontiguousarray
    return (c(yo[None, :TP]), c(yo[None, TP:]), c(po[0]), c(so[0]), c(wo[0]), c(po[1]), c(so[1]), c(wo[1]))
```

```python
from contextlib import ExitStack

import numpy as np

import concourse.bass as bass
from concourse import mybir

F32 = mybir.dt.float32
F32R = mybir.dt.float32r
ACT = mybir.ActivationFunctionType
ALU = mybir.AluOpType

P = 128
DEPTH = 2
D = 1024
KT = D // P
TP, TS = 512, 32
T = TP + TS
HT = T // 2
FF = 2816
FT = FF // P
DR = 768
NPAIR = DR // P
NSH = 20
NZ = 22
HIST = 15
CH = 64
NCH = TP // CH
ALPHA = (2.0 * DEPTH) ** 0.25
LN_EPS, LNX_EPS = 1e-5, 64e-5
DECAY = float(np.exp(-0.5))

COLS = [("ln1_g", 8), ("ln1_b", 8), ("ln2_g", 8), ("ln2_b", 8), ("ln3_g", 8), ("ln3_b", 8), ("gate_b", 8),
        ("mu", NSH), ("w0", 6), ("a0", 6), ("k_k", 6), ("k_a", 6), ("r_k", 6), ("lnx_g", 6), ("lnx_b", 6),
        ("pool_scale", 2), ("one_ka", 6), ("ab1", 8), ("ab2", 8), ("ab3", 8)]
COL = {}
NPAR = 0
for _n, _w in COLS:
    COL[_n] = NPAR
    NPAR += _w

PHASES = [("f1i", FT, [8, 8]), ("f1o", 4, [8, 7, 7, 8, 7, 7]), ("z", NZ // 2, [8, 8]), ("wo", 4, [8, 8]),
          ("f2i", FT, [8, 8]), ("f2o", 4, [8, 7, 7, 8, 7, 7]), ("gp", 4, [4, 4, 2, 4, 4, 2])]
SLOT0, SLOTS = {}, 0
for _n, _b, _k in PHASES:
    SLOT0[_n] = SLOTS
    SLOTS += _b * len(_k)
TILE0, TILES = {}, 0
for _n, _c in [("f1i", 2 * FT), ("f1o", 8), ("z", NZ), ("wo", 8), ("f2i", 2 * FT), ("f2o", 8), ("gp", 16)]:
    TILE0[_n] = TILES
    TILES += _c

CONSTS = [("ident", P), ("swap", P), ("mean_d", P), ("head_sum", P), ("head_mean", P), ("m4", P), ("m16", P), ("m64", P),
          ("m4t", P), ("am", 3 * P), ("reset", T), ("winv", 2), ("rcnt", 2 * HIST)]
CCOL, NCONST = {}, 0
for _n, _w in CONSTS:
    CCOL[_n] = (NCONST, _w)
    NCONST += _w

STEPS = ["A", "H1", "H2", "T4T", "E16", "X1", "X2", "X3", "T16T", "G", "Y0", "E64", "Y1", "Y2", "Y3", "WT"]
NSTEP = len(STEPS)
GROUPS = [(0, 1), (2, 3), (4,)]


def build(nc, xT, pT, w1i, w1o, wz, wo, w2i, w2o, wg, wp, params, consts, poolw, lora_w, g2_w,
          pool_hist, shift_hist, wkv_hist, y_out, pool_out, shift_out, wkv_out):
    ctx = ExitStack()
    with ctx:
        base = (nc.sbuf_base + 31) // 32 * 32
        top = [base]

        def at(name, shape, dt, addr):
            size = int(np.prod(shape[1:])) * 4
            return nc.alloc_sbuf_tensor_at(name, shape, dt, offset=addr), (addr + size + 31) // 32 * 32

        def sb(name, shape, dt=F32):
            t, top[0] = at(name, shape, dt, top[0])
            return t

        y = sb("y", [P, KT, T])
        xh_addr = top[0]
        xh = sb("xh", [P, KT, T], F32R)
        xl_addr = top[0]
        xl = sb("xl", [P, KT, T], F32R)
        w_raw = [sb(f"w_raw{i}", [P, 8, P]) for i in range(2)]
        w_hi = [sb(f"w_hi{i}", [P, 8, P], F32R) for i in range(2)]
        w_lo = [sb(f"w_lo{i}", [P, 8, P], F32R) for i in range(2)]
        cst = sb("cst", [P, NCONST])
        par = sb("par", [P, DEPTH * NPAR])
        shift_in = sb("shift_in", [P, DEPTH, NSH])
        wkv_in = sb("wkv_in", [P, DEPTH, NPAIR, 64])
        pool_w = sb("pool_w", [P, DEPTH, 2, 64])
        pool_hs = sb("pool_hs", [P, DEPTH, 2, HIST])
        last_z = sb("last_z", [P, NSH, 2])
        eps = sb("eps", [P, 2])
        lora_all = sb("lora_all", [P, DR])
        g2_all = sb("g2_all", [P, DR])
        lora_st = sb("lora_st", [P, P])
        g2_st = sb("g2_st", [P, P])
        h_addr = top[0]
        hh = sb("hh", [P, FT, T], F32R)
        hl = sb("hl", [P, FT, T], F32R)
        sqs, _ = at("sqs", [P, KT, T], F32, h_addr)
        sg = sb("sg", [P, T])
        hf = sb("hf", [P, T])
        sq = [sb(f"sq{i}", [P, T]) for i in range(2)]
        rs = sb("rs", [P, T])
        ysum = sb("ysum", [P, T])
        assert top[0] <= nc.sbuf_usable_end
        top[0] = h_addr
        zs = sb("zs", [P, 18, T])
        lora = sb("lora", [P, T])
        lgate = sb("lgate", [P, T])
        mix_addr = top[0]
        ar = sb("ar", [P, 2, T])
        bt = sb("bt", [P, 2, T])
        kt = sb("kt", [P, 2, T])
        vc = sb("vc", [P, T])
        Lb = sb("Lb", [P, T])
        Pb = sb("Pb", [P, T + 8])
        Pi = sb("Pi", [P, T])
        aa = sb("aa", [P, T])
        kkb = sb("kkb", [P, T])
        tA = sb("tA", [P, T])
        tB = sb("tB", [P, T])
        tm = sb("tm", [P, 5, 3, P])
        rhs = sb("rhs", [P, 5, 2, 2, 64])
        um = sb("um", [P, 5, P])
        wt = sb("wt", [P, T])
        S = [sb(f"S{i}", [P, P]) for i in range(2)]
        Ss = [sb(f"Ss{i}", [P, P]) for i in range(2)]
        dS = sb("dS", [P, P])
        nv, rn = Lb, tA
        pd, psq = Lb, tA

        def mats(name):
            return sb(name, [P, 8, P]), sb(name + "s", [TS, 2, TS])

        mats_addr = top[0]
        n16, n64, a4t, xm = mats("n16"), mats("n64"), mats("a4t"), mats("xm")
        em = a4t
        dec = sb("dec", [P, NPAIR * (NCH + 1)])
        nt = sb("nt", [P, T])
        assert top[0] <= nc.sbuf_usable_end
        a = xl_addr + 2 * T * 4
        am, a = at("am", [P, 8, 3, P], F32, a)
        ams, a = at("ams", [TS, 2, 3, TS], F32, a)
        assert a <= xl_addr + KT * T * 4
        a = xh_addr + 2 * T * 4
        t4, a = at("t4", [P, 8, P], F32, a)
        t4s, a = at("t4s", [TS, 2, TS], F32, a)
        tt, a = at("tt", [P, 8, P], F32, a)
        tts, a = at("tts", [TS, 2, TS], F32, a)
        ys, a = at("ys", [TS, 2, P], F32, a)
        y0s, a = at("y0s", [TS, 2, P], F32, a)
        prs, a = at("prs", [P, T], F32, a)
        assert a <= xh_addr + KT * T * 4
        t4, tt = (t4, t4s), (tt, tts)
        top[0] = mix_addr
        zb = [sb(f"zb{i}", [P, T + 8]) for i in range(2)]
        zd = sb("zd", [P, T])
        UW = HIST + TP + HIST + TS
        ub = [sb(f"ub{i}", [P, UW + 2]) for i in range(2)]
        swA = sb("swA", [P, UW + 2])
        swB = sb("swB", [P, UW + 2])
        pooled = [sb(f"pooled{i}", [P, T]) for i in range(2)]
        top[0] = mats_addr
        mf = [sb(f"mf{i}", [P, T]) for i in range(2)]
        pool_bd = sb("pool_bd", [P, 2, P])

        ps = ctx.enter_context(nc.psum_tensor("ps", [P, 8, 512], F32))

        def pair_bank(i):
            return ps[:, i:i + 2, 0:HT]

        def halves(ap):
            return ap.rearrange("p (a b) -> p a b", a=2)

        def const(name, rows=P, cols=None):
            o, w = CCOL[name]
            return cst[0:rows, o:o + (cols or w)]

        def sem(name):
            return ctx.enter_context(nc.semaphore(name))

        loaded, layer_loaded, p_loaded = (sem(n) for n in ("loaded", "layer_loaded", "p_loaded"))
        x_loaded = [sem(f"x_loaded{m}") for m in range(KT)]
        pool_stored, shift_stored, wkv_stored, y_stored = (sem(n) for n in ("pool_stored", "shift_stored", "wkv_stored", "y_stored"))
        w_loaded = [sem(f"w_loaded{i}") for i in range(2)]
        w_hi_done, w_split, slot_used = sem("w_hi_done"), sem("w_split"), sem("slot_used")
        tile_out = [sem(f"tile_out{i}") for i in range(2)]
        xh_ready, xl_ready, hh_ready, hl_ready = sem("xh_ready"), sem("xl_ready"), sem("hh_ready"), sem("hl_ready")
        ph_ready, pl_ready = sem("ph_ready"), sem("pl_ready")
        set_done, y_ready, sum_ready, mean_mm, d_ready = (sem(n) for n in ("set_done", "y_ready", "sum_ready", "mean_mm", "d_ready"))
        sq_sum = sem("sq_sum")
        sq_ready, var_mm, rs_ready, t_ready, ax_ready = (
            sem(n) for n in ("sq_ready", "var_mm", "rs_ready", "t_ready", "ax_ready"))
        bd_zero = sem("bd_zero")
        z_set, zd_ready, last_ready, zs_ready, lora_act, u_part = (
            sem(n) for n in ("z_set", "zd_ready", "last_ready", "zs_ready", "lora_act", "u_part"))
        pool_step, pool_mm, mf_ready = sem("pool_step"), sem("pool_mm"), sem("mf_ready")
        staged, wa_mm, sig_ready, scan_ready, decay_ready, kf_ready = (
            sem(n) for n in ("staged", "wa_mm", "sig_ready", "scan_ready", "decay_ready", "kf_ready"))
        kk_ready, kksq_ready, kkn_mm, kkn_max, rn_ready, kkb_ready, kp_ready = (
            sem(n) for n in ("kk_ready", "kksq_ready", "kkn_mm", "kkn_max", "rn_ready", "kkb_ready", "kp_ready"))
        ar_ready, bk_ready, vc_ready, rp_ready, rkk_ready, rk_mm, bonus_ready = (
            sem(n) for n in ("ar_ready", "bk_ready", "vc_ready", "rp_ready", "rkk_ready", "rk_mm", "bonus_ready"))
        tm_mm, tm_part, tm_ready, am_mm, am_part, am_ready = (
            sem(n) for n in ("tm_mm", "tm_part", "tm_ready", "am_mm", "am_part", "am_ready"))
        t_mm = [sem(f"t_mm{g}") for g in range(3)]
        t_part = [sem(f"t_part{g}") for g in range(3)]
        t_out = [sem(f"t_out{g}") for g in range(3)]
        n_ready = [sem(f"n_ready{g}") for g in range(3)]
        half_mm = [sem(f"half_mm{g}") for g in range(2)]
        half_out = [sem(f"half_out{g}") for g in range(2)]
        u_mm, um_ready, s_mm, ds_ready, s_ready, y_mm, yw_ready = (
            sem(n) for n in ("u_mm", "um_ready", "s_mm", "ds_ready", "s_ready", "y_mm", "yw_ready"))
        ss_part, ss_init, ss_done = sem("ss_part"), sem("ss_init"), sem("ss_done")
        g_staged, pm_mm, pg_mm, pd_ready, psq_ready, pv_mm, prs_ready = (
            sem(n) for n in ("g_staged", "pm_mm", "pg_mm", "pd_ready", "psq_ready", "pv_mm", "prs_ready"))
        pt_ready, pi_ready, pb_ready, g_ready, po_ready, fin_ready = (
            sem(n) for n in ("pt_ready", "pi_ready", "pb_ready", "g_ready", "po_ready", "fin_ready"))
        ln_newton, kk_newton, hn_newton = sem("ln_newton"), sem("kk_newton"), sem("hn_newton")
        NLOAD = 6

        def flat(ap):
            return ap.rearrange("p a t -> p (a t)")

        def row(t, i):
            return flat(t[:, bass.ds(i, 1), :])

        def col(l, c):
            return par[:, bass.ds(l * NPAR + c, 1)]

        def out_count(l, name, m):
            return l * (TILES // 2) + TILE0[name] // 2 + m + 1

        def used_count(l, name, i):
            return l * SLOTS + SLOT0[name] + i + 3

        SPLIT = [range(4, 8), range(3, 7), ()]

        def step_bank(g, part):
            return 1 - g if part == 1 else g

        def half_count(s, g, n):
            return n * 4 + (s - SPLIT[g][0] + 1)

        def group_view(g, wide, bank=None):
            n, U = (P, 4) if g < 2 else (TS, 2)
            return ps[0:n, g if bank is None else bank, 0:U * P].rearrange("p (u c) -> p u c", u=U)[:, :, 0:wide]

        def a_view(g):
            n, tiles = (P, 2) if g < 2 else (TS, 1)
            return ps[0:n, 3:5, 0:tiles * P].rearrange("p h (j c) -> p h j c", j=tiles)[:, :, :, 0:n]

        def a_units(m, g):
            return units(m, g).rearrange("p (j h) c -> p h j c", h=2)

        def a_spread(name, g):
            n, tiles = (P, 2) if g < 2 else (TS, 1)
            return const(name, n, n).unsqueeze(1).unsqueeze(1).to_broadcast([n, 2, tiles, n])

        def units(m, g):
            return m[0][:, 4 * g:4 * g + 4, :] if g < 2 else m[1][:, :, :]

        def spread(name, g):
            n, U = (P, 4) if g < 2 else (TS, 2)
            return const(name, n, n).unsqueeze(1).to_broadcast([n, U, n])

        block = ctx.enter_context(nc.Block())

        SLOTS_A, SLOTS_B = 13, 14
        Z_POOLED, Z_LAST = 5, 5
        Z_PIECES = {5: (0,), 6: (1,), 7: (2, 3), 8: (4, 5), 9: range(6, SLOTS_A)}

        def heads(eng, l, half_a, half_b, normalise):
            half_a(l, 0, True, False, True)
            half_b(l, 0, True, False)
            with eng.Fori(0, NPAIR - 2) as q:
                half_a(l, q + 1, True, True, True)
                half_b(l, q + 1, True, True)
            half_a(l, NPAIR - 1, True, True, False)
            half_b(l, NPAIR - 1, False, True)
            half_a(l, NPAIR, False, True, False)
            for k in range(SLOTS_B):
                normalise(l, NPAIR - 1, k, False)

        @block.sync
        def _(sp):
            arrays = {"f1i": w1i, "f1o": w1o, "z": wz, "wo": wo, "f2i": w2i, "f2o": w2o}
            with sp.Fori(0, DEPTH) as l:
                sp.wait_ge(xl_ready, l * 40)
                sp.dma_start(lora_all[:, :], flat(lora_w[bass.ds(l, 1)].rearrange("a p n -> p a n"))).then_inc(layer_loaded, 16)
                sp.dma_start(g2_all[:, :], flat(g2_w[bass.ds(l, 1)].rearrange("a p n -> p a n"))).then_inc(layer_loaded, 16)
                for name, bodies, ks in PHASES:
                    B = len(ks)
                    if name == "wo":
                        with sp.Fori(0, NPAIR - 1) as p:
                            n = l * NPAIR + p
                            due, due_sample = sp.to_reg(n * 8 + 8), sp.to_reg(n + 1)
                            sp.wait_ge(s_ready, due)
                            sp.wait_ge(ss_done, due_sample)
                            for q, st in enumerate((S[0], Ss[1])):
                                for h in range(2):
                                    hs = slice(64 * h, 64 * h + 64)
                                    sp.dma_start(wkv_out[bass.ds(n, 1), q, hs, :].rearrange("a p v -> p (a v)"), st[hs, hs]).then_inc(wkv_stored, 16)
                    if name == "f2o":
                        sp.wait_ge(var_mm, l * 12 + 8)
                        for k in range(2):
                            sp.dma_start(sq[k][:, :], flat(pT[bass.ds(l, 1), :, k, :].rearrange("a p t -> p a t"))).then_inc(p_loaded, 16)
                    with sp.Fori(0, bodies) as m:
                        for i, nk in enumerate(ks):
                            if name == "gp":
                                tile = bass.ds(l * 8 + m * 2 + i // 3, 1)
                                src = wp[tile] if i % 3 == 2 else wg[tile, :, i % 3 * 4:i % 3 * 4 + 4, :]
                            elif name in ("f1o", "f2o"):
                                k0 = (0, 8, 15)[i % 3]
                                src = arrays[name][bass.ds(l * 8 + m * 2 + i // 3, 1), :, k0:k0 + nk, :]
                            else:
                                src = arrays[name][bass.ds(l * (bodies * B) + m * B + i, 1)]
                            sp.wait_ge(w_split, l * SLOTS + SLOT0[name] + m * B + i + 1)
                            sp.dma_start(w_raw[i % 2][:, 0:nk, :], src.rearrange("a p k n -> p (a k) n")).then_inc(w_loaded[i % 2], 16)
            for m in range(KT):
                sp.wait_ge(fin_ready, m + 1)
                sp.dma_start(y_out[:, m, :], y[:, m, :]).then_inc(y_stored, 16)
            sp.wait_ge(y_stored, 16 * KT)
            sp.wait_ge(pool_stored, DEPTH * 64)
            sp.wait_ge(shift_stored, DEPTH * 16)
            sp.wait_ge(wkv_stored, DEPTH * NPAIR * 64)

        @block.gpsimd
        def _(pool):
            pool.sem_inc(w_split, 2)

            def norm(inst):
                for m in range(KT // 2):
                    pool.wait_ge(sq_ready, inst * 8 + 2 * m + 2)
                    pool.tensor_tensor(sqs[:, 2 * m, :], sqs[:, 2 * m, :], sqs[:, 2 * m + 1, :], ALU.add).then_inc(sq_sum, 1)

            def prepare_1(l, p, k, first):
                n = l * NPAIR + p
                if k == 3:
                    pool.wait_ge(kf_ready, n + 1)
                    pool.tensor_tensor(tB[:, :], row(zs, p + 6), tB[:, :], ALU.mult).then_inc(kp_ready, 1)
                if k == 5:
                    pool.wait_ge(rn_ready, n + 1)
                    pool.tensor_tensor(nt[:, :], nv[:, :], rn[:, :], ALU.mult).then_inc(kk_newton, 1)
                    pool.wait_ge(kk_newton, n * 4 + 1)
                    pool.tensor_tensor(nt[:, :], nt[:, :], rn[:, :], ALU.mult).then_inc(kk_newton, 1)
                    due = pool.to_reg(n * 4 + 2)
                    pool.wait_ge(w_split, 2)
                    pool.wait_ge(kk_newton, due)
                    pool.tensor_scalar(nt[:, :], nt[:, :], -0.5, 1.5, ALU.mult, ALU.add).then_inc(kk_newton, 1)
                    pool.wait_ge(kk_newton, n * 4 + 3)
                    pool.tensor_tensor(rn[:, :], nt[:, :], rn[:, :], ALU.mult).then_inc(kk_newton, 1)
                    pool.wait_ge(kk_newton, n * 4 + 4)
                    pool.tensor_tensor(kkb[:, :], rn[:, :], kkb[:, :], ALU.mult).then_inc(kkb_ready, 1)

            def prepare_2(l, p, k, first):
                n = l * NPAIR + p
                if k == 8:
                    pool.wait_ge(kp_ready, n + 1)
                    if not first:
                        pool.wait_ge(ar_ready, n * 3 + 1)
                    for h in range(2):
                        hs = slice(64 * h, 64 * h + 64)
                        pool.tensor_tensor(kt[hs, h, :], tB[hs, :], Pi[hs, :], ALU.mult).then_inc(bk_ready, 1)
                        pool.wait_ge(bk_ready, n * 5 + h + 1)
                    pool.wait_ge(kkb_ready, n + 1)
                    pool.tensor_tensor(nt[:, :], kkb[:, :], aa[:, :], ALU.mult).then_inc(bk_ready, 1)
                    pool.wait_ge(bk_ready, n * 5 + 3)
                    if first:
                        pool.wait_ge(ar_ready, n * 3 + 1)
                    for h in range(2):
                        hs = slice(64 * h, 64 * h + 64)
                        pool.tensor_tensor(bt[hs, h, :], nt[hs, :], Pi[hs, :], ALU.mult).then_inc(bk_ready, 1)
                        due = pool.to_reg(n * 5 + h + 4)
                        pool.wait_ge(w_split, 2)
                        pool.wait_ge(bk_ready, due)

            def normalise(l, p, k, after_bonus):
                if k == 4:
                    pool.wait_ge(hn_newton, (l * NPAIR + p) * 3 + 3)
                    pool.tensor_tensor(pd[:, :], pd[:, :], prs[:, :], ALU.mult).then_inc(pt_ready, 1)
                if k == 6:
                    pool.wait_ge(pi_ready, l * NPAIR + p + 1)
                    pool.tensor_tensor(psq[:, :], psq[:, :], row(zs, p + 6), ALU.add).then_inc(pb_ready, 1)
                    pool.wait_ge(pb_ready, l * NPAIR + p + 1)
                    pool.wait_ge(g_ready, l * NPAIR + p + 1)
                    pool.tensor_tensor(row(zs, p), psq[:, :], nt[:, :], ALU.mult).then_inc(po_ready, 1)

            def half_a(l, p, left, right, nxt):
                for k in range(SLOTS_A):
                    if nxt:
                        prepare_1(l, p + 1, k, False)

            def half_b(l, p, nxt, norm_before):
                for k in range(SLOTS_B):
                    if norm_before:
                        normalise(l, p - 1, k, nxt)
                    if nxt:
                        prepare_2(l, p + 1, k, False)

            with pool.Fori(0, DEPTH) as l:
                for name, bodies, ks in PHASES:
                    B = len(ks)
                    if name == "wo":
                        for k in range(SLOTS_B):
                            prepare_2(l, 0, k, True)
                        heads(pool, l, half_a, half_b, normalise)

                    def split(m):
                        for i, nk in enumerate(ks):
                            n, k = l * SLOTS + SLOT0[name] + m * B + i, i % 2
                            pool.wait_ge(w_loaded[k], (l * (SLOTS // 2) + m * (B // 2) + (SLOT0[name] // 2 + i // 2 + 1)) * 16)
                            due = pool.to_reg(n + 1)
                            pool.wait_ge(w_split, 2)
                            pool.wait_ge(slot_used, due)
                            pool.tensor_scalar(w_hi[k][:, 0:nk, :], w_raw[k][:, 0:nk, :], 1.0, 0.0, ALU.mult, ALU.add).then_inc(w_hi_done, 1)
                            pool.wait_ge(w_hi_done, n + 1)
                            pool.tensor_tensor(w_lo[k][:, 0:nk, :], w_raw[k][:, 0:nk, :], w_hi[k][:, 0:nk, :].bitcast(F32),
                                               ALU.subtract).then_inc(w_split, 1)

                    last = Z_LAST if name == "z" else bodies
                    if name in ("z", "f2i"):
                        norm(l * 3 + (name == "f2i"))
                    with pool.Fori(0, last) as m:
                        split(m)
                    for m in range(last, bodies):
                        split(m)
                        for q in Z_PIECES.get(m - 1, ()):
                            prepare_1(l, 0, q, True)
                norm(l * 3 + 2)

        @block.tensor
        def _(pe):
            pe.sem_inc(slot_used, 2)
            pe.sem_inc(y_mm, 5)

            def constants_there():
                pe.wait_ge(loaded, 16 * NLOAD)

            def dense(l, name, hi, lo, ready, base, start=0, end=None):
                _, bodies, ks = next(p for p in PHASES if p[0] == name)
                B = len(ks)
                per = B // 2

                def body(m, first):
                    for i, nk in enumerate(ks):
                        k, pair, part, tile = i % 2, i // per, i % per, m
                        if name == "gp":
                            pair, part, tile = i % 3 // 2, i % 3 % 2, m * 2 + i // 3
                        n = l * SLOTS + SLOT0[name] + m * B + i
                        if part == 0:
                            pe.wait_ge(tile_out[pair], out_count(l, name, tile) - 1)
                        if name == "gp" and i == 2 and first:
                            pe.wait_ge(pl_ready, l * 2 + 2)
                        pe.wait_ge(w_split, n + 3)
                        embedding = name == "gp" and pair == 1
                        x_hi, x_lo = (hh, hl) if embedding else (hi, lo)
                        k0 = (0, 4)[part] if name == "gp" else (0, 8, 15)[part]
                        last_part = part == (1 if name == "gp" else per - 1) or embedding
                        for j in range(nk):
                            if first and pair == 0 and i < per:
                                pe.wait_ge(ready, base + k0 + j + 1)
                            for q, (w, x) in enumerate(((w_hi[k], x_hi), (w_hi[k], x_lo), (w_lo[k], x_hi))):
                                for h in range(2):
                                    mm = pe.matmul(ps[:, 2 * pair + h, 0:HT], w[:, j, :], x[:, k0 + j, h * HT:(h + 1) * HT],
                                                   start=(part == 0 and j == 0 and q == 0),
                                                   stop=(last_part and j == nk - 1 and q == 2))
                        mm.then_inc(slot_used, 1)

                if start == 0:
                    body(0, True)
                if end == start + 1:
                    body(start, False)
                else:
                    with pe.Fori(max(start, 1), end or bodies) as m:
                        body(m, False)

            def two(bank, lhsT, r, start=True, stop=True):
                for h in range(2):
                    mm = pe.matmul(ps[:, bank + h, 0:HT], lhsT, r[:, h * HT:(h + 1) * HT], start=start, stop=stop)
                return mm

            def norm(inst):
                constants_there()
                pe.wait_ge(sum_ready, inst * 9 + 9)
                two(4, const("mean_d"), ysum).then_inc(mean_mm, 1)
                for m in range(KT // 2):
                    pe.wait_ge(sq_sum, inst * 4 + m + 1)
                    two(6, const("mean_d"), sqs[:, 2 * m, :], m == 0, m == KT // 2 - 1).then_inc(var_mm, 1)

            def step_waits(name, s, g, n):
                due, blocks = pe.to_reg(n * NSTEP + s), pe.to_reg(n * 2 + 2)
                if g == 2:
                    constants_there()
                if name == "A":
                    if g == 2:
                        pe.wait_ge(n_ready[1], blocks)
                    else:
                        pe.wait_ge(am_ready, n * 10 + (4, 10)[g])
                if name == "E16":
                    pe.wait_ge(n_ready[g], blocks)
                if s - 1 in SPLIT[g] and s in SPLIT[g]:
                    pe.wait_ge(half_out[g], half_count(s - 1, g, n))
                else:
                    pe.wait_ge(t_out[g], due)

            def step(s, g, n, part=None):
                name, tiles, rows = STEPS[s], GROUPS[g], (P if g < 2 else TS)
                if part == 1:
                    pe.wait_ge(t_out[g], n * NSTEP + s)
                else:
                    step_waits(name, s, g, n)
                if name == "WT":
                    for q, j in enumerate(tiles):
                        src = xm[0][:, 2 * j, :] if g < 2 else ys[:, 0, :]
                        mm = pe.transpose(ps[:, g, q * P:q * P + rows], src, const("ident", rows, rows))
                    mm.then_inc(t_mm[g], 1)
                    return
                for q, (j, h) in enumerate((j, h) for j in tiles for h in range(2)):
                    if part is not None and q // 2 != part:
                        continue
                    u, hs, ts = 2 * j + h, slice(64 * h, 64 * h + 64), slice(j * P, j * P + rows)

                    def mat(m):
                        return m[0][:, u, :] if g < 2 else m[1][:, h, :]

                    b, o = (3 + h, q // 2 * P) if name == "A" else (step_bank(g, part), q * P)
                    out = ps[0:rows, b, o:o + (P if name[0] == "Y" else 64 if name == "G" else rows)]
                    if name in ("T4T", "T16T"):
                        mm = pe.transpose(out, mat(t4 if name == "T4T" else xm), const("ident", rows, rows))
                        continue
                    y0v = t4[0][:, u, :] if g < 2 else y0s[:, h, :]
                    yv = xm[0][:, u, :] if g < 2 else ys[:, h, :]
                    lhsT, r = {
                        "A": (ar[:, 0, ts], bt[:, h, ts]), "H1": (mat(a4t), mat(xm)), "H2": (mat(a4t), mat(xm)),
                        "E16": (mat(n16), mat(tt)), "X1": (mat(em), mat(t4)), "X2": (mat(em), mat(xm)),
                        "X3": (mat(em), mat(xm)), "E64": (mat(n64), mat(tt)),
                        "G": (am[:, u, 1, :] if g < 2 else ams[:, h, 1, :], tm[0:rows, j, 2, hs]),
                        "Y0": (mat(tt), rhs[0:rows, j, h, :, :].rearrange("p a b -> p (a b)")),
                        "Y1": (mat(em), y0v), "Y2": (mat(em), yv), "Y3": (mat(em), yv),
                    }[name]
                    mm = pe.matmul(out, lhsT, r, start=True, stop=True)
                mm.then_inc(half_mm[g] if part == 0 else t_mm[g], 1)

            def chunk_in(c, l, p):
                n = l * NPAIR + p
                j, ro, rows = (c // 2, 64 * (c % 2), CH) if c < NCH else (4, 0, TS)
                st = S[c % 2] if c < NCH else Ss[0]
                ts = slice(c * CH, c * CH + rows)
                if c == 0:
                    return
                if c in (1, 4, 8):
                    pe.wait_ge(t_out[(1, 4, 8).index(c)], n * NSTEP + NSTEP)
                if c < NCH:
                    pe.wait_ge(s_ready, n * 8 + c)
                else:
                    pe.wait_ge(ss_init, n + 1)
                pe.matmul(ps[ro:ro + rows, 5, 0:P], wt[:, ts], st[:, :], start=True, stop=True).then_inc(u_mm, 1)
                first = c in (1, 2, 4, 6, 8)
                if first:
                    pe.wait_ge(yw_ready, n * 5 + j)
                    pe.wait_ge(rp_ready, n + 1)
                pe.matmul(ps[:, 7, ro:ro + rows], st[:, :], flat(zs[:, bass.ds(p, 1), ts]), start=first, stop=True, skip_group_check=True)

            def chunk_out(c, l, p):
                n = l * NPAIR + p
                j, ro, rows = (c // 2, 64 * (c % 2), CH) if c < NCH else (4, 0, TS)
                pe.wait_ge(um_ready, n * 9 + c + 1)
                pe.matmul(ps[:, 6, 0:P], tm[ro:ro + rows, j, 0, :], um[ro:ro + rows, j, :], start=True, stop=False)
                pe.matmul(ps[:, 6, 0:P], tm[ro:ro + rows, j, 1, :], tm[ro:ro + rows, j, 2, :], start=False, stop=True).then_inc(s_mm, 1)

            def chunk_y(c, l, p):
                j = c // 2
                if c % 2 == 1 or c == NCH:
                    m = P if j < 4 else TS
                    for h in range(2):
                        hs = slice(64 * h, 64 * h + 64)
                        for src, q in ((um[0:m, j, hs], 0), (tm[0:m, j, 2, hs], 2)):
                            mm = pe.matmul(ps[hs, 7, 0:m], src, am[:, 2 * j + h, q, :] if j < 4 else ams[:, h, q, :],
                                           start=False, stop=True, skip_group_check=True)
                    mm.then_inc(y_mm, 1)

            def token_major(j, n, used):
                rows = P if j < 4 else TS
                for who, count in used:
                    pe.wait_ge(who, count)
                ts, b = slice(j * P, j * P + rows), 3 + j % 2
                pe.transpose(ps[0:rows, b, 0:P], ar[:, 0, ts], const("ident"))
                for q, src in ((1, bt), (2, kt)):
                    for h in range(2):
                        at_col = q * P + 64 * h
                        pe.transpose(ps[0:rows, b, at_col:at_col + P], src[:, h, ts], const(("ident", "swap")[h]))
                mm = pe.transpose(ps[0:rows, b, 3 * P:4 * P], vc[:, ts], const("ident"))
                mm.then_inc(tm_mm, 1)

            def products(u, n):
                j, h = u // 2, u % 2
                rows = P if j < 4 else TS
                if u in (0, 4):
                    pe.wait_ge(tm_ready, n * 5 + (2 if u == 0 else 5))
                elif u not in (1, 5):
                    due = pe.to_reg(n * 10 + u - 1)
                    if j == 4:
                        constants_there()
                    pe.wait_ge(am_ready, due)
                for q, src in enumerate((bt, kt)):
                    mm = pe.matmul(ps[0:rows, 3 + u % 2, 2 * q * rows:2 * (q + 1) * rows].rearrange("p (a t) -> p a t", a=2),
                                   src[:, h, j * P:j * P + rows], ar[:, :, j * P:j * P + rows], start=(q == 0), stop=True,
                                   skip_group_check=True)
                mm.then_inc(am_mm, 1)

            def prepare_1(l, p, k, first):
                n = l * NPAIR + p
                if k == 1:
                    pe.wait_ge(bonus_ready, n)
                    if not first:
                        pe.wait_ge(s_ready, n * 8 - 12)
                    pe.wait_ge(staged, n + 1)
                    two(5, lora_st[0:64, :], lora[0:64, :]).then_inc(wa_mm, 1)
                if k == 2:
                    pe.wait_ge(sig_ready, n * 2 + 1)
                    two(5, lora_st[64:128, :], lora[64:128, :]).then_inc(wa_mm, 1)
                if k == 4:
                    pe.wait_ge(sig_ready, n * 2 + 2)
                    pe.wait_ge(kksq_ready, n + 1)
                    two(5, const("head_sum"), tA).then_inc(kkn_mm, 1)

            def prepare_2(l, p, k, first):
                n = l * NPAIR + p
                if k == 0:
                    if not first:
                        pe.wait_ge(ss_done, n - 1)
                    pe.wait_ge(rkk_ready, n + 1)
                    two(5, const("head_sum"), tA).then_inc(rk_mm, 1)

            def normalise(l, p, k, after_bonus):
                n = l * NPAIR + p
                if k == 1:
                    pe.wait_ge(ss_done, n + 1)
                    if after_bonus:
                        pe.wait_ge(bonus_ready, n + 3)
                    pe.wait_ge(yw_ready, n * 5 + 5)
                    for h in range(2):
                        mm = pe.matmul(ps[:, 5 + h, 0:HT], const("head_mean"), flat(zs[:, bass.ds(p, 1), h * HT:(h + 1) * HT]),
                                       start=True, stop=True)
                    mm.then_inc(pm_mm, 1)
                if k == 3:
                    pe.wait_ge(psq_ready, n + 1)
                    two(5, const("head_mean"), psq).then_inc(pv_mm, 1)
                if k == 5:
                    pe.wait_ge(hn_newton, n * 3 + 1)
                    pe.wait_ge(g_staged, n + 1)
                    two(5, g2_st[:, :], lgate).then_inc(pg_mm, 1)

            def half_a(l, p, left, right, nxt):
                n = l * NPAIR + p
                for k in range(SLOTS_A):
                    if right and k < 8:
                        step(8 + k, 1, n - 1)
                        step(8 + k, 2, n - 1)
                    if right and k == 8 and nxt:
                        pe.wait_ge(kkn_max, n + 2)
                    if right and k >= 8:
                        chunk_in(k - 4, l, p - 1)
                    if left and k < 2:
                        used = []
                        if k == 0:
                            used = [(ar_ready, n * 3 + 3), (bk_ready, n * 5 + 5), (vc_ready, n + 1), (n_ready[2], n * 2)]
                        token_major(k, n, used)
                    elif left and k < 4:
                        products(2 * k - 4, n)
                        products(2 * k - 3, n)
                    elif left and k < 8:
                        step(k - 4, 0, n)
                    elif left and k < 12:
                        step(k - 4, 0, n, 0)
                    if right and k >= 8:
                        chunk_out(k - 4, l, p - 1)
                    if left and 8 <= k < 12:
                        step(k - 4, 0, n, 1)
                    if right and k >= 8:
                        chunk_y(k - 4, l, p - 1)
                    if nxt:
                        prepare_1(l, p + 1, k, not right)

            def half_b(l, p, nxt, norm_before):
                n = l * NPAIR + p
                for k in range(SLOTS_B):
                    if k < 8:
                        step(8 + k, 0, n)
                    elif k < 12:
                        if k == 8:
                            pe.wait_ge(g_ready, n)
                            if nxt:
                                pe.wait_ge(bonus_ready, n + 2)
                            pe.wait_ge(t_out[0], n * NSTEP + NSTEP)
                        chunk_in(k - 8, l, p)
                    if k == 0:
                        token_major(2, n, [(n_ready[0], n * 2 + 2)])
                    elif k == 1:
                        token_major(3, n, [])
                        token_major(4, n, [(tm_ready, n * 5 + 3)])
                    elif k < 5:
                        products(2 * k, n)
                        products(2 * k + 1, n)
                    if 5 <= k < 8 or k == 12:
                        step(k - 5, 1, n)
                    if 8 <= k < 12:
                        step(k - 5, 1, n, 0)
                        chunk_out(k - 8, l, p)
                        step(k - 5, 1, n, 1)
                        chunk_y(k - 8, l, p)
                    if 6 <= k:
                        step(k - 6, 2, n)
                    if nxt:
                        prepare_2(l, p + 1, k, False)
                    if norm_before:
                        normalise(l, p - 1, k, nxt)

            with pe.Fori(0, DEPTH) as l:
                dense(l, "f1i", xh, xl, xl_ready, l * 40)
                dense(l, "f1o", hh, hl, hl_ready, l * (2 * FT))
                norm(l * 3)
                dense(l, "z", xh, xl, xl_ready, l * 40 + 8, end=Z_POOLED)
                for q in range(2):
                    pe.wait_ge(pool_step, l * 16 + (7, 16)[q])
                    two(4 + 2 * q, pool_bd[:, q, :], pooled[q]).then_inc(pool_mm, 1)
                for m in range(Z_POOLED, NZ // 2):
                    dense(l, "z", xh, xl, xl_ready, l * 40 + 8, start=m, end=m + 1)
                    if m == Z_LAST:
                        pe.wait_ge(mf_ready, l * 2 + 2)
                    for k in Z_PIECES.get(m, ()):
                        prepare_1(l, 0, k, True)
                for k in range(SLOTS_B):
                    prepare_2(l, 0, k, True)
                heads(pe, l, half_a, half_b, normalise)
                dense(l, "wo", xh, xl, xl_ready, l * 40 + 16)
                norm(l * 3 + 1)
                dense(l, "f2i", xh, xl, xl_ready, l * 40 + 24)
                dense(l, "f2o", hh, hl, hl_ready, l * (2 * FT) + FT)
                dense(l, "gp", xh, xl, xl_ready, l * 40 + 32)
                norm(l * 3 + 2)

        @block.scalar
        def _(act):
            for m in range(KT):
                act.dma_start(y[:, m, :], xT[:, m, :]).then_inc(x_loaded[m], 16)
            for m in range(KT):
                act.wait_ge(x_loaded[m], 16)
                act.activation(xh[:, m, :], y[:, m, :], ACT.Copy).then_inc(xh_ready, 1)
            for dst, src in ((cst[:, :], consts), (par[:, :], params), (shift_in[:, :, :], shift_hist),
                             (wkv_in[:, :, :, :], wkv_hist), (pool_w[:, :, :, :], poolw), (pool_hs[:, :, :, :], pool_hist)):
                act.dma_start(dst, src).then_inc(loaded, 16)
            for m in range(KT):
                act.wait_ge(xl_ready, m + 1)
                act.activation(y[:, m, :], y[:, m, :], ACT.Copy, scale=ALPHA).then_inc(ax_ready, 1)
            act.wait_ge(set_done, 2)
            act.wait_ge(loaded, 16 * NLOAD)

            def ffn(l, which, name):
                with act.Fori(0, FT) as m:
                    act.wait_ge(slot_used, used_count(l, name, 2 * m))
                    act.wait_ge(tile_out[1], out_count(l, name, m) - 1)
                    act.activation(halves(sg[:, :]), pair_bank(0), ACT.Silu).then_inc(tile_out[0], 1)
                    act.wait_ge(tile_out[1], out_count(l, name, m))
                    act.activation(row(hh, m), hf[:, :], ACT.Copy).then_inc(hh_ready, 1)

            def norm(l, which, b, ab, count):
                inst = l * 3 + which
                for m in range(KT):
                    act.wait_ge(d_ready, inst * 8 + m + 1)
                    act.activation(sqs[:, m, :], y[:, m, :], ACT.Square).then_inc(sq_ready, 1)
                act.wait_ge(var_mm, inst * 4 + 4)
                act.activation(halves(rs[:, :]), pair_bank(6), ACT.Abs_reciprocal_sqrt, bias=eps[:, 0:1]).then_inc(rs_ready, 1)
                for m in range(KT):
                    act.wait_ge(t_ready, inst * 8 + m + 1)
                    act.activation(xh[:, m, :], y[:, m, :], ACT.Identity, bias=col(l, b + m)).then_inc(xh_ready, 1)
                for m in range(KT):
                    act.wait_ge(xl_ready, count + m + 1)
                    act.activation(y[:, m, :], y[:, m, :], ACT.Identity, scale=ALPHA, bias=col(l, ab + m)).then_inc(ax_ready, 1)

            def z_copy(l, m, k, i):
                act.wait_ge(slot_used, used_count(l, "z", 2 * m + k))
                act.wait_ge(zs_ready, l * NSH + i + 1)
                act.activation(halves(zb[k][:, 1:T + 1]), pair_bank(2 * k), ACT.Copy).then_inc(tile_out[k], 1)

            def prepare_1(l, p, k, first):
                n = l * NPAIR + p
                if k == 1:
                    if first:
                        act.wait_ge(staged, n + 1)
                    act.wait_ge(ar_ready, n * 3)
                    act.wait_ge(bk_ready, n * 5)
                    if not first:
                        act.wait_ge(po_ready, n - 2)
                    act.wait_ge(rk_mm, n)
                    act.activation(kkb[:, :], row(zs, p + 6), ACT.Identity, scale=col(l, p + COL["k_k"])).then_inc(kk_ready, 1)
                    act.wait_ge(kk_ready, n + 1)
                    act.activation(tA[:, :], kkb[:, :], ACT.Square).then_inc(kksq_ready, 1)
                if k == 1:
                    act.wait_ge(wa_mm, n * 2 + 1)
                    act.activation(halves(tB[:, :]), pair_bank(5), ACT.Sigmoid, bias=col(l, p + COL["w0"])).then_inc(sig_ready, 1)
                if k == 2:
                    act.wait_ge(wa_mm, n * 2 + 2)
                    act.activation(halves(aa[:, :]), pair_bank(5), ACT.Sigmoid, bias=col(l, p + COL["a0"])).then_inc(sig_ready, 1)
                if k == 3:
                    act.wait_ge(scan_ready, n + 1)
                    act.activation(Pb[:, 1:T + 1], Lb[:, :], ACT.Exp, scale=-DECAY).then_inc(decay_ready, 1)
                    act.activation(Pi[:, :], Lb[:, :], ACT.Exp, scale=DECAY).then_inc(decay_ready, 1)
                    act.activation(dec[:, bass.ds(p * (NCH + 1), NCH)], Lb[:, CH - 1:TP:CH], ACT.Exp, scale=-DECAY).then_inc(decay_ready, 1)
                    act.activation(dec[:, bass.ds(p * (NCH + 1) + NCH, 1)], Lb[:, T - 1:T], ACT.Exp, scale=-DECAY).then_inc(decay_ready, 1)
                    act.wait_ge(sig_ready, n * 2 + 2)
                    act.activation(tB[:, :], aa[:, :], ACT.Identity, scale=col(l, p + COL["k_a"]), bias=col(l, p + COL["one_ka"])).then_inc(kf_ready, 1)
                if k == 5:
                    act.wait_ge(kkn_max, n + 1)
                    act.activation(rn[:, :], nv[:, :], ACT.Abs_reciprocal_sqrt).then_inc(rn_ready, 1)

            def prepare_2(l, p, k, first):
                n = l * NPAIR + p
                if k == 6:
                    act.activation(vc[:, :], row(zs, p + 12), ACT.Copy).then_inc(vc_ready, 1)
                if k == 9:
                    act.wait_ge(rkk_ready, n + 1)
                    act.wait_ge(ar_ready, n * 3 + 1)
                    act.activation(row(zs, p), ar[:, 1, :], ACT.Copy).then_inc(rp_ready, 1)

            def normalise(l, p, k, after_bonus):
                n = l * NPAIR + p
                if k == 2:
                    act.wait_ge(po_ready, n)
                    act.wait_ge(pd_ready, n + 1)
                    act.activation(psq[:, :], pd[:, :], ACT.Square).then_inc(psq_ready, 1)
                if k == 3:
                    act.wait_ge(pv_mm, n + 1)
                    act.activation(halves(prs[:, :]), pair_bank(5), ACT.Abs_reciprocal_sqrt, bias=eps[:, 1:2]).then_inc(prs_ready, 1)
                if k == 5:
                    act.wait_ge(pt_ready, n + 1)
                    act.activation(psq[:, :], pd[:, :], ACT.Identity, scale=col(l, p + COL["lnx_g"]), bias=col(l, p + COL["lnx_b"])).then_inc(pi_ready, 1)
                if k == 6:
                    act.wait_ge(pg_mm, n + 1)
                    act.activation(halves(nt[:, :]), pair_bank(5), ACT.Copy).then_inc(g_ready, 1)

            def token_major(j, n):
                rows, b = (P if j < 4 else TS), 3 + j % 2
                act.wait_ge(tm_mm, n * 5 + j + 1)
                act.activation(rhs[0:rows, j, :, 0, :], ps[0:rows, b, 0:P].rearrange("p (h c) -> p h c", h=2), ACT.Copy).then_inc(tm_part, 1)
                act.activation(tm[0:rows, j, :, :].rearrange("p a b -> p (a b)"), ps[0:rows, b, P:4 * P], ACT.Copy).then_inc(tm_ready, 1)

            def step(s, g, n, part=None):
                if s in SPLIT[g] and part is None:
                    step(s, g, n, 0)
                    step(s, g, n, 1)
                    return
                name, tiles = STEPS[s], GROUPS[g]
                if name not in ("T4T", "T16T", "E16", "E64", "G", "Y0", "WT"):
                    return
                rows, nt_ = (P if g < 2 else TS), len(tiles)
                if part == 0:
                    act.wait_ge(half_mm[g], half_count(s, g, n))
                else:
                    act.wait_ge(t_mm[g], n * NSTEP + s + 1)
                if name == "WT":
                    out, src = wt[:, tiles[0] * P:tiles[0] * P + rows * nt_], ps[:, g, 0:rows * nt_]
                elif name == "G":
                    out = rhs[0:rows, tiles[0]:tiles[0] + nt_, :, 1, :].rearrange("p j h c -> p (j h) c")
                    src = group_view(g, 64)
                elif name == "Y0":
                    out, src = (units(t4, g) if g < 2 else y0s[:, :, :]), group_view(g, P)
                else:
                    out, src = units(tt if name[0] == "T" else em, g), group_view(g, rows, step_bank(g, part))
                if part is not None:
                    out, src = (x[:, 2 * part:2 * part + 2] for x in (out, src))
                act.activation(out, src, ACT.Copy).then_inc(half_out[g] if part == 0 else t_out[g], 1)

            def y_tile(j, l, p):
                rows = P if j < 4 else TS
                act.wait_ge(y_mm, (l * NPAIR + p) * 5 + j + 6)
                act.activation(flat(zs[:, bass.ds(p, 1), j * P:j * P + rows]), ps[:, 7, 0:rows], ACT.Copy).then_inc(yw_ready, 1)

            def half_a(l, p, left, right, nxt):
                n = l * NPAIR + p
                for k in range(SLOTS_A):
                    if right and k < 8:
                        step(8 + k, 1, n - 1)
                        step(8 + k, 2, n - 1)
                    if left and k < 2:
                        token_major(k, n)
                    if left and 4 <= k < 12:
                        step(k - 4, 0, n)
                    if right and k in (9, 11, 12):
                        y_tile({9: 2, 11: 3, 12: 4}[k], l, p - 1)
                    if nxt:
                        prepare_1(l, p + 1, k, not right)
                if not left:
                    act.wait_ge(s_ready, n * 8)
                    act.wait_ge(ss_done, n)
                    for q, st in enumerate((S[0], Ss[1])):
                        for h in range(2):
                            hs = slice(64 * h, 64 * h + 64)
                            act.dma_start(wkv_out[bass.ds(n - 1, 1), q, hs, :].rearrange("a p v -> p (a v)"), st[hs, hs]).then_inc(wkv_stored, 16)

            def half_b(l, p, nxt, norm_before):
                n = l * NPAIR + p
                for k in range(SLOTS_B):
                    if k < 8:
                        step(8 + k, 0, n)
                    if k == 0:
                        token_major(2, n)
                    if k == 1:
                        token_major(3, n)
                        token_major(4, n)
                    if 5 <= k < 13:
                        step(k - 5, 1, n)
                    if 6 <= k:
                        step(k - 6, 2, n)
                    if k in (9, 11):
                        y_tile({9: 0, 11: 1}[k], l, p)
                    if nxt:
                        prepare_2(l, p + 1, k, False)
                    if norm_before:
                        normalise(l, p - 1, k, nxt)

            with act.Fori(0, DEPTH) as l:
                ffn(l, 0, "f1i")
                norm(l, 0, COL["ln1_b"], COL["ab1"], l * 40 + 8)
                act.wait_ge(z_set, l + 1)
                for k in range(2):
                    z_copy(l, 0, k, k)
                for q in range(2):
                    act.wait_ge(slot_used, used_count(l, "z", 2 + q))
                    act.activation(ub[q][:, HIST:HIST + HT], ps[:, 2 * q, 0:HT], ACT.Copy).then_inc(u_part, 1)
                    act.activation(ub[q][:, UW - TS:UW], ps[:, 2 * q + 1, TP - HT:HT], ACT.Copy).then_inc(u_part, 1)
                    act.activation(ub[q][:, HIST + HT:HIST + TP], ps[:, 2 * q + 1, 0:TP - HT], ACT.Copy).then_inc(tile_out[q], 1)
                    act.wait_ge(tile_out[q], out_count(l, "z", 1))
                    for s, a in enumerate((TP, UW - HIST)):
                        act.dma_start(pool_out[bass.ds(l, 1), s, :, q, :].rearrange("a p t -> p (a t)"),
                                      ub[q][:, a:a + HIST]).then_inc(pool_stored, 16)
                act.wait_ge(zs_ready, l * NSH + 1 + 2)
                act.activation(lora[0:64, :], lora[0:64, :], ACT.Tanh).then_inc(lora_act, 1)
                act.wait_ge(zs_ready, l * NSH + 2 + 2)
                act.activation(lgate[:, :], lgate[:, :], ACT.Sigmoid).then_inc(lora_act, 1)
                with act.Fori(2, Z_POOLED) as m:
                    for k in range(2):
                        z_copy(l, m, k, 2 * m + k - 2)
                for q in range(2):
                    act.wait_ge(pool_mm, l * 2 + q + 1)
                    act.activation(halves(mf[q][:, :]), pair_bank(4 + 2 * q), ACT.Identity, scale=col(l, COL["pool_scale"] + q)).then_inc(mf_ready, 1)
                for m in range(Z_POOLED, NZ // 2):
                    for k in range(2):
                        z_copy(l, m, k, 2 * m + k - 2)
                    for k in Z_PIECES.get(m, ()):
                        prepare_1(l, 0, k, True)
                act.wait_ge(mf_ready, l * 2 + 2)
                for q in range(2):
                    act.activation(xh[:, q, :], mf[q][:, :], ACT.Copy).then_inc(xh_ready, 1)
                act.wait_ge(last_ready, l * NSH + NSH)
                act.dma_start(shift_out[bass.ds(l, 1)].rearrange("a p k s -> p (a k) s"), last_z[:, :, :]).then_inc(shift_stored, 16)
                for k in range(SLOTS_B):
                    prepare_2(l, 0, k, True)
                heads(act, l, half_a, half_b, normalise)
                with act.Fori(0, NPAIR) as p:
                    act.wait_ge(po_ready, (l + 1) * NPAIR)
                    act.activation(row(xh, p + 2), row(zs, p), ACT.Copy).then_inc(xh_ready, 1)
                norm(l, 1, COL["ln2_b"], COL["ab2"], l * 40 + 24)
                act.wait_ge(wkv_stored, (l + 1) * (NPAIR * 64))
                ffn(l, 1, "f2i")
                with act.Fori(0, 4) as m:
                    for k in range(2):
                        act.wait_ge(tile_out[k], out_count(l, "f2o", m))
                        act.activation(row(xh, 2 * m + k), row(y, 2 * m + k), ACT.Copy).then_inc(xh_ready, 1)
                act.wait_ge(p_loaded, l * 32 + 32)
                act.wait_ge(slot_used, used_count(l, "f2o", 23))
                for k in range(2):
                    act.activation(hh[:, k, :], sq[k][:, :], ACT.Copy).then_inc(ph_ready, 1)
                with act.Fori(0, 4) as m:
                    for k in range(2):
                        act.wait_ge(slot_used, used_count(l, "gp", 6 * m + (3 * k + 1)))
                        act.wait_ge(tile_out[1], out_count(l, "gp", 2 * m + k) - 1)
                        act.activation(halves(sg[:, :]), pair_bank(0), ACT.Sigmoid, bias=col(l, 2 * m + (k + COL["gate_b"]))).then_inc(tile_out[0], 1)
                norm(l, 2, COL["ln3_b"], COL["ab3"], l * 40 + 40)

        @block.vector
        def _(dve):
            dve.memset(eps[:, 0:1], LN_EPS).then_inc(set_done, 1)
            dve.memset(eps[:, 1:2], LNX_EPS).then_inc(set_done, 1)
            dve.sem_inc(zs_ready, 2)

            for m in range(KT):
                dve.wait_ge(xh_ready, m + 1)
                dve.tensor_tensor(xl[:, m, :], y[:, m, :], xh[:, m, :].bitcast(F32), ALU.subtract).then_inc(xl_ready, 1)
            dve.wait_ge(loaded, 16 * NLOAD)
            pv = par[:, :].rearrange("p (l c) -> p l c", l=DEPTH)
            ka, ab = (pv[:, :, COL[c]:COL[c] + w] for c, w in (("one_ka", NPAIR), ("ab1", 3 * KT)))
            dve.tensor_scalar(ka, ka, -1.0, 1.0, ALU.mult, ALU.add)
            dve.tensor_scalar(ab, ab, ALPHA, None, ALU.mult)

            def ffn(l, which, name):
                with dve.Fori(0, FT) as m:
                    f = l * (2 * FT) + which * FT + m
                    dve.wait_ge(slot_used, used_count(l, name, 2 * m + 1))
                    dve.wait_ge(tile_out[0], out_count(l, name, m))
                    dve.wait_ge(hl_ready, f)
                    dve.tensor_tensor(halves(hf[:, :]), halves(sg[:, :]), pair_bank(2), ALU.mult).then_inc(tile_out[1], 1)
                    dve.wait_ge(hh_ready, f + 1)
                    dve.tensor_tensor(row(hl, m), hf[:, :], row(hh, m).bitcast(F32), ALU.subtract).then_inc(hl_ready, 1)

            def residual(l, inst, name, scale, parts):
                if parts is None:
                    dve.memset(ysum[:, :], 0.0).then_inc(sum_ready, 1)
                due = dve.to_reg(inst * 8 + 8)
                dve.wait_ge(loaded, 16 * NLOAD)
                dve.wait_ge(ax_ready, due)
                per = 3 if name in ("f1o", "f2o") else 1
                with dve.Fori(0, 4) as m:
                    for k in range(2):
                        dve.wait_ge(slot_used, used_count(l, name, 2 * per * m + per * k + per - 1))
                        dve.scalar_tensor_tensor(halves(row(y, 2 * m + k)), pair_bank(2 * k), scale, halves(row(y, 2 * m + k)),
                                                 ALU.mult, ALU.add).then_inc(tile_out[k], 1)
                        if parts is None:
                            dve.wait_ge(tile_out[k], out_count(l, name, m))
                            dve.wait_ge(sum_ready, inst * 9 + 2 * m + k + 1)
                            dve.tensor_tensor(ysum[:, :], ysum[:, :], row(y, 2 * m + k), ALU.add).then_inc(sum_ready, 1)
                        else:
                            dve.wait_ge(xh_ready, parts + 2 * m + k + 1)
                            dve.tensor_tensor(row(xl, 2 * m + k), row(y, 2 * m + k), row(xh, 2 * m + k).bitcast(F32),
                                              ALU.subtract).then_inc(xl_ready, 1)

            def newton(r, tmp, v, bias, steps, count):
                dve.scalar_tensor_tensor(halves(tmp), v, bias, halves(r), ALU.add, ALU.mult).then_inc(steps, 1)
                dve.wait_ge(steps, count + 1)
                dve.scalar_tensor_tensor(tmp, tmp, -0.5, r, ALU.mult, ALU.mult).then_inc(steps, 1)
                dve.wait_ge(steps, count + 2)
                dve.scalar_tensor_tensor(r, tmp, 1.5, r, ALU.add, ALU.mult).then_inc(steps, 1)

            def norm(l, inst, count, g, b):
                dve.wait_ge(mean_mm, inst + 1)
                for m in range(KT):
                    dve.tensor_tensor(halves(y[:, m, :]), halves(y[:, m, :]), pair_bank(4), ALU.subtract).then_inc(d_ready, 1)
                dve.wait_ge(rs_ready, inst + 1)
                newton(rs[:, :], hf[:, :], pair_bank(6), LN_EPS, ln_newton, inst * 3)
                dve.wait_ge(ln_newton, inst * 3 + 3)
                for m in range(KT + 1):
                    if m < KT:
                        dve.scalar_tensor_tensor(y[:, m, :], y[:, m, :], col(l, g + m), rs[:, :], ALU.mult, ALU.mult).then_inc(t_ready, 1)
                    if m >= 1:
                        dve.wait_ge(xh_ready, count + m)
                        dve.scalar_tensor_tensor(xl[:, m - 1, :], y[:, m - 1, :], col(l, b + m - 1), xh[:, m - 1, :].bitcast(F32),
                                                 ALU.add, ALU.subtract).then_inc(xl_ready, 1)

            def shifted(l, m, k, j, order, dst):
                i = l * NSH + order
                z = zb[k]
                dve.wait_ge(tile_out[k], out_count(l, "z", m))
                dve.wait_ge(zs_ready, i + 2)
                dve.tensor_tensor(zd[:, :], z[:, 0:T], z[:, 1:T + 1], ALU.subtract).then_inc(zd_ready, 1)
                dve.tensor_copy(last_z[:, bass.ds(j, 1), :].rearrange("p a s -> p (a s)"), z[:, TP:T + 1:TS]).then_inc(last_ready, 1)
                dve.wait_ge(zd_ready, i * 2 + 1)
                dve.tensor_tensor(zd[:, TP:TP + 1], flat(shift_in[:, bass.ds(l, 1), bass.ds(j, 1)]), z[:, TP + 1:TP + 2],
                                  ALU.subtract).then_inc(zd_ready, 1)
                dve.wait_ge(zd_ready, i * 2 + 2)
                dve.scalar_tensor_tensor(dst, zd[:, :], col(l, j + COL["mu"]), z[:, 1:T + 1], ALU.mult, ALU.add).then_inc(zs_ready, 1)

            def pooling(l):
                step = [l * 16]

                def link(ins):
                    ins.then_inc(pool_step, 1)
                    step[0] = step[0] + 1
                    dve.wait_ge(pool_step, step[0])

                for q in range(2):
                    e = ub[q]
                    dve.wait_ge(tile_out[q], out_count(l, "z", 1))
                    link(dve.tensor_tensor(swA[:, 1:UW], e[:, 1:UW], e[:, 0:UW - 1], ALU.add))
                    link(dve.tensor_tensor(swB[:, 3:UW], swA[:, 3:UW], swA[:, 1:UW - 2], ALU.add))
                    if q == 1:
                        link(dve.tensor_tensor(swA[:, 7:UW], swB[:, 7:UW], swB[:, 3:UW - 4], ALU.add))
                        link(dve.tensor_tensor(swB[:, 15:UW], swA[:, 15:UW], swA[:, 7:UW - 8], ALU.add))
                    link(dve.tensor_copy(swB[0:64, 15:UW], swA[0:64, 15:UW]))
                    w = cst[:, CCOL["winv"][0] + q:CCOL["winv"][0] + q + 1]
                    link(dve.scalar_tensor_tensor(pooled[q][:, 0:TP], swB[:, HIST:HIST + TP], w, e[:, HIST:HIST + TP], ALU.mult, ALU.subtract))
                    link(dve.scalar_tensor_tensor(pooled[q][:, TP:T], swB[:, UW - TS:UW], w, e[:, UW - TS:UW], ALU.mult, ALU.subtract))
                    r = CCOL["rcnt"][0] + q * HIST
                    link(dve.tensor_tensor(swA[:, 0:HIST], swB[:, HIST:2 * HIST], cst[:, r:r + HIST], ALU.mult))
                    link(dve.tensor_tensor(pooled[q][:, 0:HIST], swA[:, 0:HIST], e[:, HIST:2 * HIST], ALU.subtract))

            def prepare_1(l, p, k, first):
                n = l * NPAIR + p
                r_ = row(zs, p)
                if k == 0:
                    dve.wait_ge(wa_mm, n * 2)
                    dve.tensor_copy(lora_st[:, :], lora_all[:, bass.ds(p * P, P)]).then_inc(staged, 1)
                if k == 2:
                    if not first:
                        dve.wait_ge(po_ready, n - 2)
                    dve.wait_ge(sig_ready, n * 2 + 1)
                    dve.tensor_tensor_scan(Lb[:, :], const("reset"), tB[:, :], 0.0, ALU.mult, ALU.add).then_inc(scan_ready, 1)
                if k == 5:
                    dve.wait_ge(decay_ready, n * 4 + 4)
                    dve.wait_ge(kkn_mm, n + 1)
                    dve.tensor_scalar(halves(nv[:, :]), pair_bank(5), 1e-24, None, ALU.max).then_inc(kkn_max, 1)
                if k == 10:
                    dve.wait_ge(kkb_ready, n + 1)
                    dve.wait_ge(kp_ready, n + 1)
                    dve.scalar_tensor_tensor(tA[:, :], r_, col(l, p + COL["r_k"]), tB[:, :], ALU.mult, ALU.mult).then_inc(rkk_ready, 1)

            def prepare_2(l, p, k, first):
                n = l * NPAIR + p
                r_, k_, v_ = row(zs, p), row(zs, p + 6), row(zs, p + 12)
                if k == 8:
                    dve.tensor_tensor(ar[:, 1, :], r_, Pb[:, 1:T + 1], ALU.mult).then_inc(ar_ready, 1)
                if k == 1:
                    dve.wait_ge(rk_mm, n + 1)
                    dve.tensor_tensor(halves(k_), pair_bank(5), halves(v_), ALU.mult).then_inc(bonus_ready, 1)
                if k == 9:
                    dve.scalar_tensor_tensor(ar[:, 0, :], kkb[:, :], -1.0, Pb[:, 0:T], ALU.mult, ALU.mult).then_inc(ar_ready, 1)
                    dve.wait_ge(ar_ready, n * 3 + 2)
                    dve.tensor_scalar(ar[:, 0, 0:T:CH], kkb[:, 0:T:CH], -1.0, None, ALU.mult).then_inc(ar_ready, 1)

            def normalise(l, p, k, after_bonus):
                n = l * NPAIR + p
                if k == 0:
                    dve.wait_ge(pg_mm, n)
                    dve.tensor_copy(g2_st[:, :], g2_all[:, bass.ds(p * P, P)]).then_inc(g_staged, 1)
                if k == 2:
                    dve.wait_ge(pm_mm, n + 1)
                    dve.tensor_tensor(halves(pd[:, :]), halves(row(zs, p)), pair_bank(5), ALU.subtract).then_inc(pd_ready, 1)
                if k == 4:
                    dve.wait_ge(prs_ready, n + 1)
                    newton(prs[:, :], psq[:, :], pair_bank(5), LNX_EPS, hn_newton, n * 3)

            def products(u, n):
                j, h = u // 2, u % 2
                rows, b = (P if j < 4 else TS), 3 + u % 2
                dve.wait_ge(y_mm, n * 5 + j + 1)
                dve.wait_ge(am_mm, n * 10 + u + 1)
                dve.tensor_tensor(a4t[0][:, u, :] if j < 4 else a4t[1][:, h, :], ps[0:rows, b, 0:rows], const("m4t", rows, rows), ALU.mult).then_inc(am_part, 1)
                mask = const("am", rows).rearrange("p (a t) -> p a t", a=3)[:, :, 0:rows]
                dve.tensor_tensor(am[:, u, :, :] if j < 4 else ams[:, h, :, :], ps[0:rows, b, rows:4 * rows].rearrange("p (a t) -> p a t", a=3),
                                  mask, ALU.mult).then_inc(am_ready, 1)

            def step(s, g, n, part=None):
                name = STEPS[s]
                if name not in ("A", "H1", "H2", "X1", "X2", "X3", "Y1", "Y2", "Y3"):
                    return
                rows = P if g < 2 else TS
                if part is not None:
                    if part == 0:
                        dve.wait_ge(half_mm[g], half_count(s, g, n))
                    else:
                        dve.wait_ge(t_mm[g], n * NSTEP + s + 1)
                    us = slice(2 * part, 2 * part + 2)
                    dve.tensor_tensor(units(xm, g)[:, us], group_view(g, rows, step_bank(g, part))[:, us], units(t4, g)[:, us], ALU.add).then_inc(
                        (t_out if part else half_out)[g], 1)
                    return
                dve.wait_ge(t_mm[g], n * NSTEP + s + 1)
                src = group_view(g, P if name[0] == "Y" else rows)
                if name == "A":
                    dve.tensor_tensor(a_units(xm, g), a_view(g), a_spread("m4", g), ALU.mult).then_inc(t_part[g], 1)
                    dve.wait_ge(t_part[g], n * (2, 2, 1)[g] + 1)
                    dve.tensor_tensor(units(xm, g), units(xm, g), spread("ident", g), ALU.add).then_inc(t_out[g], 1)
                    dve.tensor_tensor(a_units(n16, g), a_view(g), a_spread("m16", g), ALU.mult).then_inc(n_ready[g], 1)
                    dve.tensor_tensor(a_units(n64, g), a_view(g), a_spread("m64", g), ALU.mult).then_inc(n_ready[g], 1)
                elif name[0] == "H":
                    dve.tensor_tensor(units(xm if name == "H1" else t4, g), src, spread("ident", g), ALU.add).then_inc(t_out[g], 1)
                elif name == "Y3":
                    for q in range(2 if g < 2 else 1):
                        j = 2 * g + q
                        o = xm[0][:, 2 * j:2 * j + 2, :] if g < 2 else ys[:, :, :]
                        i1 = t4[0][:, 2 * j:2 * j + 2, :] if g < 2 else y0s[:, :, :]
                        dve.tensor_tensor(o.rearrange("p a (h c) -> p h a c", h=2), src[:, 2 * q:2 * q + 2, :].rearrange("p h (a c) -> p h a c", a=2),
                                          i1.rearrange("p h (a c) -> p h a c", a=2), ALU.add).then_inc((t_part if g < 2 and q == 0 else t_out)[g], 1)
                elif name[0] == "Y" and g == 2:
                    dve.tensor_tensor(ys[:, :, :], src, y0s[:, :, :], ALU.add).then_inc(t_out[g], 1)
                else:
                    dve.tensor_tensor(units(xm, g), src, units(t4, g), ALU.add).then_inc(t_out[g], 1)

            def chunk_in(c, n):
                j, ro, rows = (c // 2, 64 * (c % 2), CH) if c < NCH else (4, 0, TS)
                g_part = xm[0][ro:ro + rows, 2 * j + 1, :] if j < 4 else ys[:, 1, :]
                out = um[ro:ro + rows, j, :]
                if c == 0:
                    dve.wait_ge(t_out[0], n * NSTEP + NSTEP - 1)
                    dve.tensor_copy(out, g_part).then_inc(um_ready, 1)
                else:
                    dve.wait_ge(u_mm, n * 8 + c)
                    dve.tensor_tensor(out, ps[ro:ro + rows, 5, 0:P], g_part, ALU.add).then_inc(um_ready, 1)

            def chunk_out(c, l, p):
                n = l * NPAIR + p
                decay = dec[:, bass.ds(p * (NCH + 1) + c, 1)]
                dve.wait_ge(s_mm, n * 9 + c + 1)
                if c == 0:
                    dve.scalar_tensor_tensor(S[1][:, :], ps[:, 6, 0:P], decay, const("head_sum"), ALU.mult, ALU.mult).then_inc(s_ready, 1)
                    return
                dve.scalar_tensor_tensor(dS[:, :], ps[:, 6, 0:P], decay, const("head_sum"), ALU.mult, ALU.mult).then_inc(ds_ready, 1)
                dve.wait_ge(ds_ready, n * 8 + c)
                if c == NCH:
                    dve.scalar_tensor_tensor(Ss[1][:, :], Ss[0][:, :], decay, dS[:, :], ALU.mult, ALU.add).then_inc(ss_done, 1)
                    return
                if c == 1:
                    dve.wait_ge(wkv_stored, n * 64)
                dve.wait_ge(s_ready, n * 8 + c)
                dve.scalar_tensor_tensor(S[(c + 1) % 2][:, :], S[c % 2][:, :], decay, dS[:, :], ALU.mult, ALU.add).then_inc(s_ready, 1)

            def sample_state(l, p):
                n = l * NPAIR + p
                dve.wait_ge(y_mm, n * 5 + 5)
                dve.wait_ge(ss_done, n)
                for h in range(2):
                    hs = slice(64 * h, 64 * h + 64)
                    dve.tensor_copy(Ss[0][hs, hs], wkv_in[hs, bass.ds(l, 1), bass.ds(p, 1), :].rearrange("p a b v -> p (a b v)")).then_inc(
                        (ss_part, ss_init)[h], 1)

            def half_a(l, p, left, right, nxt):
                n = l * NPAIR + p
                for k in range(SLOTS_A):
                    if right and k < 8:
                        step(8 + k, 1, n - 1)
                        step(8 + k, 2, n - 1)
                    if right and k == 7:
                        sample_state(l, p - 1)
                    if right and k >= 8:
                        chunk_in(k - 4, n - 1)
                        if left and k < 12:
                            step(k - 4, 0, n, 0)
                        chunk_out(k - 4, l, p - 1)
                    if left and 2 <= k < 4:
                        products(2 * k - 4, n)
                        products(2 * k - 3, n)
                    if left and not right and 8 <= k < 12:
                        step(k - 4, 0, n, 0)
                    if left and 4 <= k < 12:
                        step(k - 4, 0, n, 1 if k >= 8 else None)
                    if nxt:
                        prepare_1(l, p + 1, k, not right)

            def half_b(l, p, nxt, norm_before):
                n = l * NPAIR + p
                for k in range(SLOTS_B):
                    if k < 8:
                        step(8 + k, 0, n)
                    elif k < 12:
                        chunk_in(k - 8, n)
                        step(k - 5, 1, n, 0)
                        chunk_out(k - 8, l, p)
                    if 2 <= k < 5:
                        products(2 * k, n)
                        products(2 * k + 1, n)
                    if 5 <= k < 13:
                        step(k - 5, 1, n, 1 if 8 <= k < 12 else None)
                    if 6 <= k:
                        step(k - 6, 2, n)
                    if nxt:
                        prepare_2(l, p + 1, k, False)
                    if norm_before:
                        normalise(l, p - 1, k, nxt)

            with dve.Fori(0, DEPTH) as l:
                ffn(l, 0, "f1i")
                residual(l, l * 3, "f1o", 0.5, None)
                norm(l, l * 3, l * 40 + 8, COL["ln1_g"], COL["ln1_b"])
                dve.wait_ge(shift_stored, l * 16)
                dve.memset(pool_bd[:, :, :], 0.0).then_inc(bd_zero, 1)
                dve.wait_ge(bd_zero, l + 1)
                for k in range(2):
                    dve.memset(zb[k][:, 0:1], 0.0)
                    dve.memset(ub[k][:, 0:HIST], 0.0)
                    dve.tensor_copy(ub[k][:, HIST + TP:HIST + TP + HIST], flat(pool_hs[:, bass.ds(l, 1), k, :]))
                    for h in range(2):
                        hs = slice(64 * h, 64 * h + 64)
                        ins = dve.tensor_copy(pool_bd[hs, k, hs], flat(pool_w[hs, bass.ds(l, 1), k, :]))
                ins.then_inc(z_set, 1)
                shifted(l, 0, 0, 18, 0, lora[:, :])
                shifted(l, 0, 1, 19, 1, lgate[:, :])
                pooling(l)
                for k in range(2):
                    shifted(l, 2, k, k, 2 + k, zs[:, k, :])
                with dve.Fori(3, Z_LAST) as m:
                    for k in range(2):
                        shifted(l, m, k, 2 * m + (k - 4), 2 * m + (k - 2), row(zs, 2 * m + (k - 4)))
                for m in range(Z_LAST, NZ // 2):
                    for k in range(2):
                        shifted(l, m, k, 2 * m + k - 4, 2 * m + k - 2, zs[:, 2 * m + k - 4, :])
                    if m == Z_LAST:
                        dve.wait_ge(pool_stored, l * 64 + 64)
                        dve.wait_ge(mf_ready, l * 2 + 2)
                        dve.wait_ge(lora_act, l * 2 + 2)
                        dve.wait_ge(layer_loaded, l * 32 + 32)
                        for h in range(2):
                            dve.memset(kt[64 - 64 * h:128 - 64 * h, h, :], 0.0)
                        dve.memset(Pb[:, 0:1], 1.0)
                        dve.memset(Ss[0][:, :], 0.0).then_inc(set_done, 1)
                        dve.wait_ge(set_done, l + 3)
                    for k in Z_PIECES.get(m, ()):
                        prepare_1(l, 0, k, True)
                dve.wait_ge(zs_ready, l * NSH + NSH + 2)
                for h in range(2):
                    dve.memset(bt[64 - 64 * h:128 - 64 * h, h, :], 0.0)
                for k in range(SLOTS_B):
                    prepare_2(l, 0, k, True)
                for q in range(2):
                    dve.wait_ge(xh_ready, l * 40 + 17 + q)
                    dve.tensor_tensor(xl[:, q, :], mf[q][:, :], xh[:, q, :].bitcast(F32), ALU.subtract).then_inc(xl_ready, 1)
                heads(dve, l, half_a, half_b, normalise)
                with dve.Fori(0, NPAIR) as p:
                    dve.wait_ge(xh_ready, l * 40 + p + 19)
                    dve.tensor_tensor(row(xl, p + 2), row(zs, p), row(xh, p + 2).bitcast(F32), ALU.subtract).then_inc(xl_ready, 1)
                residual(l, l * 3 + 1, "wo", 1.0, None)
                norm(l, l * 3 + 1, l * 40 + 24, COL["ln2_g"], COL["ln2_b"])
                due = dve.to_reg((l + 1) * (NPAIR * 64))
                dve.wait_ge(loaded, 16 * NLOAD)
                dve.wait_ge(wkv_stored, due)
                ffn(l, 1, "f2i")
                residual(l, l * 3 + 2, "f2o", 0.5, l * 40 + 32)
                for k in range(2):
                    dve.wait_ge(ph_ready, l * 2 + k + 1)
                    dve.tensor_tensor(hl[:, k, :], sq[k][:, :], hh[:, k, :].bitcast(F32), ALU.subtract).then_inc(pl_ready, 1)
                dve.memset(ysum[:, :], 0.0).then_inc(sum_ready, 1)
                with dve.Fori(0, 4) as m:
                    for k in range(2):
                        dve.wait_ge(slot_used, used_count(l, "gp", 6 * m + (3 * k + 2)))
                        dve.wait_ge(tile_out[0], out_count(l, "gp", 2 * m + k))
                        dve.tensor_tensor(halves(hf[:, :]), halves(sg[:, :]), pair_bank(2), ALU.mult).then_inc(tile_out[1], 1)
                        dve.wait_ge(tile_out[1], out_count(l, "gp", 2 * m + k))
                        dve.tensor_tensor(row(y, 2 * m + k), row(y, 2 * m + k), hf[:, :], ALU.add).then_inc(y_ready, 1)
                        dve.wait_ge(y_ready, l * 8 + 2 * m + (k + 1))
                        dve.wait_ge(sum_ready, l * 27 + 2 * m + (k + 19))
                        dve.tensor_tensor(ysum[:, :], ysum[:, :], row(y, 2 * m + k), ALU.add).then_inc(sum_ready, 1)
                norm(l, l * 3 + 2, l * 40 + 40, COL["ln3_g"], COL["ln3_b"])
            dve.wait_ge(xl_ready, DEPTH * 40 + 8)
            dve.wait_ge(ax_ready, DEPTH * 24 + 8)
            for m in range(KT):
                dve.tensor_tensor(y[:, m, :], xh[:, m, :].bitcast(F32), xl[:, m, :].bitcast(F32), ALU.add).then_inc(fin_ready, 1)


def constants():
    i = np.arange(P)
    t, s = i[:, None], i[None, :]
    same = lambda n: (t // n) == (s // n)
    low = s < t
    c = {
        "ident": t == s, "swap": t == (s + 64) % P, "mean_d": np.full((P, P), 1.0 / D), "head_sum": same(64), "head_mean": same(64) / 64.0,
        "m4": low & same(4), "m16": low & same(16) & ~same(4), "m64": low & same(64) & ~same(16), "m4t": (t < s) & same(4),
        "am": np.concatenate([(t <= s) & same(64), (t < s) & same(64), (t <= s) & same(64)], axis=1),
        "reset": np.tile((np.arange(T) % CH != 0), (P, 1)),
    }
    wins = np.array([[2, 8], [4, 16]])[i // 64]
    c["winv"] = 1.0 / wins
    c["rcnt"] = np.concatenate([1.0 / np.minimum(np.arange(HIST)[None, :] + 1, wins[:, q:q + 1]) for q in range(2)], axis=1)
    return np.ascontiguousarray(np.concatenate([np.asarray(c[n], np.float32) for n, _ in CONSTS], axis=1))


def kernel(**inputs):
    import concourse.bacc as bacc
    from concourse.bass_utils import run_bass_kernel_spmd

    a = {k: np.asarray(v) for k, v in inputs.items()}
    L = DEPTH

    def channels(x, n):
        x = x.reshape(x.shape[:-1] + (n, P))
        return np.moveaxis(x, -1, 0)

    def tokens(x):
        return x.T.reshape(-1, P, x.shape[0]).transpose(1, 0, 2)

    def slots(w):
        n, k, m = w.shape
        return w.reshape(n, k // P, P, m // P, P).transpose(0, 3, 2, 1, 4)

    def ffn_in(w):
        s = slots(w)
        return np.stack([s[:, :FT], s[:, FT:]], axis=2).reshape((L * 2 * FT,) + s.shape[2:])

    def flat_slots(s):
        return s.reshape((-1,) + s.shape[2:])

    z = slots(a["w_in"])
    cols = []
    for n, w in COLS:
        src = {"gate_b": "ple_gate_b", "mu": "mu_shift", "one_ka": "k_a", "ab1": "ln1_b", "ab2": "ln2_b", "ab3": "ln3_b"}.get(n, n)
        cols.append(channels(a[src].reshape(L, -1), w))
    lora = np.concatenate([a["w2"], a["a2"]], axis=1)
    pw = a["pool_w"].reshape(L, 2, 2, 64, 64)
    st = a["state_wkv"][:, 0].reshape(L, NPAIR, 2, 64, 64)
    arrays = {
        "xT": tokens(np.concatenate([a["x_prompt"][0], a["x_sample"][0]], axis=0)),
        "pT": np.stack([tokens(np.concatenate([a["p_prompt"][i, 0], a["p_sample"][i, 0]], axis=0)) for i in range(L)]),
        "w1i": ffn_in(a["ffn1_w_in"]), "w1o": flat_slots(slots(a["ffn1_w_out"])),
        "wz": flat_slots(np.concatenate([z[:, 20:], z[:, :2], z[:, 2:20]], axis=1)), "wo": flat_slots(slots(a["w_out"])),
        "w2i": ffn_in(a["ffn2_w_in"]), "w2o": flat_slots(slots(a["ffn2_w_out"])),
        "wg": flat_slots(slots(a["ple_gate_w"])), "wp": flat_slots(slots(a["ple_w"])),
        "params": np.concatenate(cols, axis=2).reshape(P, L * NPAR),
        "consts": constants(),
        "poolw": pw.transpose(2, 3, 0, 1, 4).reshape(P, L, 2, 64),
        "lora_w": lora, "g2_w": a["g2"],
        "pool_hist": channels(a["state_pool"][:, 0], 2).transpose(0, 1, 3, 2),
        "shift_hist": channels(a["state_shift"][:, 0], NSH),
        "wkv_hist": st.transpose(2, 4, 0, 1, 3).reshape(P, L, NPAIR, 64),
    }
    arrays = {k: np.ascontiguousarray(v) for k, v in arrays.items()}
    outs = {"y_out": (P, KT, T), "pool_out": (L, 2, P, 2, HIST), "shift_out": (L, P, NSH, 2), "wkv_out": (L * NPAIR, 2, P, 64)}
    nc = bacc.Bacc("TRN2", target_bir_lowering=False, num_devices=1)
    args = [nc.dram_tensor("in_" + k, v.shape, F32, kind="ExternalInput").ap() for k, v in arrays.items()]
    args += [nc.dram_tensor(k, s, F32, kind="ExternalOutput").ap() for k, s in outs.items()]
    build(nc, *args)
    r = run_bass_kernel_spmd(nc, [{"in_" + k: v for k, v in arrays.items()}], core_ids=[0]).results[0]
    yo = np.asarray(r["y_out"]).transpose(2, 1, 0).reshape(T, D)
    po = np.asarray(r["pool_out"]).transpose(1, 0, 4, 3, 2).reshape(2, L, 1, HIST, 2 * P)
    so = np.asarray(r["shift_out"]).transpose(3, 0, 2, 1).reshape(2, L, 1, NSH * P)
    wo = np.asarray(r["wkv_out"]).reshape(L, NPAIR, 2, 2, 64, 64).transpose(2, 0, 1, 3, 5, 4).reshape(2, L, 1, 2 * NPAIR, 64, 64)
    c = np.ascontiguousarray
    return (c(yo[None, :TP]), c(yo[None, TP:]), c(po[0]), c(so[0]), c(wo[0]), c(po[1]), c(so[1]), c(wo[1]))
```
